# Optimizing a Trainium2 kernel written in Bass

```python
import math
import jax
import jax.numpy as jnp
from jax import lax
import numpy as np

D_MODEL = 1024
BATCH = 1
SEQ = 128
DEPTH = 1
DEC_BATCH = 1
DEC_SEQ = 1024
PAST_LEN = 128

GRID_W = 64
MLA_HEADS = 8
QK_NOPE = 64
QK_ROPE = 32
V_DIM = 64
Q_LORA = 384
KV_LORA = 256
ROPE_BASE = 10000.0
Q_BLOCK = 128
HG_HEADS = 4
HG_DK = 128
HG_DV = 128
HG_WIDTH = HG_HEADS * HG_DV
HG_CHUNK = 16
D_FF = 2816
CONV_W = 3
EPS = 1e-6
IN_SPLITS = [Q_LORA, KV_LORA, QK_ROPE,
             HG_HEADS * HG_DK,
             HG_HEADS * HG_DK,
             HG_HEADS * HG_DK,
             HG_WIDTH,
             HG_WIDTH,
             D_MODEL,
             D_MODEL]
D_IN = sum(IN_SPLITS)

kernel_name = 'mla_hgrn2_convglu_prefix_diffusion_step'

def rmsnorm(x, g):
    xf = x.astype(jnp.float32)
    y = xf * lax.rsqrt(jnp.mean(xf * xf, axis=-1, keepdims=True) + EPS)
    return (y * g).astype(x.dtype)

def split_cols(p):
    offs = [int(o) for o in np.cumsum(IN_SPLITS)[:-1]]
    return jnp.split(p, offs, axis=-1)

def axial_rope_tables(T):
    rows = T // GRID_W
    rr, cc = jnp.meshgrid(jnp.arange(rows, dtype=jnp.float32),
                          jnp.arange(GRID_W, dtype=jnp.float32), indexing='ij')
    r_pos, c_pos = rr.reshape(-1), cc.reshape(-1)
    n_freq = QK_ROPE // 4
    inv = jnp.power(ROPE_BASE, -jnp.arange(n_freq, dtype=jnp.float32) / n_freq)
    ang = jnp.concatenate([r_pos[:, None] * inv, c_pos[:, None] * inv], axis=-1)
    ang = jnp.concatenate([ang, ang], axis=-1)
    return jnp.cos(ang), jnp.sin(ang)

def rotate_half(x):
    x1, x2 = jnp.split(x, 2, axis=-1)
    return jnp.concatenate([-x2, x1], axis=-1)

def apply_rope(x, cos, sin):
    xf = x.astype(jnp.float32)
    return (xf * cos + rotate_half(xf) * sin).astype(x.dtype)

def mla_attention(q_nope, q_rope, k_nope, k_rope, v):
    B, T = q_nope.shape[:2]
    nb = T // Q_BLOCK
    scale = (QK_NOPE + QK_ROPE) ** -0.5
    qn = jnp.moveaxis(q_nope.reshape(B, nb, Q_BLOCK, MLA_HEADS, QK_NOPE), 1, 0)
    qr = jnp.moveaxis(q_rope.reshape(B, nb, Q_BLOCK, MLA_HEADS, QK_ROPE), 1, 0)

    def block(args):
        qn_b, qr_b = args
        s = (jnp.einsum('bqhd,bkhd->bhqk', qn_b, k_nope)
             + jnp.einsum('bqhr,bkr->bhqk', qr_b, k_rope)).astype(jnp.float32)
        p = jax.nn.softmax(s * scale, axis=-1).astype(v.dtype)
        return jnp.einsum('bhqk,bkhd->bqhd', p, v)

    o = lax.map(block, (qn, qr))
    return jnp.moveaxis(o, 0, 1).reshape(B, T, MLA_HEADS * V_DIM)

def hgrn2_chunk_scan(q, k, v, logf, s0):
    B, T = q.shape[:2]
    n = T // HG_CHUNK

    def chunks(a):
        return a.astype(jnp.float32).reshape(B, n, HG_CHUNK, HG_HEADS, a.shape[-1])

    qc, kc, vc, gc = chunks(q), chunks(k), chunks(v), chunks(logf)
    G = jnp.cumsum(gc, axis=2)
    G_last = G[:, :, -1]
    causal = jnp.tril(jnp.ones((HG_CHUNK, HG_CHUNK), dtype=bool))[None, None, :, :, None, None]
    diff = G[:, :, :, None] - G[:, :, None, :]
    decay = jnp.exp(jnp.where(causal, diff, -jnp.inf))
    A = jnp.einsum('bntshk,bnthk,bnshk->bnhts', decay, qc, kc)
    o_intra = jnp.einsum('bnhts,bnshv->bnthv', A, vc)
    U = jnp.einsum('bnshk,bnshv->bnhkv', kc * jnp.exp(G_last[:, :, None] - G), vc)

    def step(S, inp):
        dec, u = inp
        return dec[..., None] * S + u, S

    S_final, S_prev = lax.scan(step, s0.astype(jnp.float32),
                               (jnp.moveaxis(jnp.exp(G_last), 1, 0), jnp.moveaxis(U, 1, 0)))
    S_prev = jnp.moveaxis(S_prev, 0, 1)
    o_inter = jnp.einsum('bnthk,bnhkv->bnthv', qc * jnp.exp(G), S_prev)
    return (o_intra + o_inter).reshape(B, T, HG_HEADS, HG_DV), S_final

def hgrn2_direction(q, v, z_f, lb, s0, reverse):
    B, T = q.shape[:2]
    f = lb + (1.0 - lb) * jax.nn.sigmoid(z_f.astype(jnp.float32))
    f = f.reshape(B, T, HG_HEADS, HG_DK)
    logf = jnp.log(f)
    k = 1.0 - f
    if reverse:
        q, k, v, logf = jnp.flip(q, 1), jnp.flip(k, 1), jnp.flip(v, 1), jnp.flip(logf, 1)
    o, s = hgrn2_chunk_scan(q, k, v, logf, s0)
    if reverse:
        o = jnp.flip(o, 1)
    return o, s

def hgrn2_branch(hq, hf_f, hf_b, hi, hg, lb_f, lb_b, s0_f, s0_b, g_hg):
    B, T = hq.shape[:2]
    q = jax.nn.silu(hq).reshape(B, T, HG_HEADS, HG_DK)
    v = hi.reshape(B, T, HG_HEADS, HG_DV)
    o_f, s_f = hgrn2_direction(q, v, hf_f, lb_f, s0_f, False)
    o_b, s_b = hgrn2_direction(q, v, hf_b, lb_b, s0_b, True)
    o = rmsnorm(o_f + o_b, g_hg.reshape(HG_HEADS, HG_DV))
    o = o.reshape(B, T, HG_WIDTH).astype(hq.dtype) * jax.nn.silu(hg)
    return o, s_f, s_b

def conv_glu(h, w_ffn_in, conv_w, conv_b, w_ffn_out):
    T = h.shape[1]
    gate, val = jnp.split(h @ w_ffn_in, 2, axis=-1)
    pad = CONV_W // 2
    gp = jnp.pad(gate, ((0, 0), (pad, pad), (0, 0)))
    gconv = conv_b + sum(gp[:, j:j + T] * conv_w[j] for j in range(CONV_W))
    return (jax.nn.gelu(gconv) * val) @ w_ffn_out

def trunk_layer(x, mod, rope, cache, lw):
    B, T, _ = x.shape
    sh1, sc1, gt1, sh2, sc2, gt2 = jnp.split(mod, 6, axis=-1)
    h = rmsnorm(x, lw['g_mix']) * (1.0 + sc1) + sh1
    pq, pkv, pkr, hq, hf_f, hf_b, hi, hg, ga, gb = split_cols(h @ lw['w_in'])
    q = (rmsnorm(pq, lw['g_q']) @ lw['w_uq']).reshape(B, T, MLA_HEADS, QK_NOPE + QK_ROPE)
    q_nope, q_rope = q[..., :QK_NOPE], q[..., QK_NOPE:]
    ckv = rmsnorm(pkv, lw['g_kv'])
    k_rope = pkr
    if rope is None:
        ckv_keys, krope_keys = ckv, k_rope
        s0_f = jnp.zeros((B, HG_HEADS, HG_DK, HG_DV), jnp.float32)
        s0_b = s0_f
    else:
        cos, sin = rope
        q_rope = apply_rope(q_rope, cos[:, None, :], sin[:, None, :])
        ckv_ctx, krope_ctx, s0_f, s0_b = cache
        ckv_keys = jnp.concatenate([ckv, ckv_ctx], axis=1)
        krope_keys = jnp.concatenate([apply_rope(k_rope, cos, sin), krope_ctx], axis=1)
    K = ckv_keys.shape[1]
    kv = (ckv_keys @ lw['w_ukv']).reshape(B, K, MLA_HEADS, QK_NOPE + V_DIM)
    o_mla = mla_attention(q_nope, q_rope, kv[..., :QK_NOPE], krope_keys, kv[..., QK_NOPE:])
    o_hg, s_f, s_b = hgrn2_branch(hq, hf_f, hf_b, hi, hg, lw['lb_f'], lw['lb_b'], s0_f, s0_b, lw['g_hg'])
    mix = jax.nn.sigmoid(ga) * (o_mla @ lw['w_mla_o']) + jax.nn.sigmoid(gb) * (o_hg @ lw['w_hg_o'])
    x = x + gt1 * (mix @ lw['w_out'])
    h2 = rmsnorm(x, lw['g_ffn']) * (1.0 + sc2) + sh2
    x = x + gt2 * conv_glu(h2, lw['w_ffn_in'], lw['conv_w'], lw['conv_b'], lw['w_ffn_out'])
    return x, ckv, k_rope, s_f, s_b

def setup_inputs(seed: int = 0) -> dict:
    key = jax.random.key(seed)
    ks = iter(jax.random.split(key, 40))

    def nrm(shape, scale):
        return jax.random.normal(next(ks), shape, jnp.float32) * scale

    def gain(shape):
        return 1.0 + nrm(shape, 0.02)

    D = D_MODEL
    return {
        'x_prompt': nrm((BATCH, SEQ, D), 1.0),
        'x_sample': nrm((DEC_BATCH, DEC_SEQ, D), 1.0),
        'cache_ckv': nrm((DEC_BATCH, DEPTH, PAST_LEN, KV_LORA), 1.0),
        'cache_krope': nrm((DEC_BATCH, DEPTH, PAST_LEN, QK_ROPE), 1.0),
        'state_hgrn_fwd': nrm((DEC_BATCH, DEPTH, HG_HEADS, HG_DK, HG_DV), 0.3),
        'state_hgrn_bwd': nrm((DEC_BATCH, DEPTH, HG_HEADS, HG_DK, HG_DV), 0.3),
        'c': nrm((DEC_BATCH, D), 1.0),
        'c_ctx': nrm((D,), 1.0),
        'w_mod': nrm((DEPTH, D, 6 * D), D ** -0.5),
        'b_mod': nrm((DEPTH, 6 * D), 0.01),
        'g_mix': gain((DEPTH, D)),
        'w_in': nrm((DEPTH, D, D_IN), D ** -0.5),
        'g_q': gain((DEPTH, Q_LORA)),
        'w_uq': nrm((DEPTH, Q_LORA, MLA_HEADS * (QK_NOPE + QK_ROPE)), Q_LORA ** -0.5),
        'g_kv': gain((DEPTH, KV_LORA)),
        'w_ukv': nrm((DEPTH, KV_LORA, MLA_HEADS * (QK_NOPE + V_DIM)), KV_LORA ** -0.5),
        'w_mla_o': nrm((DEPTH, MLA_HEADS * V_DIM, D), (MLA_HEADS * V_DIM) ** -0.5),
        'lb_param': nrm((DEPTH + 1, 2, HG_HEADS * HG_DK), 0.5),
        'g_hg': gain((DEPTH, HG_WIDTH)),
        'w_hg_o': nrm((DEPTH, HG_WIDTH, D), HG_WIDTH ** -0.5),
        'w_out': nrm((DEPTH, D, D), D ** -0.5),
        'g_ffn': gain((DEPTH, D)),
        'w_ffn_in': nrm((DEPTH, D, 2 * D_FF), D ** -0.5),
        'conv_w': nrm((DEPTH, CONV_W, D_FF), CONV_W ** -0.5),
        'conv_b': nrm((DEPTH, D_FF), 0.01),
        'w_ffn_out': nrm((DEPTH, D_FF, D), D_FF ** -0.5),
        'g_final': gain((D,)),
    }

def reference(x_prompt, x_sample, cache_ckv, cache_krope, state_hgrn_fwd, state_hgrn_bwd,
              c, c_ctx, w_mod, b_mod, g_mix, w_in, g_q, w_uq, g_kv, w_ukv, w_mla_o,
              lb_param, g_hg, w_hg_o, w_out, g_ffn, w_ffn_in, conv_w, conv_b, w_ffn_out, g_final):
    lb_all = jnp.cumsum(jax.nn.softmax(lb_param.astype(jnp.float32), axis=0), axis=0)
    rope = axial_rope_tables(x_sample.shape[1])
    x_ctx, x_lat = x_prompt, x_sample
    new_ckv, new_krope, new_sf, new_sb = [], [], [], []
    for l in range(DEPTH):
        lw = {'g_mix': g_mix[l], 'w_in': w_in[l], 'g_q': g_q[l], 'w_uq': w_uq[l], 'g_kv': g_kv[l],
              'w_ukv': w_ukv[l], 'w_mla_o': w_mla_o[l], 'lb_f': lb_all[l, 0], 'lb_b': lb_all[l, 1],
              'g_hg': g_hg[l], 'w_hg_o': w_hg_o[l], 'w_out': w_out[l], 'g_ffn': g_ffn[l],
              'w_ffn_in': w_ffn_in[l], 'conv_w': conv_w[l], 'conv_b': conv_b[l], 'w_ffn_out': w_ffn_out[l]}
        mod_ctx = (jax.nn.silu(c_ctx) @ w_mod[l] + b_mod[l])[None, None, :]
        mod_lat = (jax.nn.silu(c) @ w_mod[l] + b_mod[l])[:, None, :]
        x_ctx, ckv_l, krope_l, sf_l, sb_l = trunk_layer(x_ctx, mod_ctx, None, None, lw)
        new_ckv.append(ckv_l)
        new_krope.append(krope_l)
        new_sf.append(sf_l)
        new_sb.append(sb_l)
        cache_l = (cache_ckv[:, l], cache_krope[:, l], state_hgrn_fwd[:, l], state_hgrn_bwd[:, l])
        x_lat, _, _, _, _ = trunk_layer(x_lat, mod_lat, rope, cache_l, lw)
    y_prompt = rmsnorm(x_ctx, g_final)
    y_sample = rmsnorm(x_lat, g_final)
    ckv_out = jnp.stack(new_ckv, axis=1)
    krope_out = jnp.stack(new_krope, axis=1)
    sf_out = jnp.stack(new_sf, axis=1).astype(x_prompt.dtype)
    sb_out = jnp.stack(new_sb, axis=1).astype(x_prompt.dtype)
    return (y_prompt, y_sample, ckv_out, krope_out, sf_out, sb_out)


_drawn_inputs = setup_inputs


def setup_inputs(seed=0):
    import zlib

    import numpy as np

    out = dict(_drawn_inputs(seed))
    spreads = {}
    factors = {'cache_ckv': 8.0,
     'cache_krope': 8.0,
     'state_hgrn_fwd': 49.656,
     'state_hgrn_bwd': 49.599,
     'b_mod': 3.693,
     'g_mix': 3.286,
     'g_q': 8.0,
     'g_kv': 8.585,
     'g_hg': 8.0,
     'g_ffn': 4.082,
     'conv_b': 36.405,
     'g_final': 7.73}
    for name, (base, spread) in spreads.items():
        noise = np.random.default_rng([zlib.crc32(name.encode()), seed]).standard_normal(out[name].shape)
        drawn = base * np.exp(spread * noise) if base else spread * noise
        out[name] = jnp.asarray(drawn.astype(out[name].dtype))
    for name, factor in factors.items():
        out[name] = (out[name] * factor).astype(out[name].dtype)
    return out
```

```python
import numpy as np
import concourse.bass as bass
from concourse import mybir
from contextlib import ExitStack

F32 = mybir.dt.float32
F32R = mybir.dt.float32r
I32 = mybir.dt.int32
ACT = mybir.ActivationFunctionType
ALU = mybir.AluOpType
AX = mybir.AxisListType

P = 128
D = 1024
KD = D // P
TL, TC = 1024, 128
NT = TL + TC
TILES = NT // P
CH, NCH = 384, 3
HEADS, NOPE, ROPE, VD = 8, 64, 32, 64
QH = NOPE + ROPE
QL, KVL = 384, 256
HH, DK = 4, 128
DFF = 2816
GRID_W = 64
EPS = 1e-6
GROUPS = ((0, TL), (TL, NT))
PAST = 128
NK = NT + PAST
KEY_CTX = TL + PAST
C_PQ, C_PKV, C_PKR, C_HG = 0, QL, QL + KVL, QL + KVL + ROPE
MAIN_CHUNKS = (5280 - C_HG) // P
SCALE = float(QH) ** -0.5
LEVELS = 7
ROWS_A = (("b_mod", 48), ("g_mix", 8), ("g_ffn", 8), ("g_final", 8), ("conv_b", 22), ("g_q", 3),
          ("g_kv", 2), ("g_hg", 4), ("lb_param", 16))
ROWS_B = (("conv_w", 66), ("c", 8), ("c_ctx", 8))


def starts(rows):
    at, out = 0, {}
    for name, n in rows:
        out[name] = at
        at += n
    return out, at


AT_A, NA = starts(ROWS_A)
AT_B, NB = starts(ROWS_B)


class Arena:

    def __init__(self, nc, offset):
        self.nc, self.at = nc, offset

    def __call__(self, name, shape, dtype=F32):
        size = int(np.prod(shape[1:])) * 4
        t = self.nc.alloc_sbuf_tensor_at(name, list(shape), dtype, offset=self.at)
        self.at += (size + 31) // 32 * 32
        return t


class Signals:

    def __init__(self, nc, ctx, prefix):
        self.nc, self.prefix, self.all = nc, prefix, []
        ctx.callback(self.clear)

    def __call__(self, name):
        self.all.append(self.nc.alloc_semaphore(f"{self.prefix}_{name}"))
        return self.all[-1]

    def clear(self):
        self.nc.clear_and_free_semaphores(self.all)
        self.nc.all_engine_barrier()


def tok3(t):
    return t.rearrange("p (j c) -> p j c", j=NCH)


class WeightStream:

    def __init__(self, nc, arena, sems, tag):
        self.nc = nc
        self.raw = [arena(f"{tag}_w_raw{s}", [P, KD, P]) for s in range(2)]
        self.hi = [arena(f"{tag}_w_hi{s}", [P, KD, P], F32R) for s in range(2)]
        self.lo = [arena(f"{tag}_w_lo{s}", [P, KD, P], F32R) for s in range(2)]
        self.loaded = [sems(f"w_loaded{s}") for s in range(2)]
        self.hi_ready = sems("w_hi_ready")
        self.lo_ready = sems("w_lo_ready")
        self.used = sems("w_used")

    def load(self, sp, c, s, pairs, free=True):
        if free:
            sp.wait_ge(self.lo_ready, c - 1)
        for n, (dst, src) in enumerate(pairs):
            sp.dma_start(dst, src).then_inc(self.loaded[s], 16)

    def split_hi(self, act, s, arrived, c, free=True, size=KD * P):
        act.wait_ge(self.loaded[s], arrived)
        if free:
            act.wait_ge(self.used, c - 1)
        flat = self.raw[s][:, :, :].rearrange("p k n -> p (k n)")[:, 0:size]
        out = self.hi[s][:, :, :].rearrange("p k n -> p (k n)")[:, 0:size]
        act.activation(out, flat, ACT.Copy).then_inc(self.hi_ready, 1)

    def split_lo(self, pool, s, c, free=True, size=KD * P):
        pool.wait_ge(self.hi_ready, c + 1)
        flat = [t[s][:, :, :].rearrange("p k n -> p (k n)")[:, 0:size] for t in (self.lo, self.raw, self.hi)]
        pool.tensor_tensor(flat[0], flat[1], flat[2], ALU.subtract).then_inc(self.lo_ready, 1)


def gemm_chunk(pe, psum, w_hi, w_lo, x_hi, x_lo, kts):
    last = None
    n, total = 0, 3 * len(kts)
    for (wk, xk) in kts:
        for w, x in ((w_hi, x_hi), (w_hi, x_lo), (w_lo, x_hi)):
            for j in range(NCH):
                last = pe.matmul(psum[:, j, 0:CH], w(wk), x(xk)[:, j * CH:(j + 1) * CH],
                                 start=(n == 0), stop=(n == total - 1))
            n += 1
    return last


class Norm:

    def __init__(self, arena, sems, tag, cst, kts, width):
        self.cst, self.kts, self.width = cst, kts, width
        self.sq = [arena(f"{tag}_sq{i}", [P, NT]) for i in range(2)]
        self.acc = arena(f"{tag}_acc", [P, NT])
        self.stat = arena(f"{tag}_stat", [P, 2 * TILES])
        self.rb = arena(f"{tag}_rb", [P, NT])
        self.sq_ready = sems(f"{tag}_sq_ready")
        self.acc_ready = sems(f"{tag}_acc_ready")
        self.sums_ready = sems(f"{tag}_sums_ready")
        self.std_ready = sems(f"{tag}_std_ready")
        self.rstd_ready = sems(f"{tag}_rstd_ready")
        self.rbp_ready = sems(f"{tag}_rbp_ready")
        self.rb_ready = sems(f"{tag}_rb_ready")

    def act_square(self, act, k, src):
        if k >= 2:
            act.wait_ge(self.acc_ready, max(1, k - 2))
        act.activation(self.sq[k % 2][:, :], src, ACT.Square).then_inc(self.sq_ready, 1)

    def dve_add(self, dve, k):
        dve.wait_ge(self.sq_ready, k + 1)
        if k == 1:
            dve.tensor_tensor(self.acc[:, :], self.sq[0][:, :], self.sq[1][:, :], ALU.add).then_inc(self.acc_ready, 1)
        if k >= 2:
            dve.wait_ge(self.acc_ready, k - 1)
            dve.tensor_tensor(self.acc[:, :], self.acc[:, :], self.sq[k % 2][:, :], ALU.add).then_inc(self.acc_ready, 1)

    def pe_sums(self, pe, psum):
        pe.wait_ge(self.acc_ready, self.kts - 1)
        for t in range(TILES):
            last = pe.matmul(psum[:, t:t + 1], self.acc[:, t * P:(t + 1) * P], self.cst.ones[:, 0:1], start=True, stop=True)
        last.then_inc(self.sums_ready, 1)

    def act_std(self, act, psum):
        act.wait_ge(self.sums_ready, 1)
        act.activation(self.stat[:, 0:TILES], psum[:, 0:TILES], ACT.Sqrt, scale=1.0 / self.width,
                       bias=self.cst.eps[:, 0:1]).then_inc(self.std_ready, 1)

    def dve_rstd(self, dve):
        dve.wait_ge(self.std_ready, 1)
        dve.reciprocal(self.stat[:, TILES:2 * TILES], self.stat[:, 0:TILES]).then_inc(self.rstd_ready, 1)

    def pe_broadcast(self, pe, psum3):
        pe.wait_ge(self.rstd_ready, 1)
        for t in range(TILES):
            last = pe.matmul(psum3[:, t // 3, (t % 3) * P:(t % 3 + 1) * P],
                             self.stat[:, TILES + t:TILES + t + 1].to_broadcast([P, P]), self.cst.ident[:, :],
                             start=True, stop=True)
        last.then_inc(self.rbp_ready, 1)

    def act_broadcast(self, act, psum3):
        act.wait_ge(self.rbp_ready, 1)
        act.activation(tok3(self.rb[:, :]), psum3[:, 0:NCH, 0:CH], ACT.Copy).then_inc(self.rb_ready, 1)


class Apply:

    def __init__(self, arena, sems, tag, norm):
        self.norm = norm
        self.y = [arena(f"{tag}_y{i}", [P, NT]) for i in range(2)]
        self.scaled = sems(f"{tag}_scaled")
        self.y_ready = sems(f"{tag}_y_ready")
        self.hi_ready = sems(f"{tag}_hi_ready")
        self.lo_ready = sems(f"{tag}_lo_ready")

    def dve(self, dve, k, src, affine):
        y = self.y[k % 2]
        dve.wait_ge(self.norm.rb_ready, 1)
        if k >= 2:
            dve.wait_ge(self.lo_ready, k - 1)
        dve.tensor_tensor(y[:, :], src, self.norm.rb[:, :], ALU.mult).then_inc(self.scaled, 1)
        dve.wait_ge(self.scaled, k + 1)
        for a, b, gain, bias in affine:
            if bias is None:
                last = dve.tensor_scalar(y[:, a:b], y[:, a:b], gain, None, ALU.mult)
            else:
                last = dve.tensor_scalar(y[:, a:b], y[:, a:b], gain, bias, ALU.mult, ALU.add)
        last.then_inc(self.y_ready, 1)

    def act(self, act, k, parts):
        act.wait_ge(self.y_ready, k + 1)
        for dst, a, b in parts:
            last = act.activation(dst, self.y[k % 2][:, a:b], ACT.Copy)
        last.then_inc(self.hi_ready, 1)

    def pool(self, pool, k, parts):
        pool.wait_ge(self.hi_ready, k + 1)
        for dst, hi, a, b in parts:
            last = pool.tensor_tensor(dst, self.y[k % 2][:, a:b], hi, ALU.subtract)
        last.then_inc(self.lo_ready, 1)


class Constants:

    def __init__(self, arena):
        self.ident = arena("ident", [P, P])
        self.ones = arena("ones", [P, P])
        self.eps = arena("eps", [P, 8])
        self.cols_a = arena("cols_a", [P, NA])
        self.cols_b = arena("cols_b", [P, NB])
        self.mod = arena("mod", [P, 48, 2])
        self.gain_mix = arena("gain_mix", [P, KD, 2])
        self.gain_ffn = arena("gain_ffn", [P, KD, 2])
        self.lb = arena("lb", [P, 8])
        self.lb1 = arena("lb1", [P, 8])

    def a(self, name, k):
        return self.cols_a[:, AT_A[name] + k:AT_A[name] + k + 1]

    def b(self, name, k):
        return self.cols_b[:, AT_B[name] + k:AT_B[name] + k + 1]


def stage_setup(nc, io, cst, arena, h_hi, h_lo):
    with ExitStack() as ctx:
        sems = Signals(nc, ctx, "s1")
        rows_a, rows_b = arena("rows_a", [P, P]), arena("rows_b", [P, P])
        x_rows = [arena(f"x_rows{i}", [P, D]) for i in range(2)]
        w_mod = [arena(f"w_mod{i}", [P, KD, 512]) for i in range(2)]
        silu_c = arena("silu_c", [P, 2, KD])
        cc = arena("cc", [P, KD, 2])
        mod_rows = arena("mod_rows", [2, 6 * D])
        x_t = arena("x_t", [P, KD, NT])
        lbt = arena("lbt", [P, 24])
        psum = ctx.enter_context(nc.psum_tensor("s1_psum", [P, 8, 512], F32))
        norm = Norm(arena, sems, "n1", cst, KD, D)
        app = Apply(arena, sems, "a1", norm)
        consts_loaded, ones_set = sems("consts_loaded"), sems("ones_set")
        x_loaded = [sems(f"x_loaded{i}") for i in range(2)]
        wm_loaded = [sems(f"wm_loaded{i}") for i in range(2)]
        vec_t, vec_cols = sems("vec_transposed"), sems("vec_columns")
        silu_ready, cc_ready = sems("silu_ready"), sems("cc_ready")
        xt_ps, xt_ready = sems("x_transposed"), sems("x_t_ready")
        mod_ps, mod_row = sems("mod_product"), sems("mod_row_ready")
        modt_ps, mod_ready = sems("mod_transposed"), sems("mod_ready")
        gain1, lb_exp, lb_step = sems("gain_ready"), sems("lb_exp"), sems("lb_step")
        x_stored = sems("x_stored")
        mod_chunks = 6 * D // 512
        first = 4
        n_a = sum(n for _, n in ROWS_A)

        with nc.Block() as block:
            @block.sync
            def _(sp):
                sp.dma_start(cst.ident[:, :], io["ident"]).then_inc(consts_loaded, 16)
                for rows, at, spec in ((rows_a, AT_A, ROWS_A), (rows_b, AT_B, ROWS_B)):
                    for name, n in spec:
                        sp.dma_start(rows[at[name]:at[name] + n, :], io[name]).then_inc(consts_loaded, 16)
                for n in range(mod_chunks):
                    if n >= 2:
                        sp.wait_ge(mod_ps, n - 1)
                    sp.dma_start(w_mod[n % 2][:, :, :],
                                 io["w_mod"][:, n * 512:(n + 1) * 512].rearrange("(k p) n -> p k n", p=P)
                                 ).then_inc(wm_loaded[n % 2], 16)
                sp.wait_ge(xt_ready, 2 * TILES)
                sp.dma_start(io["x_t"].rearrange("(k p) n -> p k n", p=P), x_t[:, :, :]).then_inc(x_stored, 16)
                sp.wait_ge(x_stored, 16)

            @block.gpsimd
            def _(pool):
                pool.memset(cst.ones[:, :], 1.0)
                pool.memset(cst.eps[:, :], EPS).then_inc(ones_set, 1)
                for t in range(TILES):
                    if t >= 2:
                        pool.wait_ge(xt_ps, 2 * (t - 1))
                    pool.dma_start(x_rows[t % 2][:, :], io["x"](t)).then_inc(x_loaded[t % 2], 16)
                for k in range(KD):
                    app.pool(pool, k, [(h_lo[:, k, :], h_hi[:, k, :], 0, NT)])

            @block.tensor
            def _(pe):
                pe.wait_ge(consts_loaded, 16 * (1 + len(ROWS_A) + len(ROWS_B)))
                pe.transpose(psum[:, 0, 0:NA], rows_a[0:NA, :], cst.ident[0:NA, 0:NA])
                pe.transpose(psum[:, 0, P:P + NB], rows_b[0:NB, :], cst.ident[0:NB, 0:NB]).then_inc(vec_t, 1)
                for t in range(TILES):
                    pe.wait_ge(x_loaded[t % 2], 16 * (t // 2 + 1))
                    for half in range(2):
                        r = 2 * t + half
                        if r >= 2:
                            pe.wait_ge(xt_ready, r - 1)
                        for k in range(4):
                            f = 4 * half + k
                            last = pe.transpose(psum[:, 1 + r % 2, k * P:(k + 1) * P],
                                                x_rows[t % 2][:, f * P:(f + 1) * P], cst.ident[:, :])
                        last.then_inc(xt_ps, 1)

                def products(n):
                    pe.wait_ge(wm_loaded[n % 2], 16 * (n // 2 + 1))
                    if n >= 2:
                        pe.wait_ge(mod_row, n - 1)
                    for k in range(KD):
                        last = pe.matmul(psum[0:2, 3 + n % 2, :], cc[:, k, :], w_mod[n % 2][:, k, :],
                                         start=(k == 0), stop=(k == KD - 1))
                    last.then_inc(mod_ps, 1)

                def columns(a, b):
                    pe.wait_ge(mod_row, (b + 3) // 4)
                    for j in range(a, b):
                        last = pe.transpose(psum[:, 0, 256 + 2 * j:256 + 2 * j + 2], mod_rows[0:2, j * P:(j + 1) * P],
                                            cst.ident[0:2, 0:2])
                    last.then_inc(modt_ps, 1)

                pe.wait_ge(cc_ready, 1)
                for n in range(first):
                    products(n)
                columns(0, 4 * first)
                pe.wait_ge(ones_set, 1)
                norm.pe_sums(pe, psum[:, 5, :])
                pe.wait_ge(xt_ready, 2 * TILES)
                norm.pe_broadcast(pe, psum[:, 5:8, :])
                for n in range(first, mod_chunks):
                    products(n)
                pe.wait_ge(mod_ready, 1)
                columns(4 * first, 4 * mod_chunks)

            @block.scalar
            def _(act):
                act.wait_ge(vec_cols, 1)
                act.activation(silu_c[:, :, :].rearrange("p g k -> p (g k)"), cst.cols_b[:, AT_B["c"]:NB],
                               ACT.Silu).then_inc(silu_ready, 1)
                act.wait_ge(silu_ready, 1)
                act.activation(cc[:, :, :], silu_c[:, :, :].rearrange("p g k -> p k g"), ACT.Copy).then_inc(cc_ready, 1)
                act.wait_ge(lb_step, 1)
                act.activation(lbt[:, 8:24], lbt[:, 8:24], ACT.Exp).then_inc(lb_exp, 1)
                act.wait_ge(xt_ready, 2 * TILES)

                def rows(n):
                    act.wait_ge(mod_ps, n + 1)
                    act.activation(mod_rows[0:2, n * 512:(n + 1) * 512], psum[0:2, 3 + n % 2, :],
                                   ACT.Copy).then_inc(mod_row, 1)

                rows(0)
                for k in range(KD):
                    norm.act_square(act, k, x_t[:, k, :])
                    if k % 2 == 1 and k < 7:
                        rows((k + 1) // 2)
                act.wait_ge(ones_set, 1)
                norm.act_std(act, psum[:, 5, :])
                norm.act_broadcast(act, psum[:, 5:8, :])
                for n in range(first, mod_chunks):
                    if n - first < KD:
                        app.act(act, n - first, [(h_hi[:, n - first, :], 0, NT)])
                    rows(n)

            @block.vector
            def _(dve):
                dve.wait_ge(vec_t, 1)
                dve.tensor_copy(cst.cols_a[:, :], psum[:, 0, 0:NA])
                dve.tensor_copy(cst.cols_b[:, :], psum[:, 0, P:P + NB]).then_inc(vec_cols, 1)
                dve.wait_ge(vec_cols, 1)
                lb0 = cst.cols_a[:, AT_A["lb_param"]:AT_A["lb_param"] + 8]
                lb1 = cst.cols_a[:, AT_A["lb_param"] + 8:AT_A["lb_param"] + 16]
                n_lb = [0]

                def step(ins):
                    ins.then_inc(lb_step, 1)
                    n_lb[0] += 1
                    dve.wait_ge(lb_step, n_lb[0])

                dve.tensor_tensor(lbt[:, 0:8], lb0, lb1, ALU.max).then_inc(vec_cols, 1)
                dve.wait_ge(vec_cols, 2)
                dve.tensor_tensor(lbt[:, 8:16], lb0, lbt[:, 0:8], ALU.subtract)
                step(dve.tensor_tensor(lbt[:, 16:24], lb1, lbt[:, 0:8], ALU.subtract))
                dve.wait_ge(lb_exp, 1)
                step(dve.tensor_tensor(lbt[:, 0:8], lbt[:, 8:16], lbt[:, 16:24], ALU.add))
                step(dve.reciprocal(lbt[:, 0:8], lbt[:, 0:8]))
                step(dve.tensor_tensor(cst.lb[:, :], lbt[:, 8:16], lbt[:, 0:8], ALU.mult))
                step(dve.tensor_scalar(cst.lb1[:, :], cst.lb[:, :], -1.0, 1.0, ALU.mult, ALU.add))
                for r in range(2 * TILES):
                    t, half = r // 2, r % 2
                    dve.wait_ge(xt_ps, r + 1)
                    dve.tensor_copy(x_t[:, 4 * half:4 * half + 4, t * P:(t + 1) * P],
                                    psum[:, 1 + r % 2, :].rearrange("p (k n) -> p k n", k=4)).then_inc(xt_ready, 1)
                for k in range(KD):
                    norm.dve_add(dve, k)

                def finish(a, b, part):
                    dve.wait_ge(modt_ps, part)
                    dve.tensor_tensor(cst.mod[:, a:b, :],
                                      psum[:, 0, 256 + 2 * a:256 + 2 * b].rearrange("p (j g) -> p j g", g=2),
                                      cst.cols_a[:, a:b].unsqueeze(2).to_broadcast([P, b - a, 2]), ALU.add
                                      ).then_inc(mod_ready, 1)
                    dve.wait_ge(mod_ready, part)

                def gain(dst, sc, g, count):
                    dve.tensor_scalar(dst[:, :, :], cst.mod[:, sc:sc + KD, :], 1.0, None, ALU.add).then_inc(gain1, 1)
                    dve.wait_ge(gain1, count)
                    dve.tensor_tensor(dst[:, :, :], dst[:, :, :],
                                      cst.cols_a[:, AT_A[g]:AT_A[g] + KD].unsqueeze(2).to_broadcast([P, KD, 2]),
                                      ALU.mult).then_inc(gain1, 1)
                    dve.wait_ge(gain1, count + 1)

                finish(0, 4 * first, 1)
                gain(cst.gain_mix, KD, "g_mix", 1)
                norm.dve_rstd(dve)
                for k in range(KD):
                    app.dve(dve, k, x_t[:, k, :], [(a, b, cst.gain_mix[:, k, g:g + 1], cst.mod[:, k, g:g + 1])
                                                   for g, (a, b) in enumerate(GROUPS)])
                finish(4 * first, 48, 2)
                gain(cst.gain_ffn, 4 * KD, "g_ffn", 3)


def stage_in_projection(nc, io, cst, arena, h_hi, h_lo, pqkv, pkr):
    with ExitStack() as ctx:
        sems = Signals(nc, ctx, "s2")
        w = WeightStream(nc, arena, sems, "s2")
        stage = [arena(f"s2_stage{i}", [P, NT]) for i in range(2)]
        psum = [ctx.enter_context(nc.psum_tensor(f"s2_psum{i}", [P, 4, 512], F32)) for i in range(2)]
        done, copied = sems("product"), sems("copied")
        stored = [sems(f"stored{i}") for i in range(2)]
        rot_ready = sems("rot_ready")
        tail = 6
        total = MAIN_CHUNKS + tail
        w_in = io["w_in"].rearrange("(k p) n -> p k n", p=P)

        with nc.Block() as block:
            @block.sync
            def _(sp):
                def load(c, s, free=True):
                    w.load(sp, c, s, [(w.raw[s][:, :, :], w_in[:, :, bass.ds(C_HG + c * P, P)])], free)

                def store(c, s):
                    sp.wait_ge(copied, c + 1)
                    sp.dma_start(io["proj"][bass.ds(c * P, P), :], stage[s][:, :]).then_inc(stored[s], 16)

                load(0, 0, False)
                load(1, 1, False)
                with sp.Fori(0, MAIN_CHUNKS // 2 - 1) as i:
                    for s in range(2):
                        load(2 * i + (2 + s), s)
                        store(2 * i + s, s)
                for c in range(MAIN_CHUNKS, total):
                    s = c % 2
                    m = c - MAIN_CHUNKS
                    if m < 5:
                        w.load(sp, c, s, [(w.raw[s][:, :, :], w_in[:, :, m * P:(m + 1) * P])])
                    else:
                        w.load(sp, c, s, [(w.raw[s][:, :, 0:96], w_in[:, :, C_PKR - 64:C_PKR + 32])])
                    if m < 2:
                        store(c - 2, s)
                for s in range(2):
                    sp.wait_ge(stored[s], 16 * MAIN_CHUNKS // 2)

            @block.scalar
            def _(act):
                w.split_hi(act, 0, 16, 0, False)
                w.split_hi(act, 1, 16, 1, False)
                with act.Fori(1, MAIN_CHUNKS // 2) as i:
                    for s in range(2):
                        w.split_hi(act, s, 16 * i + 16, 2 * i + s)
                for c in range(MAIN_CHUNKS, total):
                    s = c % 2
                    if c == total - 1:
                        act.wait_ge(w.loaded[s], 16 * (c // 2 + 1))
                        act.activation(w.raw[s][:, :, 96:112], w.raw[s][:, :, 80:96], ACT.Copy, scale=-1.0)
                        act.activation(w.raw[s][:, :, 112:128], w.raw[s][:, :, 64:80], ACT.Copy).then_inc(rot_ready, 1)
                        act.wait_ge(rot_ready, 1)
                    w.split_hi(act, s, 16 * (c // 2 + 1), c)

            @block.gpsimd
            def _(pool):
                with pool.Fori(0, total // 2) as i:
                    for s in range(2):
                        w.split_lo(pool, s, 2 * i + s)

            @block.tensor
            def _(pe):
                def chunk(c, s, free):
                    pe.wait_ge(w.lo_ready, c + 1)
                    if free:
                        pe.wait_ge(copied, c - 1)
                    last = gemm_chunk(pe, psum[s], lambda k: w.hi[s][:, k, :], lambda k: w.lo[s][:, k, :],
                                      lambda k: h_hi[:, k, :], lambda k: h_lo[:, k, :], [(k, k) for k in range(KD)])
                    last.then_inc(w.used, 1)

                chunk(0, 0, False)
                chunk(1, 1, False)
                with pe.Fori(1, total // 2) as i:
                    for s in range(2):
                        chunk(2 * i + s, s, True)

            @block.vector
            def _(dve):
                def copy(c, s, dst):
                    dve.wait_ge(w.used, c + 1)
                    dve.tensor_copy(tok3(dst), psum[s][:, 0:NCH, 0:CH]).then_inc(copied, 1)

                copy(0, 0, stage[0][:, :])
                copy(1, 1, stage[1][:, :])
                with dve.Fori(1, MAIN_CHUNKS // 2) as i:
                    for s in range(2):
                        dve.wait_ge(stored[s], 16 * i)
                        copy(2 * i + s, s, stage[s][:, :])
                for m in range(5):
                    copy(MAIN_CHUNKS + m, m % 2, pqkv[:, m, :])
                dve.wait_ge(w.used, total)
                dve.tensor_copy(tok3(pkr[64:128, :]), psum[1][64:128, 0:NCH, 0:CH]).then_inc(copied, 1)


def stage_low_rank(nc, io, cst, arena, pqkv, pkr, rope, q_hi, q_lo, c_hi, c_lo, k_hi, k_lo):
    with ExitStack() as ctx:
        sems = Signals(nc, ctx, "s3")
        norm_kv, norm_q = Norm(arena, sems, "nkv", cst, 2, KVL), Norm(arena, sems, "nq", cst, 3, QL)
        app_kv, app_q = Apply(arena, sems, "akv", norm_kv), Apply(arena, sems, "aq", norm_q)
        ckv_rows = arena("ckv_rows", [P, KVL])
        kr_rows = arena("kr_rows", [P, 96])
        ckv_t = arena("ckv_t", [P, 2, PAST])
        key = arena("key", [P, NK])
        part = [arena(f"rope_part{i}", [P, NT]) for i in range(2)]
        out_ckv = arena("out_ckv", [P, KVL])
        out_kr = arena("out_kr", [P, ROPE])
        psum = ctx.enter_context(nc.psum_tensor("s3_psum", [P, 8, 512], F32))
        loaded, cleared = sems("loaded"), sems("cleared")
        cache_t, cache_copied = sems("cache_transposed"), sems("cache_copied")
        parts_ready, key_ready = sems("parts_ready"), sems("key_ready")
        cache_hi, key_hi = sems("cache_hi"), sems("key_hi")
        ckv_out_t, outs, stored = sems("ckv_out_transposed"), sems("outs"), sems("stored")
        r = slice(64, 96)

        def places(k, dst):
            return [(dst[:, k, 0:TL], 0, TL), (dst[:, k, KEY_CTX:NK], TL, NT)]

        with nc.Block() as block:
            @block.sync
            def _(sp):
                sp.dma_start(ckv_rows[:, :], io["cache_ckv"]).then_inc(loaded, 16)
                sp.wait_ge(cleared, 1)
                sp.dma_start(kr_rows[:, 64:96], io["cache_krope"]).then_inc(loaded, 16)
                sp.dma_start(rope[64:128, :], io["rope"]).then_inc(loaded, 16)
                sp.wait_ge(outs, 1)
                sp.dma_start(io["new_krope"], out_kr[:, :]).then_inc(stored, 16)
                sp.wait_ge(outs, 2)
                sp.dma_start(io["new_ckv"], out_ckv[:, :]).then_inc(stored, 16)
                sp.wait_ge(stored, 32)

            @block.gpsimd
            def _(pool):
                pool.memset(kr_rows[:, :], 0.0).then_inc(cleared, 1)
                pool.wait_ge(cache_hi, 1)
                pool.tensor_tensor(c_lo[:, :, TL:KEY_CTX], ckv_t[:, :, :], c_hi[:, :, TL:KEY_CTX], ALU.subtract)
                for k in range(2):
                    app_kv.pool(pool, k, [(lo, hi, a, b) for (lo, a, b), (hi, _, _) in zip(places(k, c_lo), places(k, c_hi))])
                for k in range(3):
                    app_q.pool(pool, k, [(q_lo[:, k, :], q_hi[:, k, :], 0, NT)])

            @block.tensor
            def _(pe):
                pe.wait_ge(loaded, 48)
                for k in range(2):
                    pe.transpose(psum[:, 0, k * P:(k + 1) * P], ckv_rows[:, k * P:(k + 1) * P], cst.ident[:, :])
                pe.transpose(psum[0:96, 0, 256:384], kr_rows[:, :], cst.ident[:, :])
                pe.transpose(psum[:, 0, 384:384 + ROPE], pkr[r, TL:NT], cst.ident[r, r]).then_inc(cache_t, 1)
                norm_kv.pe_sums(pe, psum[:, 2, :])
                norm_kv.pe_broadcast(pe, psum[:, 2:5, :])
                norm_q.pe_sums(pe, psum[:, 5, :])
                norm_q.pe_broadcast(pe, psum[:, 5:8, :])
                pe.wait_ge(app_kv.y_ready, 2)
                for k in range(2):
                    last = pe.transpose(psum[:, 1, k * P:(k + 1) * P], app_kv.y[k][:, TL:NT], cst.ident[:, :])
                last.then_inc(ckv_out_t, 1)

            @block.scalar
            def _(act):
                for k in range(2):
                    norm_kv.act_square(act, k, pqkv[:, 3 + k, :])
                for k in range(3):
                    norm_q.act_square(act, k, pqkv[:, k, :])
                norm_kv.act_std(act, psum[:, 2, :])
                norm_kv.act_broadcast(act, psum[:, 2:5, :])
                norm_q.act_std(act, psum[:, 5, :])
                norm_q.act_broadcast(act, psum[:, 5:8, :])
                act.wait_ge(cache_copied, 1)
                act.activation(c_hi[:, :, TL:KEY_CTX], ckv_t[:, :, :], ACT.Copy).then_inc(cache_hi, 1)
                act.wait_ge(key_ready, 1)
                act.activation(k_hi[0][r, :], key[r, :], ACT.Copy)
                act.activation(k_hi[1][r, :], key[r, :], ACT.Copy).then_inc(key_hi, 1)
                for k in range(2):
                    app_kv.act(act, k, places(k, c_hi))
                for k in range(3):
                    app_q.act(act, k, [(q_hi[:, k, :], 0, NT)])

            @block.vector
            def _(dve):
                for k in range(2):
                    norm_kv.dve_add(dve, k)
                for k in range(3):
                    norm_q.dve_add(dve, k)
                norm_kv.dve_rstd(dve)
                norm_q.dve_rstd(dve)
                dve.wait_ge(cache_t, 1)
                dve.tensor_copy(ckv_t[:, :, :], psum[:, 0, 0:256].rearrange("p (k n) -> p k n", k=2)).then_inc(cache_copied, 1)
                dve.tensor_copy(key[r, TL:KEY_CTX], psum[r, 0, 256:384])
                dve.tensor_copy(out_kr[:, :], psum[:, 0, 384:384 + ROPE]).then_inc(outs, 1)
                dve.wait_ge(loaded, 48)
                dve.tensor_tensor(part[0][r, :], pkr[r, :], rope[r, :], ALU.mult)
                dve.tensor_tensor(part[1][r, :], pkr[96:128, :], rope[96:128, :], ALU.mult).then_inc(parts_ready, 1)
                dve.wait_ge(parts_ready, 1)
                dve.tensor_tensor(key[r, 0:TL], part[0][r, 0:TL], part[1][r, 0:TL], ALU.add)
                dve.tensor_tensor(key[r, KEY_CTX:NK], part[0][r, TL:NT], part[1][r, TL:NT], ALU.add).then_inc(key_ready, 1)
                dve.wait_ge(key_hi, 1)
                for b in range(2):
                    dve.tensor_tensor(k_lo[b][r, :], key[r, :], k_hi[b][r, :], ALU.subtract)
                for k in range(2):
                    app_kv.dve(dve, k, pqkv[:, 3 + k, :], [(0, NT, cst.a("g_kv", k), None)])
                for k in range(3):
                    app_q.dve(dve, k, pqkv[:, k, :], [(0, NT, cst.a("g_q", k), None)])
                dve.wait_ge(ckv_out_t, 1)
                dve.tensor_copy(out_ckv[:, :], psum[:, 1, 0:256]).then_inc(outs, 1)


HEAD_STEPS = (("S", 0), ("S", 1), ("T", 0), ("Q", 0), ("T", 1), ("S", 2), ("S", 3), ("T", 2), ("K", 0), ("T", 3),
              ("S", 4), ("V", 0), ("S", 5), ("T", 4), ("S", 6), ("T", 5), ("S", 7), ("T", 6), ("S", 8), ("T", 7),
              ("X", 0), ("V", 1), ("T", 8), ("V", 2))
LAST_STEPS = tuple(x for x in HEAD_STEPS if x[0] not in "QKX")
NEXT_STEPS = (("Q", 0), ("K", 0), ("X", 0))
ROUNDS = {"S": 0, "Q": 0, "K": 0, "T": 3, "X": 4, "V": 1}


def numbered(steps):
    slot = rnd = 0
    out = []
    for kind, u in steps:
        out.append((kind, u, slot, rnd))
        slot += kind in "SQK"
        rnd += 1 if (kind, u) == ("T", 8) else ROUNDS[kind]
    return out, slot, rnd


HIS = {"S": 0, "Q": 0, "K": 0, "T": 3, "X": 4, "V": 0}
STEP_CHAIN = {"S": 1, "Q": 1, "K": 0, "T": 1, "X": 0, "V": 0}
STEPS, SLOTS, RNDS = numbered(HEAD_STEPS)
LAST, _, _ = numbered(LAST_STEPS)
NEXT, SLOTS0, RNDS0 = numbered(NEXT_STEPS)


def stage_attention(nc, io, cst, arena, rope, qn_hi, qn_lo, c_hi, c_lo, k_hi, k_lo):
    with ExitStack() as ctx:
        sems = Signals(nc, ctx, "s4")
        hw_raw = [arena(f"hw_raw{e}", [P, 5, P]) for e in range(2)]
        hw_hi = [arena(f"hw_hi{e}", [P, 5, P], F32R) for e in range(2)]
        hw_lo = [arena(f"hw_lo{e}", [P, 5, P], F32R) for e in range(2)]
        qf = arena("qf", [P, NT])
        part = [arena(f"q_part{i}", [P, NT]) for i in range(2)]
        q_hi = [arena(f"q_hi{e}", [P, NT], F32R) for e in range(2)]
        q_lo = [arena(f"q_lo{e}", [P, NT], F32R) for e in range(2)]
        kvf = arena("kvf", [P, NK])
        v_hi = [arena(f"v_hi{e}", [P, 10, P], F32R) for e in range(2)]
        v_lo = [arena(f"v_lo{e}", [P, 10, P], F32R) for e in range(2)]
        prob = [arena(f"prob{i}", [P, NT]) for i in range(2)]
        pt_hi = arena("pt_hi", [P, TILES, 512], F32R)
        pt_lo = arena("pt_lo", [P, TILES, 512], F32R)
        out = [arena(f"att_out{e}", [P, NT]) for e in range(2)]
        small = arena("att_small", [P, 8])
        top, bias, total, inv = (small[:, 2 * n:2 * n + 2] for n in range(4))
        ps_s = [ctx.enter_context(nc.psum_tensor(f"ps_s{i}", [P, 3, 512], F32)) for i in range(2)]
        ps_t = [ctx.enter_context(nc.psum_tensor(f"ps_t{i}", [P, 512], F32)) for i in range(2)]
        hw_loaded = [sems(f"hw_loaded{e}") for e in range(2)]
        hw_rot, hw_hi_ready, hw_lo_ready = sems("hw_rot"), sems("hw_hi_ready"), sems("hw_lo_ready")
        s_full, s_read = sems("s_full"), sems("s_read")
        t_full, t_hi, t_free = sems("t_full"), sems("t_hi"), sems("t_free")
        bias_ready, p_ready, dve_step = sems("bias_ready"), sems("p_ready"), sems("dve_step")
        q_roped, q_hi_ready, q_ready = sems("q_roped"), sems("q_hi_ready"), sems("q_ready")
        k_hi_ready, k_ready = sems("k_hi_ready"), sems("k_ready")
        o_stored = [sems(f"o_stored{e}") for e in range(2)]
        r = slice(64, 96)
        uq = io["w_uq"].rearrange("(k p) n -> p k n", p=P)
        ukv = io["w_ukv"].rearrange("(k p) n -> p k n", p=P)

        def heads(engine, one):
            def pair(i, first, last):
                for e in range(2):
                    end = last and e == 1
                    one(i, 2 * i + e, e, LAST if end else STEPS, first, end)
            pair(0, True, False)
            with engine.Fori(1, HEADS // 2 - 1) as i:
                pair(i, False, False)
            pair(HEADS // 2 - 1, False, True)

        def rounds_of(kind, u, rnd):
            if kind == "X":
                return [(rnd + n, 3 * n, min(3, 10 - 3 * n)) for n in range(4)]
            if u == 8:
                return [(rnd, 0, 1)]
            return [(rnd + n, 3 * n, 3) for n in range(3)]

        with nc.Block() as block:
            @block.sync
            def _(sp):
                def load(h, e, free):
                    if free:
                        sp.wait_ge(hw_lo_ready, h - 1)
                    sp.dma_start(hw_raw[e][:, 0:3, 0:QH], uq[:, :, bass.ds(h * QH, QH)]).then_inc(hw_loaded[e], 16)
                    sp.dma_start(hw_raw[e][:, 3:5, :], ukv[:, :, bass.ds(h * P, P)]).then_inc(hw_loaded[e], 16)

                load(0, 0, False)

                def one(i, h, e, steps, first, last):
                    if not last:
                        load(h + 1, 1 - e, not (first and e == 0))
                    for kind, u, slot, rnd in steps:
                        if kind == "V":
                            a, n = (u * 512, 512) if u < 2 else (TL, TC)
                            sp.wait_ge(t_free, RNDS0 + h * RNDS + rnd + 1)
                            sp.dma_start(io["o_mla"][bass.ds(h * VD, VD), a:a + n],
                                         out[e][64:128, a:a + n]).then_inc(o_stored[e], 16)

                heads(sp, one)
                for e in range(2):
                    sp.wait_ge(o_stored[e], 16 * 3 * HEADS // 2)

            @block.tensor
            def _(pe):
                def scores(slot_buf, e, u):
                    chunks = [(0, TC, KEY_CTX)] if u == 8 else [(j, CH, j * CH) for j in range(NCH)]
                    for n, (a, b) in enumerate(((q_hi, k_hi), (q_hi, k_lo), (q_lo, k_hi))):
                        for j, width, col in chunks:
                            last = pe.matmul(ps_s[slot_buf][:, j, 0:width], a[e][0:QH, u * P:(u + 1) * P],
                                             b[e][0:QH, col:col + width], start=(n == 0), stop=(n == 2))
                    return last

                def step(kind, u, slot, rnd, h, e, slots, rounds, at_slot, waits=True):
                    n = 1 - e
                    s = (slot + at_slot) % 2
                    if kind in "SQK":
                        if waits:
                            pe.wait_ge(s_read, slots + (slot - 1))
                    if kind == "S":
                        if u == 0:
                            pe.wait_ge(q_ready, h + 1)
                            pe.wait_ge(k_ready, h + 1)
                        scores(s, e, u).then_inc(s_full, 1)
                    if kind == "Q":
                        pe.wait_ge(hw_lo_ready, h + 2)
                        last = gemm_chunk(pe, ps_s[s], lambda k: hw_hi[n][:, k, :], lambda k: hw_lo[n][:, k, :],
                                          lambda k: qn_hi[:, k, :], lambda k: qn_lo[:, k, :], [(k, k) for k in range(3)])
                        last.then_inc(s_full, 1)
                    if kind == "K":
                        for j, width in ((0, 512), (1, 512), (2, 256)):
                            m = 0
                            for k in range(2):
                                for a, b in ((hw_hi, c_hi), (hw_hi, c_lo), (hw_lo, c_hi)):
                                    last = pe.matmul(ps_s[s][:, j, 0:width], a[n][:, 3 + k, :],
                                                     b[:, k, j * 512:j * 512 + width], start=(m == 0), stop=(m == 5))
                                    m += 1
                        last.then_inc(s_full, 1)
                    if kind in "TX":
                        if kind == "T":
                            pe.wait_ge(p_ready, h * TILES + (u + 1))
                        else:
                            pe.wait_ge(k_ready, h + 2)
                        for q, first, tiles in rounds_of(kind, u, rnd):
                            b = q % 2
                            src = kvf if kind == "X" else prob[(e * TILES + u) % 2]
                            if waits or q >= 2:
                                pe.wait_ge(t_free, rounds + (q - 1))
                            for x in range(tiles):
                                last = pe.transpose(ps_t[b][:, x * P:(x + 1) * P],
                                                    src[:, (first + x) * P:(first + x + 1) * P], cst.ident[:, :])
                            last.then_inc(t_full, 1)
                    if kind == "V":
                        pe.wait_ge(t_free, rounds + rnd)
                        group = [(9, 0)] if u == 2 else [(k, k) for k in range(TILES)]
                        width, m = (TC, 0) if u == 2 else (512, 0)
                        for kv, kp in group:
                            for a, b in ((v_hi, pt_hi), (v_hi, pt_lo), (v_lo, pt_hi)):
                                last = pe.matmul(ps_t[rnd % 2][:, 0:width], a[e][:, kv, :], b[:, kp, 0:width],
                                                 start=(m == 0), stop=(m == 3 * len(group) - 1))
                                m += 1
                        last.then_inc(t_full, 1)

                for kind, u, slot, rnd in NEXT:
                    step(kind, u, slot, rnd, -1, 1, 0, 0, 0, False)

                def one(i, h, e, steps, first, last):
                    for kind, u, slot, rnd in steps:
                        step(kind, u, slot, rnd, h, e, SLOTS0 + h * SLOTS, RNDS0 + h * RNDS, e * SLOTS)

                heads(pe, one)

            @block.scalar
            def _(act):
                def split(h, e, uses):
                    act.wait_ge(hw_loaded[e], 32 * uses)
                    act.activation(hw_raw[e][:, 0:3, 96:112], hw_raw[e][:, 0:3, 80:96], ACT.Copy, scale=-1.0)
                    act.activation(hw_raw[e][:, 0:3, 112:128], hw_raw[e][:, 0:3, 64:80], ACT.Copy).then_inc(hw_rot, 1)
                    act.wait_ge(hw_rot, h + 1)
                    act.activation(hw_hi[e][:, :, :], hw_raw[e][:, :, :], ACT.Copy).then_inc(hw_hi_ready, 1)

                def step(kind, u, slot, rnd, h, e, slots, rounds, at_slot):
                    n = 1 - e
                    s = (slot + at_slot) % 2
                    if kind == "S":
                        b = (e * TILES + u) % 2
                        act.wait_ge(bias_ready, h * TILES + (u + 1))
                        if u == 8:
                            src, dst = ps_s[s][:, 0, 0:TC], prob[b][:, 0:TC]
                        else:
                            src, dst = ps_s[s][:, 0:NCH, 0:CH], tok3(prob[b][:, :])
                        act.activation(dst, src, ACT.Exp, bias=bias[:, b:b + 1], scale=SCALE,
                                       accum_out=total[:, b:b + 1]).then_inc(s_read, 1)
                    if kind == "Q":
                        act.wait_ge(q_roped, h + 2)
                        act.activation(tok3(qf[0:64, :]), ps_s[s][0:64, 0:NCH, 0:CH], ACT.Copy).then_inc(s_read, 1)
                        act.wait_ge(s_read, slots + (slot + 1))
                        act.activation(q_hi[n][0:QH, :], qf[0:QH, :], ACT.Copy).then_inc(q_hi_ready, 1)
                    if kind == "K":
                        act.wait_ge(s_full, slots + (slot + 1))
                        act.activation(kvf[:, :], ps_s[s][:, :, :].rearrange("p j c -> p (j c)")[:, 0:NK],
                                       ACT.Copy).then_inc(s_read, 1)
                        act.wait_ge(s_read, slots + (slot + 1))
                        act.activation(k_hi[n][0:64, :], kvf[0:64, :], ACT.Copy).then_inc(k_hi_ready, 1)
                    if kind in "TX":
                        for q, first, tiles in rounds_of(kind, u, rnd):
                            act.wait_ge(t_full, rounds + (q + 1))
                            src = ps_t[q % 2][:, 0:tiles * P].rearrange("p (t n) -> p t n", n=P)
                            if kind == "X":
                                dst = v_hi[n][:, first:first + tiles, :]
                            else:
                                dst = pt_hi[:, first:first + tiles, (u % 4) * P:(u % 4 + 1) * P]
                            act.activation(dst, src, ACT.Copy).then_inc(t_hi, 1)

                split(0, 0, 1)
                for kind, u, slot, rnd in NEXT:
                    step(kind, u, slot, rnd, -1, 1, 0, 0, 0)

                def one(i, h, e, steps, first, last):
                    if not last:
                        split(h + 1, 1 - e, i + 1 + e)
                    for kind, u, slot, rnd in steps:
                        step(kind, u, slot, rnd, h, e, SLOTS0 + h * SLOTS, RNDS0 + h * RNDS, e * SLOTS)

                heads(act, one)


            @block.vector
            def _(dve):
                def steps_of(steps, i, h, e, slots, rounds, at_slot, his, chain, first):
                    n = 1 - e
                    slot_of = {u: slot for kind, u, slot, _ in steps if kind == "S"}
                    n_hi = n_step = 0
                    for kind, u, slot, rnd in steps:
                        s = (slot + at_slot) % 2
                        b = (e * TILES + u) % 2
                        if kind == "S":
                            dve.wait_ge(s_full, slots + (slot + 1))
                            src = ps_s[s][:, 0, 0:TC] if u == 8 else ps_s[s][:, 0:NCH, 0:CH]
                            dve.tensor_reduce(top[:, b:b + 1], src, axis=AX.X if u == 8 else AX.XY,
                                              op=ALU.max).then_inc(dve_step, 1)
                            n_step += 1
                            dve.wait_ge(dve_step, chain + n_step)
                            dve.tensor_scalar(bias[:, b:b + 1], top[:, b:b + 1], -SCALE, None,
                                              ALU.mult).then_inc(bias_ready, 1)
                        if kind == "T":
                            dve.wait_ge(s_read, slots + (slot_of[u] + 1))
                            dve.reciprocal(inv[:, b:b + 1], total[:, b:b + 1]).then_inc(dve_step, 1)
                            n_step += 1
                            dve.wait_ge(dve_step, chain + n_step)
                            width = TC if u == 8 else NT
                            dve.tensor_scalar(prob[b][:, 0:width], prob[b][:, 0:width], inv[:, b:b + 1], None,
                                              ALU.mult).then_inc(p_ready, 1)
                        if kind == "Q":
                            dve.wait_ge(s_full, slots + (slot + 1))
                            dve.tensor_tensor(tok3(part[0][r, :]), ps_s[s][r, 0:NCH, 0:CH], tok3(rope[r, :]), ALU.mult)
                            dve.tensor_tensor(tok3(part[1][r, :]), ps_s[s][96:128, 0:NCH, 0:CH], tok3(rope[96:128, :]),
                                              ALU.mult).then_inc(dve_step, 1)
                            n_step += 1
                            dve.wait_ge(dve_step, chain + n_step)
                            dve.tensor_tensor(qf[r, :], part[0][r, :], part[1][r, :], ALU.add).then_inc(q_roped, 1)
                        if kind in "TX":
                            for q, tile, tiles in rounds_of(kind, u, rnd):
                                n_hi += 1
                                dve.wait_ge(t_hi, his + n_hi)
                                src = ps_t[q % 2][:, 0:tiles * P].rearrange("p (t n) -> p t n", n=P)
                                if kind == "X":
                                    hi, lo = (x[n][:, tile:tile + tiles, :] for x in (v_hi, v_lo))
                                else:
                                    hi, lo = (x[:, tile:tile + tiles, (u % 4) * P:(u % 4 + 1) * P] for x in (pt_hi, pt_lo))
                                dve.tensor_tensor(lo, src, hi, ALU.subtract).then_inc(t_free, 1)
                        if kind == "V":
                            a, width = (u * 512, 512) if u < 2 else (TL, TC)
                            dve.wait_ge(t_full, rounds + (rnd + 1))
                            if u == 0 and not first:
                                dve.wait_ge(o_stored[e], 48 * i)
                            dve.tensor_copy(out[e][64:128, a:a + width],
                                            ps_t[rnd % 2][64:128, 0:width]).then_inc(t_free, 1)
                    return n_hi, n_step

                his0, chain0 = steps_of(NEXT, 0, -1, 1, 0, 0, 0, 0, 0, True)
                his1 = sum(HIS[kind] for kind, _, _, _ in STEPS) - 2
                chain1 = sum(STEP_CHAIN[kind] for kind, _, _, _ in STEPS)

                def one(i, h, e, steps, first, last):
                    got = steps_of(steps, i, h, e, SLOTS0 + h * SLOTS, RNDS0 + h * RNDS, e * SLOTS,
                                   his0 + h * his1, chain0 + h * chain1, first)
                    assert last or got == (his1, chain1)

                heads(dve, one)

            @block.gpsimd
            def _(pool):
                def split_weights(h, e):
                    pool.wait_ge(hw_hi_ready, h + 1)
                    pool.tensor_tensor(hw_lo[e][:, :, :], hw_raw[e][:, :, :], hw_hi[e][:, :, :],
                                       ALU.subtract).then_inc(hw_lo_ready, 1)

                def split_heads(h, n):
                    pool.wait_ge(q_hi_ready, h + 1)
                    pool.tensor_tensor(q_lo[n][0:QH, :], qf[0:QH, :], q_hi[n][0:QH, :], ALU.subtract).then_inc(q_ready, 1)
                    pool.wait_ge(k_hi_ready, h + 1)
                    pool.tensor_tensor(k_lo[n][0:64, :], kvf[0:64, :], k_hi[n][0:64, :], ALU.subtract).then_inc(k_ready, 1)

                split_weights(0, 0)
                split_heads(0, 0)

                def one(i, h, e, steps, first, last):
                    if not last:
                        split_weights(h + 1, 1 - e)
                        split_heads(h + 1, 1 - e)

                heads(pool, one)


def sibling_view(t, first, n, b):
    base = t[:, 0, first:first + n]
    return bass.AP(base.tensor, base.offset, [base.ap[0], [2 * b, n // (2 * b)], [NT + b, 2], [1, b]])


def halves(t, plane, g, b):
    v = t[:, plane, g * CH:(g + 1) * CH].rearrange("p (n h b) -> p n h b", h=2, b=b)
    return v[:, :, 0, :], v[:, :, 1, :]


def block_totals(t, plane, g, b):
    n = CH // (2 * b)
    v = t[:, plane, 2 * n * g:2 * n * (g + 1)].rearrange("p (n h) -> p n h", h=2)
    return [v[:, :, h].unsqueeze(2).to_broadcast([P, n, b]) for h in range(2)]


def stage_hgrn(nc, io, cst, arena):
    with ExitStack() as ctx:
        sems = Signals(nc, ctx, "s5")
        raw = arena("hg_raw", [P, 5, NT])
        tot = [arena(f"tot{n}", [P, 2, NT >> n]) for n in range(LEVELS + 1)]
        sig = arena("hg_sig", [P, 2, NT])
        q, kd = arena("hg_q", [P, NT]), arena("hg_kd", [P, NT])
        qd, kk = arena("hg_qd", [P, 2, NT]), arena("hg_kk", [P, 2, NT])
        k_level = arena("k_level", [P, NT])
        gate = arena("hg_gate", [P, NT])
        v_tok, scores = arena("v_tok", [P, TILES, P]), arena("hg_scores", [P, TILES, P])
        k_tok = arena("k_tok", [P, 2, TILES, P])
        state = arena("hg_state", [P, 2, 8, P])
        ctx_state = arena("ctx_state", [P, 2, P])
        osq = [arena(f"osq{i}", [P, CH]) for i in range(2)]
        ostd = [arena(f"ostd{i}", [P, CH]) for i in range(2)]
        onorm = [arena(f"onorm{i}", [P, CH]) for i in range(2)]
        out = arena("hg_out", [P, NT])
        masks = arena("masks", [P, LEVELS + 1, P], I32)
        hv = arena("hg_vec", [P, 8])
        psum = ctx.enter_context(nc.psum_tensor("s5_psum", [P, 8, 512], F32))
        masks_loaded, loaded, state_loaded = sems("masks_loaded"), sems("loaded"), sems("state_loaded")
        sig_ready, vec_ready, f_ready, in_ready = sems("sig_ready"), sems("vec_ready"), sems("f_ready"), sems("in_ready")
        k_in, kl_ready = sems("k_in"), sems("k_level_ready")
        v_ps, v_ready = sems("v_transposed"), sems("v_ready")
        lv_ps, a_done = sems("level_product"), sems("scores_taken")
        q_upd, k_upd, tot_ready = sems("q_updated"), sems("k_updated"), sems("tot_ready")
        kt_ps, kt_ready, u_ps = sems("k_transposed"), sems("k_tok_ready"), sems("u_product")
        s_step, ctx_ready, ctx_stored = sems("state_step"), sems("ctx_ready"), sems("ctx_stored")
        o_ps, osq_ready, m_ps, std_ready = sems("o_product"), sems("osq_ready"), sems("mean_product"), sems("std_ready")
        o_step, idle, stored = sems("o_step"), sems("head_done"), sems("stored")
        LU, UPD = 3 * (LEVELS + 1), 3 * LEVELS
        STREAMS = (1, 2, 0, 4, 3)

        with nc.Block() as block:
            @block.sync
            def _(sp):
                sp.dma_start(masks[:, :, :], io["masks"]).then_inc(masks_loaded, 16)
                with sp.Fori(0, HH) as h:
                    sp.wait_ge(v_ps, 3 * h)
                    sp.wait_ge(in_ready, h)
                    for n, stream in enumerate(STREAMS):
                        sp.dma_start(raw[:, n, :], io["proj"][bass.ds((stream * HH + h) * P, P), :]).then_inc(loaded, 16)
                    sp.wait_ge(idle, h)
                    for d, (name, c) in enumerate((("state_hgrn_fwd", 0), ("state_hgrn_bwd", 7))):
                        sp.dma_start(state[:, d, c, :], io[name][bass.ds(h * P, P), :]).then_inc(state_loaded, 16)
                    sp.wait_ge(ctx_ready, h + 1)
                    for d, name in enumerate(("new_state_fwd", "new_state_bwd")):
                        sp.dma_start(io[name][bass.ds(h * P, P), :], ctx_state[:, d, :]).then_inc(ctx_stored, 16)
                    sp.wait_ge(idle, h + 1)
                    sp.dma_start(io["o_hg"][bass.ds(h * P, P), :], out[:, :]).then_inc(stored, 16)
                sp.wait_ge(ctx_stored, 32 * HH)
                sp.wait_ge(stored, 16 * HH)

            @block.scalar
            def _(act):
                with act.Fori(0, HH) as h:
                    act.wait_ge(loaded, 80 * h + 80)
                    act.wait_ge(idle, h)
                    act.activation(tot[0][:, :, :], raw[:, 0:2, :], ACT.Sigmoid).then_inc(sig_ready, 1)
                    act.activation(sig[:, :, :], raw[:, 2:4, :], ACT.Sigmoid).then_inc(sig_ready, 1)
                    for g in range(3):
                        act.wait_ge(v_ps, 3 * h + (g + 1))
                        act.activation(v_tok[:, 3 * g:3 * g + 3, :],
                                       psum[:, 6 + g % 2, 0:CH].rearrange("p (t n) -> p t n", t=3),
                                       ACT.Copy).then_inc(v_ready, 1)
                    act.wait_ge(f_ready, 3 * h + 2)
                    for lv in range(1, LEVELS + 1):
                        b = 1 << (lv - 1)
                        for g in range(3):
                            if lv >= 2:
                                act.wait_ge(k_upd, UPD * h + (3 * (lv - 2) + g + 1))
                            act.activation(k_level[:, g * CH:(g + 1) * CH].rearrange("p (n h b) -> p n h b", h=2, b=b),
                                           sibling_view(kk, g * CH, CH, b), ACT.Copy).then_inc(kl_ready, 1)
                    for n in range(6):
                        d, g = divmod(n, 3)
                        act.wait_ge(kt_ps, 6 * h + (n + 1))
                        act.activation(k_tok[:, d, 3 * g:3 * g + 3, :],
                                       psum[:, n, 0:CH].rearrange("p (t n) -> p t n", t=3), ACT.Copy).then_inc(kt_ready, 1)
                    for g in range(3):
                        act.wait_ge(o_ps, 3 * h + (g + 1))
                        if g == 2:
                            act.wait_ge(m_ps, 3 * h + 1)
                        act.activation(osq[g % 2][:, :], psum[:, 6 + g % 2, 0:CH], ACT.Square).then_inc(osq_ready, 1)
                        act.wait_ge(m_ps, 3 * h + (g + 1))
                        if g == 2:
                            act.wait_ge(o_step, 9 * h + 1)
                        act.activation(ostd[g % 2][:, :], psum[:, g, 0:CH], ACT.Sqrt, scale=1.0 / DK,
                                       bias=cst.eps[:, 0:1]).then_inc(std_ready, 1)

            @block.tensor
            def _(pe):
                with pe.Fori(0, HH) as h:
                    pe.wait_ge(loaded, 80 * h + 80)
                    pe.wait_ge(idle, h)
                    for g in range(3):
                        if g == 2:
                            pe.wait_ge(v_ready, 3 * h + 1)
                        for x in range(3):
                            t = 3 * g + x
                            last = pe.transpose(psum[:, 6 + g % 2, x * P:(x + 1) * P], raw[:, 4, t * P:(t + 1) * P],
                                                cst.ident[:, :])
                        last.then_inc(v_ps, 1)
                    pe.wait_ge(in_ready, h + 1)
                    pe.wait_ge(k_in, h + 1)
                    for lv in range(LEVELS + 1):
                        for g in range(3):
                            n = 3 * lv + g
                            if n >= 6:
                                pe.wait_ge(a_done, LU * h + (n - 5))
                            if lv >= 2:
                                pe.wait_ge(q_upd, UPD * h + (3 * (lv - 2) + g + 1))
                            if lv >= 1:
                                pe.wait_ge(kl_ready, UPD * h + (3 * (lv - 1) + g + 1))
                            for x in range(3):
                                t = 3 * g + x
                                dst = psum[:, n % 6, x * P:(x + 1) * P]
                                if lv == 0:
                                    last = pe.matmul(dst, kd[:, t * P:(t + 1) * P], q[:, t * P:(t + 1) * P],
                                                     start=True, stop=True)
                                else:
                                    b = 1 << (lv - 1)
                                    last = pe.matmul(dst.rearrange("p (n h b) -> p n h b", h=2, b=b),
                                                     k_level[:, t * P:(t + 1) * P], sibling_view(qd, t * P, P, b),
                                                     start=True, stop=True)
                            last.then_inc(lv_ps, 1)
                    pe.wait_ge(k_upd, UPD * h + UPD)
                    for n in range(6):
                        d, g = divmod(n, 3)
                        pe.wait_ge(a_done, LU * h + (LU - 5 + n))
                        for x in range(3):
                            t = 3 * g + x
                            last = pe.transpose(psum[:, n, x * P:(x + 1) * P], kk[:, d, t * P:(t + 1) * P], cst.ident[:, :])
                        last.then_inc(kt_ps, 1)
                    pe.wait_ge(v_ready, 3 * h + 3)
                    for n in range(6):
                        d, g = divmod(n, 3)
                        pe.wait_ge(kt_ready, 6 * h + (n + 1))
                        for x in range(3):
                            t = 3 * g + x
                            last = pe.matmul(psum[:, n, x * P:(x + 1) * P], k_tok[:, d, t, :], v_tok[:, t, :],
                                             start=True, stop=True)
                        last.then_inc(u_ps, 1)
                    pe.wait_ge(a_done, LU * h + LU)
                    pe.wait_ge(q_upd, UPD * h + UPD)
                    pe.wait_ge(s_step, 14 * h + 14)
                    pe.wait_ge(ctx_ready, h + 1)
                    for g in range(3):
                        if g == 2:
                            pe.wait_ge(o_step, 9 * h + 2)
                        for x in range(3):
                            t = 3 * g + x
                            dst = psum[:, 6 + g % 2, x * P:(x + 1) * P]
                            last = pe.matmul(dst, v_tok[:, t, :], scores[:, t, :], start=True, stop=(t == 8))
                            if t < 8:
                                pe.matmul(dst, state[:, 0, t, :], qd[:, 1, t * P:(t + 1) * P], start=False, stop=False)
                                last = pe.matmul(dst, state[:, 1, t, :], qd[:, 0, t * P:(t + 1) * P], start=False, stop=True)
                        last.then_inc(o_ps, 1)
                        pe.wait_ge(osq_ready, 3 * h + (g + 1))
                        pe.matmul(psum[:, g, 0:CH], cst.ones[:, :], osq[g % 2][:, :], start=True, stop=True).then_inc(m_ps, 1)

            @block.gpsimd
            def _(pool):
                with pool.Fori(0, HH) as h:
                    pool.wait_ge(f_ready, 3 * h + 2)
                    pool.tensor_tensor(kd[:, :], kk[:, 0, :], kk[:, 1, :], ALU.add).then_inc(k_in, 1)
                    pool.wait_ge(in_ready, h + 1)
                    for lv in range(1, LEVELS + 1):
                        b = 1 << (lv - 1)
                        if lv >= 2:
                            pool.wait_ge(tot_ready, LEVELS * h + (lv - 1))
                        v = tot[lv - 1][:, :, :].rearrange("p d (n h) -> p d n h", h=2)
                        pool.tensor_tensor(tot[lv][:, :, :], v[:, :, :, 0], v[:, :, :, 1], ALU.mult).then_inc(tot_ready, 1)
                        for g in range(3):
                            pool.wait_ge(lv_ps, LU * h + (3 * lv + g + 1))
                            if lv >= 2:
                                pool.wait_ge(k_upd, UPD * h + (3 * (lv - 2) + g + 1))
                            lower, _ = halves(kk, 0, g, b)
                            _, of_upper = block_totals(tot[lv - 1], 0, g, b)
                            pool.tensor_tensor(lower, lower, of_upper, ALU.mult)
                            _, upper = halves(kk, 1, g, b)
                            of_lower, _ = block_totals(tot[lv - 1], 1, g, b)
                            pool.tensor_tensor(upper, upper, of_lower, ALU.mult).then_inc(k_upd, 1)

            @block.vector
            def _(dve):
                dve.wait_ge(masks_loaded, 16)
                with dve.Fori(0, HH) as h:
                    dve.wait_ge(idle, h)
                    dve.tensor_copy(hv[:, 0:2], cst.lb[:, :].rearrange("p (d h) -> p h d", d=2)[:, bass.ds(h, 1), :])
                    dve.tensor_copy(hv[:, 2:4], cst.lb1[:, :].rearrange("p (d h) -> p h d", d=2)[:, bass.ds(h, 1), :])
                    dve.tensor_copy(hv[:, 4:5], cst.cols_a[:, bass.ds(h + AT_A["g_hg"], 1)]).then_inc(vec_ready, 1)
                    dve.wait_ge(vec_ready, h + 1)
                    dve.wait_ge(sig_ready, 2 * h + 1)
                    for d in range(2):
                        last = dve.tensor_scalar(tot[0][:, d, :], tot[0][:, d, :], hv[:, 2 + d:3 + d], hv[:, d:d + 1],
                                                 ALU.mult, ALU.add)
                    last.then_inc(f_ready, 1)
                    dve.wait_ge(f_ready, 3 * h + 1)
                    dve.tensor_scalar(kk[:, :, :], tot[0][:, :, :], -1.0, 1.0, ALU.mult, ALU.add).then_inc(f_ready, 1)
                    dve.wait_ge(sig_ready, 2 * h + 2)
                    dve.tensor_tensor(gate[:, :], sig[:, 1, :], raw[:, 3, :], ALU.mult)
                    dve.tensor_tensor(q[:, :], sig[:, 0, :], raw[:, 2, :], ALU.mult).then_inc(f_ready, 1)
                    dve.wait_ge(f_ready, 3 * h + 3)
                    dve.tensor_tensor(qd[:, 0, :], q[:, :], tot[0][:, 1, :], ALU.mult)
                    dve.tensor_tensor(qd[:, 1, :], q[:, :], tot[0][:, 0, :], ALU.mult).then_inc(in_ready, 1)
                    dve.wait_ge(in_ready, h + 1)
                    for lv in range(LEVELS + 1):
                        b = 1 << max(lv - 1, 0)
                        if lv >= 2:
                            dve.wait_ge(tot_ready, LEVELS * h + (lv - 1))
                        for g in range(3):
                            n = 3 * lv + g
                            dve.wait_ge(lv_ps, LU * h + (n + 1))
                            taken = psum[:, n % 6, 0:CH].rearrange("p (t n) -> p t n", t=3)
                            if lv == 0:
                                dve.tensor_copy(scores[:, 3 * g:3 * g + 3, :], taken).then_inc(a_done, 1)
                                continue
                            if lv >= 2:
                                dve.wait_ge(q_upd, UPD * h + (3 * (lv - 2) + g + 1))
                            dve.wait_ge(a_done, LU * h + (n - 2))
                            lower, _ = halves(qd, 0, g, b)
                            _, of_upper = block_totals(tot[lv - 1], 1, g, b)
                            dve.tensor_tensor(lower, lower, of_upper, ALU.mult)
                            _, upper = halves(qd, 1, g, b)
                            of_lower, _ = block_totals(tot[lv - 1], 0, g, b)
                            dve.tensor_tensor(upper, upper, of_lower, ALU.mult).then_inc(q_upd, 1)
                            dve.copy_predicated(scores[:, 3 * g:3 * g + 3, :],
                                                masks[:, lv:lv + 1, :].to_broadcast([P, 3, P]), taken).then_inc(a_done, 1)
                    dve.wait_ge(state_loaded, 32 * h + 32)
                    dve.wait_ge(tot_ready, LEVELS * h + LEVELS)
                    dve.wait_ge(u_ps, 6 * h + 6)
                    for n in range(14):
                        c, d = divmod(n, 2)
                        src, dst = (c, c + 1) if d == 0 else (7 - c, 6 - c)
                        if n >= 2:
                            dve.wait_ge(s_step, 14 * h + (n - 1))
                        dve.scalar_tensor_tensor(state[:, d, dst, :], state[:, d, src, :], tot[LEVELS][:, d, src:src + 1],
                                                 psum[:, 3 * d + src // 3, (src % 3) * P:(src % 3 + 1) * P],
                                                 ALU.mult, ALU.add).then_inc(s_step, 1)
                    dve.wait_ge(ctx_stored, 32 * h)
                    dve.tensor_copy(ctx_state[:, 0, :], psum[:, 2, 2 * P:3 * P])
                    dve.tensor_copy(ctx_state[:, 1, :], psum[:, 5, 2 * P:3 * P]).then_inc(ctx_ready, 1)
                    dve.wait_ge(stored, 16 * h)
                    for g in range(3):
                        dve.wait_ge(std_ready, 3 * h + (g + 1))
                        dve.reciprocal(ostd[g % 2][:, :], ostd[g % 2][:, :]).then_inc(o_step, 1)
                        dve.wait_ge(o_step, 9 * h + (3 * g + 1))
                        dve.tensor_tensor(onorm[g % 2][:, :], psum[:, 6 + g % 2, 0:CH], ostd[g % 2][:, :],
                                          ALU.mult).then_inc(o_step, 1)
                        dve.wait_ge(o_step, 9 * h + (3 * g + 2))
                        dve.scalar_tensor_tensor(out[:, g * CH:(g + 1) * CH], onorm[g % 2][:, :], hv[:, 4:5],
                                                 gate[:, g * CH:(g + 1) * CH], ALU.mult, ALU.mult).then_inc(o_step, 1)
                    dve.wait_ge(o_step, 9 * h + 9)
                    dve.tensor_copy(hv[:, 5:6], hv[:, 4:5]).then_inc(idle, 1)


def stage_merge(nc, io, cst, arena, m_hi, m_lo):
    with ExitStack() as ctx:
        sems = Signals(nc, ctx, "s6")
        o_hi, o_lo = arena("o_hi", [P, KD, NT], F32R), arena("o_lo", [P, KD, NT], F32R)
        w = WeightStream(nc, arena, sems, "s6")
        gates = [arena(f"merge_gates{i}", [P, 2, NT]) for i in range(2)]
        y = [arena(f"merge_y{i}", [P, NT]) for i in range(2)]
        psum = [ctx.enter_context(nc.psum_tensor(f"s6_psum{i}", [P, 4, 512], F32)) for i in range(2)]
        o_loaded = [sems(f"o_loaded{i}") for i in range(2)]
        g_loaded = [sems(f"g_loaded{i}") for i in range(2)]
        o_hi_ready, o_lo_ready = sems("o_hi_ready"), sems("o_lo_ready")
        g_ready, a_read, b_read = sems("gates_ready"), sems("a_read"), sems("b_read")
        y_ready, hi_ready, lo_ready = sems("y_ready"), sems("hi_ready"), sems("lo_ready")
        half_ps = sems("mla_product")
        mla = io["w_mla_o"].rearrange("(k p) n -> p k n", p=P)
        hg = io["w_hg_o"].rearrange("(k p) n -> p k n", p=P)

        with nc.Block() as block:
            @block.sync
            def _(sp):
                def load(c, s, free):
                    w.load(sp, c, s, [(w.raw[s][:, 0:4, :], mla[:, :, bass.ds(c * P, P)]),
                                      (w.raw[s][:, 4:8, :], hg[:, :, bass.ds(c * P, P)])], free)
                    if free:
                        sp.wait_ge(b_read, c - 1)
                    for n, chunk in enumerate((20, 28)):
                        sp.dma_start(gates[s][:, n, :], io["proj"][bass.ds((c + chunk) * P, P), :]).then_inc(g_loaded[s], 16)

                for k in range(2):
                    sp.dma_start(y[k][:, :], io["o_mla"][k * P:(k + 1) * P, :]).then_inc(o_loaded[k], 16)
                load(0, 0, False)
                for k in range(2, KD):
                    sp.wait_ge(o_lo_ready, k - 1)
                    src = io["o_mla"][k * P:(k + 1) * P, :] if k < 4 else io["o_hg"][(k - 4) * P:(k - 3) * P, :]
                    sp.dma_start(y[k % 2][:, :], src).then_inc(o_loaded[k % 2], 16)
                load(1, 1, False)
                with sp.Fori(1, KD // 2) as i:
                    for s in range(2):
                        load(2 * i + s, s, True)

            @block.scalar
            def _(act):
                def chunk(c, s, uses, free):
                    w.split_hi(act, s, 32 * uses, c, free)
                    act.wait_ge(g_loaded[s], 32 * uses)
                    act.activation(gates[s][:, :, :], gates[s][:, :, :], ACT.Sigmoid).then_inc(g_ready, 1)

                def split(c):
                    act.wait_ge(y_ready, c + 1)
                    act.activation(m_hi[:, bass.ds(c, 1), :].rearrange("p a n -> p (a n)"), y[1][:, :], ACT.Copy).then_inc(hi_ready, 1)

                w.split_hi(act, 0, 32, 0, False)
                for k in range(KD):
                    act.wait_ge(o_loaded[k % 2], 16 * (k // 2 + 1))
                    act.activation(o_hi[:, k, :], y[k % 2][:, :], ACT.Copy).then_inc(o_hi_ready, 1)
                act.wait_ge(g_loaded[0], 32)
                act.activation(gates[0][:, :, :], gates[0][:, :, :], ACT.Sigmoid).then_inc(g_ready, 1)
                chunk(1, 1, 1, False)
                with act.Fori(1, KD // 2) as i:
                    for s in range(2):
                        split(2 * i + (s - 2))
                        chunk(2 * i + s, s, i + 1, True)
                split(KD - 2)
                split(KD - 1)

            @block.gpsimd
            def _(pool):
                def split(c):
                    pool.wait_ge(hi_ready, c + 1)
                    pool.tensor_tensor(m_lo[:, bass.ds(c, 1), :].rearrange("p a n -> p (a n)"), y[1][:, :],
                                       m_hi[:, bass.ds(c, 1), :].rearrange("p a n -> p (a n)"), ALU.subtract).then_inc(lo_ready, 1)

                w.split_lo(pool, 0, 0)
                w.split_lo(pool, 1, 1)
                with pool.Fori(1, KD // 2) as i:
                    for s in range(2):
                        split(2 * i + (s - 2))
                        w.split_lo(pool, s, 2 * i + s)
                split(KD - 2)
                split(KD - 1)

            @block.tensor
            def _(pe):
                with pe.Fori(0, KD // 2) as i:
                    for s in range(2):
                        c = 2 * i + s
                        pe.wait_ge(w.lo_ready, c + 1)
                        parts = [lambda k: w.hi[s][:, k, :], lambda k: w.lo[s][:, k, :],
                                 lambda k: o_hi[:, k, :], lambda k: o_lo[:, k, :]]
                        pe.wait_ge(o_lo_ready, 4)
                        pe.wait_ge(a_read, c)
                        gemm_chunk(pe, psum[0], *parts, [(k, k) for k in range(4)]).then_inc(half_ps, 1)
                        pe.wait_ge(o_lo_ready, KD)
                        pe.wait_ge(b_read, c)
                        gemm_chunk(pe, psum[1], *parts, [(k, k) for k in range(4, KD)]).then_inc(w.used, 1)

            @block.vector
            def _(dve):
                for k in range(KD):
                    dve.wait_ge(o_hi_ready, k + 1)
                    dve.tensor_tensor(o_lo[:, k, :], y[k % 2][:, :], o_hi[:, k, :], ALU.subtract).then_inc(o_lo_ready, 1)
                dve.wait_ge(o_lo_ready, KD)
                with dve.Fori(0, KD // 2) as i:
                    for s in range(2):
                        c = 2 * i + s
                        dve.wait_ge(half_ps, c + 1)
                        dve.wait_ge(g_ready, c + 1)
                        dve.tensor_tensor(tok3(y[0][:, :]), psum[0][:, 0:NCH, 0:CH], tok3(gates[s][:, 0, :]), ALU.mult).then_inc(a_read, 1)
                        dve.wait_ge(w.used, c + 1)
                        dve.wait_ge(lo_ready, c)
                        dve.tensor_tensor(tok3(y[1][:, :]), psum[1][:, 0:NCH, 0:CH], tok3(gates[s][:, 1, :]), ALU.mult).then_inc(b_read, 1)
                        dve.wait_ge(b_read, c + 1)
                        dve.wait_ge(a_read, c + 1)
                        dve.tensor_tensor(y[1][:, :], y[1][:, :], y[0][:, :], ALU.add).then_inc(y_ready, 1)
                        dve.wait_ge(y_ready, c + 1)


def add_scaled(dve, x, psum, gate):
    v = tok3(x)
    dve.scalar_tensor_tensor(v[:, 0:2, :], psum[:, 0:2, 0:CH], gate[:, 0:1], v[:, 0:2, :], ALU.mult, ALU.add)
    cut = TL - 2 * CH
    dve.scalar_tensor_tensor(v[:, 2, 0:cut], psum[:, 2, 0:cut], gate[:, 0:1], v[:, 2, 0:cut], ALU.mult, ALU.add)
    return dve.scalar_tensor_tensor(v[:, 2, cut:CH], psum[:, 2, cut:CH], gate[:, 1:2], v[:, 2, cut:CH], ALU.mult, ALU.add)


def stage_out_projection(nc, io, cst, arena, m_hi, m_lo, x_t):
    with ExitStack() as ctx:
        sems = Signals(nc, ctx, "s7")
        w = WeightStream(nc, arena, sems, "s7")
        col = arena("gt1_cols", [P, 4])
        psum = [ctx.enter_context(nc.psum_tensor(f"s7_psum{i}", [P, 4, 512], F32)) for i in range(2)]
        x_loaded, added, col_ready = sems("x_loaded"), sems("added"), sems("col_ready")
        wo = io["w_out"].rearrange("(k p) n -> p k n", p=P)
        with nc.Block() as block:
            @block.sync
            def _(sp):
                for s in range(2):
                    w.load(sp, s, s, [(w.raw[s][:, :, :], wo[:, :, s * P:(s + 1) * P])], False)
                sp.dma_start(x_t[:, :, :], io["x_t"].rearrange("(k p) n -> p k n", p=P)).then_inc(x_loaded, 16)
                with sp.Fori(1, KD // 2) as i:
                    for s in range(2):
                        c = 2 * i + s
                        w.load(sp, c, s, [(w.raw[s][:, :, :], wo[:, :, bass.ds(c * P, P)])])

            @block.scalar
            def _(act):
                for s in range(2):
                    w.split_hi(act, s, 16, s, False)
                with act.Fori(1, KD // 2) as i:
                    for s in range(2):
                        w.split_hi(act, s, 16 * i + 16, 2 * i + s)

            @block.gpsimd
            def _(pool):
                with pool.Fori(0, KD // 2) as i:
                    for s in range(2):
                        w.split_lo(pool, s, 2 * i + s)

            @block.tensor
            def _(pe):
                def chunk(c, s, free):
                    pe.wait_ge(w.lo_ready, c + 1)
                    if free:
                        pe.wait_ge(added, c - 1)
                    gemm_chunk(pe, psum[s], lambda k: w.hi[s][:, k, :], lambda k: w.lo[s][:, k, :],
                               lambda k: m_hi[:, k, :], lambda k: m_lo[:, k, :],
                               [(k, k) for k in range(KD)]).then_inc(w.used, 1)
                for s in range(2):
                    chunk(s, s, False)
                with pe.Fori(1, KD // 2) as i:
                    for s in range(2):
                        chunk(2 * i + s, s, True)

            @block.vector
            def _(dve):
                dve.wait_ge(x_loaded, 16)
                with dve.Fori(0, KD // 2) as i:
                    for s in range(2):
                        c = 2 * i + s
                        dve.wait_ge(added, c)
                        dve.tensor_copy(col[:, 0:2], cst.mod[:, bass.ds(c + 2 * KD, 1), :].rearrange("p a g -> p (a g)")).then_inc(col_ready, 1)
                        dve.wait_ge(col_ready, c + 1)
                        dve.wait_ge(w.used, c + 1)
                        add_scaled(dve, x_t[:, bass.ds(c, 1), :].rearrange("p a n -> p (a n)"), psum[s], col).then_inc(added, 1)


def stage_second_norm(nc, io, cst, arena, x_t, h_hi, h_lo):
    with ExitStack() as ctx:
        sems = Signals(nc, ctx, "s8")
        norm = Norm(arena, sems, "n2", cst, KD, D)
        app = Apply(arena, sems, "a2", norm)
        psum = ctx.enter_context(nc.psum_tensor("s8_psum", [P, 4, 512], F32))
        with nc.Block() as block:
            @block.scalar
            def _(act):
                for k in range(KD):
                    norm.act_square(act, k, x_t[:, k, :])
                norm.act_std(act, psum[:, 0, :])
                norm.act_broadcast(act, psum)
                for k in range(KD):
                    app.act(act, k, [(h_hi[:, k, :], 0, NT)])

            @block.gpsimd
            def _(pool):
                for k in range(KD):
                    app.pool(pool, k, [(h_lo[:, k, :], h_hi[:, k, :], 0, NT)])

            @block.tensor
            def _(pe):
                norm.pe_sums(pe, psum[:, 0, :])
                norm.pe_broadcast(pe, psum)

            @block.vector
            def _(dve):
                for k in range(KD):
                    norm.dve_add(dve, k)
                norm.dve_rstd(dve)
                for k in range(KD):
                    app.dve(dve, k, x_t[:, k, :], [(a, b, cst.gain_ffn[:, k, g:g + 1], cst.mod[:, 3 * KD + k, g:g + 1])
                                                   for g, (a, b) in enumerate(GROUPS)])


PAIRS = DFF // P // 2
PAD = NT + 4
LAT0, CTX0 = 1, TL + 3


def stage_ffn(nc, io, cst, arena, h_hi, h_lo, x_t):
    with ExitStack() as ctx:
        sems = Signals(nc, ctx, "s9")
        w = WeightStream(nc, arena, sems, "s9")
        gpad = [arena(f"gate_pad{i}", [P, PAD]) for i in range(2)]
        conv = [arena(f"conv{i}", [P, PAD]) for i in range(2)]
        u = arena("u_f32", [P, NT])
        u_hi, u_lo = arena("u_hi", [P, 2, NT], F32R), arena("u_lo", [P, 2, NT], F32R)
        taps = arena("taps", [P, 2, 4])
        psum = [ctx.enter_context(nc.psum_tensor(f"s9_psum{i}", [P, 4, 512], F32)) for i in range(2)]
        padded, taps_ready = sems("padded"), sems("taps_ready")
        y_ps = sems("out_product")
        g_read, v_read, y_read = sems("gate_read"), sems("value_read"), sems("out_added")
        conv_step, gelu_ready = sems("conv_step"), sems("gelu_ready")
        u_hi_ready, u_lo_ready = sems("u_hi_ready"), sems("u_lo_ready")
        win = io["w_ffn_in"].rearrange("(k p) n -> p k n", p=P)
        wout = io["w_ffn_out"].rearrange("(k p) n -> p k n", p=P)
        cut = TL - 2 * CH

        def out_view(t, m):
            return t[:, :, :].rearrange("p k n -> p (k n)").rearrange("p (k n) -> p k n", k=2)[:, :, (m % 4) * P:(m % 4 + 1) * P]

        def pieces(padded_t, bank):
            return [(padded_t[:, LAT0:LAT0 + 2 * CH].rearrange("p (j c) -> p j c", j=2), bank[:, 0:2, 0:CH]),
                    (padded_t[:, LAT0 + 2 * CH:LAT0 + TL], bank[:, 2, 0:cut]),
                    (padded_t[:, CTX0:CTX0 + TC], bank[:, 2, cut:CH])]

        def all_chunks(engine, one):
            for n, (kind, x) in enumerate((("g", 0), ("g", 1), ("v", 0), ("v", 1))):
                one(n, n % 2, kind, x, 0)
            with engine.Fori(1, PAIRS) as g:
                for n, (kind, x) in enumerate((("g", 0), ("o", 0), ("o", 1), ("g", 1), ("v", 0), ("v", 1))):
                    one(6 * g + (n - 2), n % 2, kind, x, g)
            for n, x in enumerate((0, 1)):
                one(6 * PAIRS - 2 + n, n % 2, "o", x, PAIRS)

        with nc.Block() as block:
            @block.sync
            def _(sp):
                def one(c, s, kind, x, g):
                    raw = w.raw[s]
                    free = not (isinstance(c, int) and c < 2)
                    if kind == "o":
                        dst = raw[:, :, :].rearrange("p k n -> p (k n)").rearrange("p (k n) -> p k n", k=2)
                        rows = wout[:, bass.ds(2 * (g - 1), 2), x * 512:(x + 1) * 512]
                        w.load(sp, c, s, [(dst, rows)], free)
                    else:
                        at = (0 if kind == "g" else DFF) + x * P
                        w.load(sp, c, s, [(raw[:, :, :], win[:, :, bass.ds(2 * P * g + at, P)])], free)
                all_chunks(sp, one)

            @block.scalar
            def _(act):
                act.wait_ge(padded, 1)

                def weights(c, s):
                    free = not (isinstance(c, int) and c < 2)
                    w.split_hi(act, s, 8 * (c - s) + 16, c, free)

                def gate(g, x, used):
                    act.wait_ge(w.used, used)
                    bank = psum[0] if x == 0 else psum[1]
                    for dst, src in pieces(gpad[x], bank):
                        last = act.activation(dst, src, ACT.Copy)
                    last.then_inc(g_read, 1)

                def gelu(g, x):
                    act.wait_ge(conv_step, 6 * g + 3 * x + 3)
                    act.activation(conv[x][:, 1:PAD - 1], conv[x][:, 1:PAD - 1], ACT.Gelu_apprx_tanh).then_inc(gelu_ready, 1)

                def split(g, x):
                    act.wait_ge(v_read, 2 * g + (x + 1))
                    act.activation(u_hi[:, x, :], u[:, :], ACT.Copy).then_inc(u_hi_ready, 1)

                weights(0, 0)
                weights(1, 1)
                gate(0, 0, 1)
                weights(2, 0)
                gelu(0, 0)
                gate(0, 1, 2)
                weights(3, 1)
                gelu(0, 1)
                with act.Fori(1, PAIRS) as g:
                    c = 6 * g - 2
                    weights(c, 0)
                    split(g - 1, 0)
                    weights(c + 1, 1)
                    split(g - 1, 1)
                    gate(g, 0, c + 1)
                    weights(c + 2, 0)
                    gelu(g, 0)
                    weights(c + 3, 1)
                    weights(c + 4, 0)
                    gate(g, 1, c + 4)
                    weights(c + 5, 1)
                    gelu(g, 1)
                c = 6 * PAIRS - 2
                weights(c, 0)
                split(PAIRS - 1, 0)
                weights(c + 1, 1)
                split(PAIRS - 1, 1)

            @block.gpsimd
            def _(pool):
                def split(g, x):
                    pool.wait_ge(u_hi_ready, 2 * g + (x + 1))
                    pool.tensor_tensor(u_lo[:, x, :], u[:, :], u_hi[:, x, :], ALU.subtract).then_inc(u_lo_ready, 1)

                for x in range(2):
                    pool.memset(gpad[x][:, :], 0.0)
                pool.memset(conv[0][:, 0:1], 0.0).then_inc(padded, 1)
                w.split_lo(pool, 0, 0)
                w.split_lo(pool, 1, 1)
                w.split_lo(pool, 0, 2)
                w.split_lo(pool, 1, 3)
                with pool.Fori(1, PAIRS) as g:
                    c = 6 * g - 2
                    w.split_lo(pool, 0, c)
                    split(g - 1, 0)
                    w.split_lo(pool, 1, c + 1)
                    split(g - 1, 1)
                    for n in range(2, 6):
                        w.split_lo(pool, n % 2, c + n)
                c = 6 * PAIRS - 2
                w.split_lo(pool, 0, c)
                split(PAIRS - 1, 0)
                w.split_lo(pool, 1, c + 1)
                split(PAIRS - 1, 1)

            @block.tensor
            def _(pe):
                def h_product(c, s, bank):
                    pe.wait_ge(w.lo_ready, c + 1)
                    return gemm_chunk(pe, bank, lambda k: w.hi[s][:, k, :], lambda k: w.lo[s][:, k, :],
                                      lambda k: h_hi[:, k, :], lambda k: h_lo[:, k, :], [(k, k) for k in range(KD)])

                def h_tile(c, s, bank):
                    h_product(c, s, bank).then_inc(w.used, 1)

                def outs(c, s, x, g, last):
                    pe.wait_ge(w.lo_ready, c + 1)
                    pe.wait_ge(u_lo_ready, 2 * g)
                    for m in range(4 * x, 4 * x + 4):
                        if m == 0 or (m == 1 and last):
                            pe.wait_ge(v_read, 2 * g)
                        elif m == 1:
                            pe.wait_ge(g_read, 2 * g + 1)
                        else:
                            pe.wait_ge(y_read, 8 * (g - 1) + (m - 1))
                        mm = gemm_chunk(pe, psum[(m + 1) % 2], lambda k: out_view(w.hi[s], m)[:, k, :],
                                        lambda k: out_view(w.lo[s], m)[:, k, :],
                                        lambda k: u_hi[:, k, :], lambda k: u_lo[:, k, :], [(0, 0), (1, 1)])
                        mm.then_inc(w.used if m % 4 == 3 else y_ps, 1)

                h_tile(0, 0, psum[0])
                h_tile(1, 1, psum[1])
                pe.wait_ge(g_read, 1)
                h_tile(2, 0, psum[0])
                pe.wait_ge(g_read, 2)
                h_tile(3, 1, psum[1])
                with pe.Fori(1, PAIRS) as g:
                    c = 6 * g - 2
                    pe.wait_ge(v_read, 2 * g - 1)
                    h_tile(c, 0, psum[0])
                    outs(c + 1, 1, 0, g, False)
                    outs(c + 2, 0, 1, g, False)
                    pe.wait_ge(y_read, 8 * g - 1)
                    h_tile(c + 3, 1, psum[1])
                    pe.wait_ge(y_read, 8 * g)
                    h_tile(c + 4, 0, psum[0])
                    pe.wait_ge(g_read, 2 * g + 2)
                    h_tile(c + 5, 1, psum[1])
                c = 6 * PAIRS - 2
                outs(c, 0, 0, PAIRS, True)
                outs(c + 1, 1, 1, PAIRS, True)

            @block.vector
            def _(dve):
                def conv_gate(g, x):
                    n = 2 * g + x
                    dve.tensor_copy(taps[:, x, 0:3],
                                    cst.cols_b[:, AT_B["conv_w"]:AT_B["conv_w"] + 66].rearrange("p (j m) -> p j m", j=3)
                                    [:, :, bass.ds(n, 1)].rearrange("p j a -> p (j a)"))
                    dve.tensor_copy(taps[:, x, 3:4], cst.cols_a[:, bass.ds(n + AT_A["conv_b"], 1)]).then_inc(taps_ready, 1)
                    dve.wait_ge(taps_ready, n + 1)
                    dve.wait_ge(g_read, n + 1)
                    out = conv[x][:, 1:PAD - 1]
                    dve.tensor_scalar(out, gpad[x][:, 1:PAD - 1], taps[:, x, 1:2], taps[:, x, 3:4],
                                      ALU.mult, ALU.add).then_inc(conv_step, 1)
                    for j, first in ((0, 0), (2, 2)):
                        dve.wait_ge(conv_step, 3 * n + (1 + j // 2))
                        dve.scalar_tensor_tensor(out, gpad[x][:, first:first + PAD - 2], taps[:, x, j:j + 1], out,
                                                 ALU.mult, ALU.add).then_inc(conv_step, 1)

                def value(g, x, used):
                    dve.wait_ge(w.used, used)
                    dve.wait_ge(gelu_ready, 2 * g + (x + 1))
                    dve.wait_ge(u_lo_ready, 2 * g + x)
                    flat = tok3(u[:, :])
                    outs = [flat[:, 0:2, :], flat[:, 2, 0:cut], flat[:, 2, cut:CH]]
                    for dst, (a, b) in zip(outs, pieces(conv[x], psum[x])):
                        last = dve.tensor_tensor(dst, b, a, ALU.mult)
                    last.then_inc(v_read, 1)
                    dve.wait_ge(v_read, 2 * g + (x + 1))

                def adds(g, chunk0, chunk1):
                    for m in range(KD):
                        if m % 4 == 3:
                            dve.wait_ge(w.used, (chunk0 if m == 3 else chunk1) + 1)
                        else:
                            dve.wait_ge(y_ps, 6 * (g - 1) + (3 * (m // 4) + m % 4 + 1))
                        dve.wait_ge(y_read, 8 * (g - 1) + m)
                        add_scaled(dve, x_t[:, m, :], psum[(m + 1) % 2], cst.mod[:, 5 * KD + m, :]).then_inc(y_read, 1)

                conv_gate(0, 0)
                conv_gate(0, 1)
                value(0, 0, 3)
                value(0, 1, 4)
                with dve.Fori(1, PAIRS) as g:
                    c = 6 * g - 2
                    conv_gate(g, 0)
                    adds(g, c + 1, c + 2)
                    conv_gate(g, 1)
                    value(g, 0, c + 5)
                    value(g, 1, c + 6)
                c = 6 * PAIRS - 2
                adds(PAIRS, c, c + 1)


def stage_final(nc, io, cst, arena, x_t):
    with ExitStack() as ctx:
        sems = Signals(nc, ctx, "s10")
        norm = Norm(arena, sems, "n3", cst, KD, D)
        y = arena("final_y", [P, KD, NT])
        rows = [arena(f"final_rows{i}", [P, D]) for i in range(2)]
        psum = ctx.enter_context(nc.psum_tensor("s10_psum", [P, 8, 512], F32))
        y_ready, y_t, row_ready = sems("y_ready"), sems("y_transposed"), sems("row_ready")
        stored = [sems(f"stored{i}") for i in range(2)]
        with nc.Block() as block:
            @block.sync
            def _(sp):
                for t in range(TILES):
                    dst = io["y_prompt"] if t == TILES - 1 else io["y_sample"][t * P:(t + 1) * P, :]
                    sp.wait_ge(row_ready, 2 * t + 2)
                    sp.dma_start(dst, rows[t % 2][:, :]).then_inc(stored[t % 2], 16)
                sp.wait_ge(stored[0], 16 * 5)
                sp.wait_ge(stored[1], 16 * 4)

            @block.scalar
            def _(act):
                for k in range(KD):
                    norm.act_square(act, k, x_t[:, k, :])
                norm.act_std(act, psum[:, 0, :])
                norm.act_broadcast(act, psum)

            @block.tensor
            def _(pe):
                norm.pe_sums(pe, psum[:, 0, :])
                norm.pe_broadcast(pe, psum)
                pe.wait_ge(y_ready, KD)
                for r in range(2 * TILES):
                    t, half = r // 2, r % 2
                    if r >= 2:
                        pe.wait_ge(row_ready, r - 1)
                    for k in range(4):
                        last = pe.transpose(psum[:, 4 + r % 2, k * P:(k + 1) * P],
                                            y[:, 4 * half + k, t * P:(t + 1) * P], cst.ident[:, :])
                    last.then_inc(y_t, 1)

            @block.vector
            def _(dve):
                for k in range(KD):
                    norm.dve_add(dve, k)
                norm.dve_rstd(dve)
                dve.wait_ge(norm.rb_ready, 1)
                for k in range(KD):
                    dve.scalar_tensor_tensor(y[:, k, :], x_t[:, k, :], cst.a("g_final", k), norm.rb[:, :],
                                             ALU.mult, ALU.mult).then_inc(y_ready, 1)
                for r in range(2 * TILES):
                    t, half = r // 2, r % 2
                    dve.wait_ge(y_t, r + 1)
                    if t >= 2:
                        dve.wait_ge(stored[t % 2], 16 * (t // 2))
                    dve.tensor_copy(rows[t % 2][:, 4 * half * P:4 * (half + 1) * P], psum[:, 4 + r % 2, :]).then_inc(row_ready, 1)


LOW = 16512


def program(nc, io):
    persistent = Arena(nc, LOW)
    cst = Constants(persistent)
    base = persistent.at
    arena = Arena(nc, base)
    h_hi, h_lo = arena("h_hi", [P, KD, NT], F32R), arena("h_lo", [P, KD, NT], F32R)
    stage_setup(nc, io, cst, Arena(nc, arena.at), h_hi, h_lo)
    pqkv, pkr = arena("pqkv", [P, 5, NT]), arena("pkr", [P, NT])
    after_pkr = arena.at
    stage_in_projection(nc, io, cst, arena, h_hi, h_lo, pqkv, pkr)
    low = Arena(nc, base)
    qn_hi, qn_lo = low("qn_hi", [P, 3, NT], F32R), low("qn_lo", [P, 3, NT], F32R)
    c_hi, c_lo = low("ckv_hi", [P, 2, NK], F32R), low("ckv_lo", [P, 2, NK], F32R)
    k_hi = [low(f"k_hi{e}", [P, NK], F32R) for e in range(2)]
    k_lo = [low(f"k_lo{e}", [P, NK], F32R) for e in range(2)]
    rope = low("rope", [P, NT])
    assert low.at <= base + 2 * KD * NT * 4
    stage_low_rank(nc, io, cst, Arena(nc, after_pkr), pqkv, pkr, rope, qn_hi, qn_lo, c_hi, c_lo, k_hi, k_lo)
    stage_attention(nc, io, cst, low, rope, qn_hi, qn_lo, c_hi, c_lo, k_hi, k_lo)
    stage_hgrn(nc, io, cst, Arena(nc, base))
    half = 2 * KD * NT * 4
    mix = Arena(nc, base)
    m_hi, m_lo = mix("m_hi", [P, KD, NT], F32R), mix("m_lo", [P, KD, NT], F32R)
    stage_merge(nc, io, cst, Arena(nc, base + half), m_hi, m_lo)
    rest = Arena(nc, base + half)
    x_t = rest("x_res", [P, KD, NT])
    after_x = rest.at
    stage_out_projection(nc, io, cst, Arena(nc, after_x), m_hi, m_lo, x_t)
    again = Arena(nc, base)
    h2_hi, h2_lo = again("h2_hi", [P, KD, NT], F32R), again("h2_lo", [P, KD, NT], F32R)
    stage_second_norm(nc, io, cst, Arena(nc, after_x), x_t, h2_hi, h2_lo)
    stage_ffn(nc, io, cst, Arena(nc, after_x), h2_hi, h2_lo, x_t)
    stage_final(nc, io, cst, Arena(nc, after_x), x_t)


def constants():
    ident = np.eye(P, dtype=np.float32)
    s, t = np.meshgrid(np.arange(P), np.arange(P), indexing="ij")
    masks = [s == t]
    for level in range(LEVELS):
        b = 1 << level
        masks.append((s // (2 * b) == t // (2 * b)) & (s // b != t // b))
    masks = np.stack(masks, 1).astype(np.int32)
    n_freq = ROPE // 4
    inv = np.power(np.float32(10000.0), -np.arange(n_freq, dtype=np.float32) / np.float32(n_freq)).astype(np.float32)
    tok = np.arange(TL)
    ang = np.concatenate([(tok // GRID_W)[:, None].astype(np.float32) * inv,
                          (tok % GRID_W)[:, None].astype(np.float32) * inv], -1)
    ang = np.concatenate([ang, ang], -1).astype(np.float32).T
    rope = np.zeros((2 * ROPE, NT), np.float32)
    rope[:ROPE, :TL], rope[ROPE:, :TL] = np.cos(ang), np.sin(ang)
    rope[:ROPE, TL:] = 1.0
    return {"ident": ident, "masks": masks, "rope": rope}


INPUTS = ["x_prompt", "x_sample", "cache_ckv", "cache_krope", "state_hgrn_fwd", "state_hgrn_bwd", "c", "c_ctx",
          "w_mod", "b_mod", "g_mix", "w_in", "g_q", "w_uq", "g_kv", "w_ukv", "w_mla_o", "lb_param", "g_hg",
          "w_hg_o", "w_out", "g_ffn", "w_ffn_in", "conv_w", "conv_b", "w_ffn_out", "g_final"]
ROW_VECTORS = ("b_mod", "g_mix", "g_ffn", "g_final", "conv_b", "g_q", "g_kv", "g_hg", "lb_param", "conv_w", "c", "c_ctx")
MATRICES = ("w_mod", "w_in", "w_uq", "w_ukv", "w_mla_o", "w_hg_o", "w_out", "w_ffn_in", "w_ffn_out")
OUTPUTS = [("y_prompt", (1, TC, D)), ("y_sample", (1, TL, D)), ("new_ckv", (1, 1, TC, KVL)),
           ("new_krope", (1, 1, TC, ROPE)), ("new_state_fwd", (1, 1, HH, DK, DK)),
           ("new_state_bwd", (1, 1, HH, DK, DK))]


def layout(inputs):
    arrays = {}
    for name in INPUTS:
        a = np.ascontiguousarray(inputs[name])
        if name in ROW_VECTORS:
            a = a.reshape(-1, P)
        elif name in MATRICES:
            a = a.reshape(a.shape[-2], a.shape[-1])
        elif name in ("state_hgrn_fwd", "state_hgrn_bwd"):
            a = a.reshape(HH * DK, DK)
        else:
            a = a.reshape(-1, a.shape[-1])
        arrays[name] = a
    arrays.update(constants())
    return arrays


def build(nc, arrays):
    io = {}
    for name, a in arrays.items():
        io[name] = nc.dram_tensor(f"in_{name}", a.shape, mybir.dt.from_np(a.dtype), kind="ExternalInput").ap()
    for name, shape in OUTPUTS:
        flat = (int(np.prod(shape[:-1])), shape[-1])
        io[name] = nc.dram_tensor(f"out_{name}", flat, F32, kind="ExternalOutput").ap()
    for name, rows in (("x_t", D), ("proj", MAIN_CHUNKS * P), ("o_mla", HEADS * VD), ("o_hg", HH * DK)):
        io[name] = nc.dram_tensor(f"scratch_{name}", (rows, NT), F32, kind=SCRATCH).ap()
    io["x"] = lambda t: io["x_prompt"] if t == TILES - 1 else io["x_sample"][t * P:(t + 1) * P, :]
    program(nc, io)


SCRATCH = "Internal"


def kernel(**inputs):
    import concourse.bacc as bacc
    from concourse.bass_utils import run_bass_kernel_spmd

    nc = bacc.Bacc("TRN2", target_bir_lowering=False, num_devices=1)
    arrays = layout(inputs)
    build(nc, arrays)
    r = run_bass_kernel_spmd(nc, [{f"in_{k}": v for k, v in arrays.items()}], core_ids=[0])
    return tuple(r.results[0][f"out_{name}"].reshape(shape) for name, shape in OUTPUTS)
```

```python
import numpy as np
import concourse.bass as bass
from concourse import mybir
from contextlib import ExitStack

F32 = mybir.dt.float32
F32R = mybir.dt.float32r
I32 = mybir.dt.int32
ACT = mybir.ActivationFunctionType
ALU = mybir.AluOpType
AX = mybir.AxisListType

P = 128
D = 1024
KD = D // P
TL, TC = 1024, 128
NT = TL + TC
TILES = NT // P
CH, NCH = 384, 3
HEADS, NOPE, ROPE, VD = 8, 64, 32, 64
QH = NOPE + ROPE
QL, KVL = 384, 256
HH, DK = 4, 128
DFF = 2816
GRID_W = 64
EPS = 1e-6
GROUPS = ((0, TL), (TL, NT))
PAST = 128
NK = NT + PAST
KEY_CTX = TL + PAST
C_PQ, C_PKV, C_PKR, C_HG = 0, QL, QL + KVL, QL + KVL + ROPE
MAIN_CHUNKS = (5280 - C_HG) // P
SCALE = float(QH) ** -0.5
LEVELS = 7
ROWS_A = (("b_mod", 48), ("g_mix", 8), ("g_ffn", 8), ("g_final", 8), ("conv_b", 22), ("g_q", 3),
          ("g_kv", 2), ("g_hg", 4), ("lb_param", 16))
ROWS_B = (("conv_w", 66), ("c", 8), ("c_ctx", 8))


def starts(rows):
    at, out = 0, {}
    for name, n in rows:
        out[name] = at
        at += n
    return out, at


AT_A, NA = starts(ROWS_A)
AT_B, NB = starts(ROWS_B)


class Arena:

    def __init__(self, nc, offset):
        self.nc, self.at = nc, offset

    def __call__(self, name, shape, dtype=F32):
        size = int(np.prod(shape[1:])) * 4
        t = self.nc.alloc_sbuf_tensor_at(name, list(shape), dtype, offset=self.at)
        self.at += (size + 31) // 32 * 32
        return t


class Signals:

    def __init__(self, nc, ctx, prefix):
        self.nc, self.prefix, self.all = nc, prefix, []
        ctx.callback(self.clear)

    def __call__(self, name):
        self.all.append(self.nc.alloc_semaphore(f"{self.prefix}_{name}"))
        return self.all[-1]

    def clear(self):
        self.nc.clear_and_free_semaphores(self.all)
        self.nc.all_engine_barrier()


def tok3(t):
    return t.rearrange("p (j c) -> p j c", j=NCH)


class WeightStream:

    def __init__(self, nc, arena, sems, tag):
        self.nc = nc
        self.raw = [arena(f"{tag}_w_raw{s}", [P, KD, P]) for s in range(2)]
        self.hi = [arena(f"{tag}_w_hi{s}", [P, KD, P], F32R) for s in range(2)]
        self.lo = [arena(f"{tag}_w_lo{s}", [P, KD, P], F32R) for s in range(2)]
        self.loaded = [sems(f"w_loaded{s}") for s in range(2)]
        self.hi_ready = sems("w_hi_ready")
        self.lo_ready = sems("w_lo_ready")
        self.used = sems("w_used")

    def load(self, sp, c, s, pairs, free=True):
        if free:
            sp.wait_ge(self.lo_ready, c - 1)
        for n, (dst, src) in enumerate(pairs):
            sp.dma_start(dst, src).then_inc(self.loaded[s], 16)

    def split_hi(self, act, s, arrived, c, free=True, size=KD * P):
        act.wait_ge(self.loaded[s], arrived)
        if free:
            act.wait_ge(self.used, c - 1)
        flat = self.raw[s][:, :, :].rearrange("p k n -> p (k n)")[:, 0:size]
        out = self.hi[s][:, :, :].rearrange("p k n -> p (k n)")[:, 0:size]
        act.activation(out, flat, ACT.Copy).then_inc(self.hi_ready, 1)

    def split_lo(self, pool, s, c, free=True, size=KD * P):
        pool.wait_ge(self.hi_ready, c + 1)
        flat = [t[s][:, :, :].rearrange("p k n -> p (k n)")[:, 0:size] for t in (self.lo, self.raw, self.hi)]
        pool.tensor_tensor(flat[0], flat[1], flat[2], ALU.subtract).then_inc(self.lo_ready, 1)


def gemm_chunk(pe, psum, w_hi, w_lo, x_hi, x_lo, kts, before=None):
    last = None
    n, total = 0, 3 * len(kts)
    for (wk, xk) in kts:
        if before:
            before(xk)
        for w, x in ((w_hi, x_hi), (w_hi, x_lo), (w_lo, x_hi)):
            for j in range(NCH):
                last = pe.matmul(psum[:, j, 0:CH], w(wk), x(xk)[:, j * CH:(j + 1) * CH],
                                 start=(n == 0), stop=(n == total - 1))
            n += 1
    return last


class Norm:

    def __init__(self, arena, sems, tag, cst, kts, width, rb=None):
        self.cst, self.kts, self.width = cst, kts, width
        self.sq = [arena(f"{tag}_sq{i}", [P, NT]) for i in range(2)]
        self.acc = arena(f"{tag}_acc", [P, NT])
        self.stat = arena(f"{tag}_stat", [P, 2 * TILES])
        self.rb = arena(f"{tag}_rb", [P, NT]) if rb is None else rb
        self.sq_ready = sems(f"{tag}_sq_ready")
        self.acc_ready = sems(f"{tag}_acc_ready")
        self.sums_ready = sems(f"{tag}_sums_ready")
        self.std_ready = sems(f"{tag}_std_ready")
        self.rstd_ready = sems(f"{tag}_rstd_ready")
        self.rbp_ready = sems(f"{tag}_rbp_ready")
        self.rb_ready = sems(f"{tag}_rb_ready")

    def act_square(self, act, k, src):
        if k >= 2:
            act.wait_ge(self.acc_ready, max(1, k - 2))
        act.activation(self.sq[k % 2][:, :], src, ACT.Square).then_inc(self.sq_ready, 1)

    def dve_add(self, dve, k):
        dve.wait_ge(self.sq_ready, k + 1)
        if k == 1:
            dve.tensor_tensor(self.acc[:, :], self.sq[0][:, :], self.sq[1][:, :], ALU.add).then_inc(self.acc_ready, 1)
        if k >= 2:
            dve.wait_ge(self.acc_ready, k - 1)
            dve.tensor_tensor(self.acc[:, :], self.acc[:, :], self.sq[k % 2][:, :], ALU.add).then_inc(self.acc_ready, 1)

    def pe_sums(self, pe, psum):
        pe.wait_ge(self.acc_ready, self.kts - 1)
        for t in range(TILES):
            last = pe.matmul(psum[:, t:t + 1], self.acc[:, t * P:(t + 1) * P], self.cst.ones[:, 0:1], start=True, stop=True)
        last.then_inc(self.sums_ready, 1)

    def act_std(self, act, psum):
        act.wait_ge(self.sums_ready, 1)
        act.activation(self.stat[:, 0:TILES], psum[:, 0:TILES], ACT.Sqrt, scale=1.0 / self.width,
                       bias=self.cst.eps[:, 0:1]).then_inc(self.std_ready, 1)

    def dve_rstd(self, dve):
        dve.wait_ge(self.std_ready, 1)
        dve.reciprocal(self.stat[:, TILES:2 * TILES], self.stat[:, 0:TILES]).then_inc(self.rstd_ready, 1)

    def pe_broadcast(self, pe, psum3):
        pe.wait_ge(self.rstd_ready, 1)
        for t in range(TILES):
            last = pe.matmul(psum3[:, t // 3, (t % 3) * P:(t % 3 + 1) * P],
                             self.stat[:, TILES + t:TILES + t + 1].to_broadcast([P, P]), self.cst.ident[:, :],
                             start=True, stop=True)
        last.then_inc(self.rbp_ready, 1)

    def act_broadcast(self, act, psum3):
        act.wait_ge(self.rbp_ready, 1)
        act.activation(tok3(self.rb[:, :]), psum3[:, 0:NCH, 0:CH], ACT.Copy).then_inc(self.rb_ready, 1)


class Apply:

    def __init__(self, arena, sems, tag, rb, rb_ready=None):
        self.rb, self.rb_ready = rb, rb_ready
        self.y = [arena(f"{tag}_y{i}", [P, NT]) for i in range(2)]
        self.scaled = sems(f"{tag}_scaled")
        self.y_ready = sems(f"{tag}_y_ready")
        self.hi_ready = sems(f"{tag}_hi_ready")
        self.lo_ready = sems(f"{tag}_lo_ready")

    def dve(self, dve, k, src, affine):
        y = self.y[k % 2]
        if self.rb_ready is not None:
            dve.wait_ge(self.rb_ready, 1)
        if k >= 2:
            dve.wait_ge(self.lo_ready, k - 1)
        dve.tensor_tensor(y[:, :], src, self.rb[:, :], ALU.mult).then_inc(self.scaled, 1)
        dve.wait_ge(self.scaled, k + 1)
        for a, b, gain, bias in affine:
            if bias is None:
                last = dve.tensor_scalar(y[:, a:b], y[:, a:b], gain, None, ALU.mult)
            else:
                last = dve.tensor_scalar(y[:, a:b], y[:, a:b], gain, bias, ALU.mult, ALU.add)
        last.then_inc(self.y_ready, 1)

    def act(self, act, k, parts):
        act.wait_ge(self.y_ready, k + 1)
        for dst, a, b in parts:
            last = act.activation(dst, self.y[k % 2][:, a:b], ACT.Copy)
        last.then_inc(self.hi_ready, 1)

    def pool(self, pool, k, parts):
        pool.wait_ge(self.hi_ready, k + 1)
        for dst, hi, a, b in parts:
            last = pool.tensor_tensor(dst, self.y[k % 2][:, a:b], hi, ALU.subtract)
        last.then_inc(self.lo_ready, 1)


class Constants:

    def __init__(self, arena):
        self.ident = arena("ident", [P, P])
        self.ones = arena("ones", [P, P])
        self.eps = arena("eps", [P, 8])
        self.cols_a = arena("cols_a", [P, NA])
        self.cols_b = arena("cols_b", [P, NB])
        self.cc = arena("cc", [P, KD, 2])
        self.mod = arena("mod", [P, 48, 2])
        self.gain_mix = arena("gain_mix", [P, KD, 2])
        self.gain_ffn = arena("gain_ffn", [P, KD, 2])
        self.lb = arena("lb", [P, 8])
        self.lb1 = arena("lb1", [P, 8])

    def a(self, name, k):
        return self.cols_a[:, AT_A[name] + k:AT_A[name] + k + 1]

    def b(self, name, k):
        return self.cols_b[:, AT_B[name] + k:AT_B[name] + k + 1]


def make_gain(dve, cst, dst, sc, g, done):
    dve.tensor_scalar(dst[:, :, :], cst.mod[:, sc:sc + KD, :], 1.0, None, ALU.add).then_inc(done, 1)
    dve.wait_ge(done, 1)
    dve.tensor_tensor(dst[:, :, :], dst[:, :, :], cst.cols_a[:, AT_A[g]:AT_A[g] + KD].unsqueeze(2).to_broadcast([P, KD, 2]),
                      ALU.mult).then_inc(done, 1)
    dve.wait_ge(done, 2)


def stage_setup(nc, io, cst, arena, x_t, rb):
    with ExitStack() as ctx:
        sems = Signals(nc, ctx, "s1")
        XR = 4
        rows_a, rows_b = arena("rows_a", [P, P]), arena("rows_b", [P, P])
        x_rows = [arena(f"x_rows{i}", [P, D]) for i in range(XR)]
        w_mod = [arena(f"w_mod{i}", [P, KD, 512]) for i in range(2)]
        silu_c = arena("silu_c", [P, 2, KD])
        cc, mod_rows = cst.cc, arena("mod_rows", [2, 2 * D])
        lbt = arena("lbt", [P, 24])
        psum = ctx.enter_context(nc.psum_tensor("s1_psum", [P, 8, 512], F32))
        norm = Norm(arena, sems, "n1", cst, KD, D, rb)
        consts_loaded, ones_set = sems("consts_loaded"), sems("ones_set")
        x_loaded = [sems(f"x_loaded{i}") for i in range(XR)]
        wm_loaded = [sems(f"wm_loaded{i}") for i in range(2)]
        vec_t, vec_cols = sems("vec_transposed"), sems("vec_columns")
        silu_ready, cc_ready = sems("silu_ready"), sems("cc_ready")
        xt_ps, xt_ready = sems("x_transposed"), sems("x_t_ready")
        mod_ps, mod_row = sems("mod_product"), sems("mod_row_ready")
        modt_ps, mod_ready = sems("mod_transposed"), sems("mod_ready")
        gain1, lb_exp, lb_step = sems("gain_ready"), sems("lb_exp"), sems("lb_step")
        x_stored = sems("x_stored")
        mod_chunks = 2 * D // 512
        n_a = sum(n for _, n in ROWS_A)

        with nc.Block() as block:
            @block.sync
            def _(sp):
                sp.dma_start(cst.ident[:, :], io["ident"]).then_inc(consts_loaded, 16)
                for rows, at, spec in ((rows_a, AT_A, ROWS_A), (rows_b, AT_B, ROWS_B)):
                    for name, n in spec:
                        sp.dma_start(rows[at[name]:at[name] + n, :], io[name]).then_inc(consts_loaded, 16)
                for n in range(mod_chunks):
                    if n >= 2:
                        sp.wait_ge(mod_ps, n - 1)
                    sp.dma_start(w_mod[n % 2][:, :, :],
                                 io["w_mod"][:, n * 512:(n + 1) * 512].rearrange("(k p) n -> p k n", p=P)
                                 ).then_inc(wm_loaded[n % 2], 16)
                sp.wait_ge(xt_ready, 2 * TILES)
                sp.dma_start(io["x_t"].rearrange("(k p) n -> p k n", p=P), x_t[:, :, :]).then_inc(x_stored, 16)
                sp.wait_ge(x_stored, 16)

            @block.gpsimd
            def _(pool):
                pool.memset(cst.ones[:, :], 1.0)
                pool.memset(cst.eps[:, :], EPS).then_inc(ones_set, 1)
                for t in range(TILES):
                    if t >= XR:
                        pool.wait_ge(xt_ps, 2 * (t - XR + 1))
                    pool.dma_start(x_rows[t % XR][:, :], io["x"](t)).then_inc(x_loaded[t % XR], 16)

            @block.tensor
            def _(pe):
                pe.wait_ge(consts_loaded, 16 * (1 + len(ROWS_A) + len(ROWS_B)))
                pe.transpose(psum[:, 0, 0:NA], rows_a[0:NA, :], cst.ident[0:NA, 0:NA])
                pe.transpose(psum[:, 0, P:P + NB], rows_b[0:NB, :], cst.ident[0:NB, 0:NB]).then_inc(vec_t, 1)
                def products(n):
                    pe.wait_ge(wm_loaded[n % 2], 16 * (n // 2 + 1))
                    if n >= 2:
                        pe.wait_ge(mod_row, n - 1)
                    for k in range(KD):
                        last = pe.matmul(psum[0:2, 3 + n % 2, :], cc[:, k, :], w_mod[n % 2][:, k, :],
                                         start=(k == 0), stop=(k == KD - 1))
                    last.then_inc(mod_ps, 1)

                def columns(a, b):
                    pe.wait_ge(mod_row, (b + 3) // 4)
                    for j in range(a, b):
                        last = pe.transpose(psum[:, 0, 256 + 2 * j:256 + 2 * j + 2], mod_rows[0:2, j * P:(j + 1) * P],
                                            cst.ident[0:2, 0:2])
                    last.then_inc(modt_ps, 1)

                def tile(t):
                    pe.wait_ge(x_loaded[t % XR], 16 * (t // XR + 1))
                    for half in range(2):
                        r = 2 * t + half
                        if r >= 2:
                            pe.wait_ge(xt_ready, r - 1)
                        for k in range(4):
                            f = 4 * half + k
                            last = pe.transpose(psum[:, 1 + r % 2, k * P:(k + 1) * P],
                                                x_rows[t % XR][:, f * P:(f + 1) * P], cst.ident[:, :])
                        last.then_inc(xt_ps, 1)

                for t in range(TILES):
                    tile(t)
                    if t % 2 == 0 and t >= 2:
                        if t == 2:
                            pe.wait_ge(cc_ready, 1)
                        products(t // 2 - 1)
                pe.wait_ge(ones_set, 1)
                norm.pe_sums(pe, psum[:, 5, :])
                columns(0, 4 * mod_chunks)
                norm.pe_broadcast(pe, psum[:, 5:8, :])

            @block.scalar
            def _(act):
                act.wait_ge(vec_cols, 1)
                act.activation(silu_c[:, :, :].rearrange("p g k -> p (g k)"), cst.cols_b[:, AT_B["c"]:NB],
                               ACT.Silu).then_inc(silu_ready, 1)
                act.wait_ge(silu_ready, 1)
                act.activation(cc[:, :, :], silu_c[:, :, :].rearrange("p g k -> p k g"), ACT.Copy).then_inc(cc_ready, 1)
                act.wait_ge(lb_step, 1)
                act.activation(lbt[:, 8:24], lbt[:, 8:24], ACT.Exp).then_inc(lb_exp, 1)

                def rows(n):
                    act.wait_ge(mod_ps, n + 1)
                    act.activation(mod_rows[0:2, n * 512:(n + 1) * 512], psum[0:2, 3 + n % 2, :],
                                   ACT.Copy).then_inc(mod_row, 1)

                for n in range(mod_chunks - 1):
                    rows(n)
                act.wait_ge(xt_ready, 2 * TILES)
                for k in range(KD):
                    norm.act_square(act, k, x_t[:, k, :])
                rows(mod_chunks - 1)
                act.wait_ge(ones_set, 1)
                norm.act_std(act, psum[:, 5, :])
                norm.act_broadcast(act, psum[:, 5:8, :])

            @block.vector
            def _(dve):
                dve.wait_ge(vec_t, 1)
                dve.tensor_copy(cst.cols_a[:, :], psum[:, 0, 0:NA])
                dve.tensor_copy(cst.cols_b[:, :], psum[:, 0, P:P + NB]).then_inc(vec_cols, 1)
                dve.wait_ge(vec_cols, 1)
                lb0 = cst.cols_a[:, AT_A["lb_param"]:AT_A["lb_param"] + 8]
                lb1 = cst.cols_a[:, AT_A["lb_param"] + 8:AT_A["lb_param"] + 16]
                n_lb = [0]

                def step(ins):
                    ins.then_inc(lb_step, 1)
                    n_lb[0] += 1
                    dve.wait_ge(lb_step, n_lb[0])

                dve.tensor_tensor(lbt[:, 0:8], lb0, lb1, ALU.max).then_inc(vec_cols, 1)
                dve.wait_ge(vec_cols, 2)
                dve.tensor_tensor(lbt[:, 8:16], lb0, lbt[:, 0:8], ALU.subtract)
                step(dve.tensor_tensor(lbt[:, 16:24], lb1, lbt[:, 0:8], ALU.subtract))
                dve.wait_ge(lb_exp, 1)
                step(dve.tensor_tensor(lbt[:, 0:8], lbt[:, 8:16], lbt[:, 16:24], ALU.add))
                step(dve.reciprocal(lbt[:, 0:8], lbt[:, 0:8]))
                step(dve.tensor_tensor(cst.lb[:, :], lbt[:, 8:16], lbt[:, 0:8], ALU.mult))
                step(dve.tensor_scalar(cst.lb1[:, :], cst.lb[:, :], -1.0, 1.0, ALU.mult, ALU.add))
                for r in range(2 * TILES):
                    t, half = r // 2, r % 2
                    dve.wait_ge(xt_ps, r + 1)
                    dve.tensor_copy(x_t[:, 4 * half:4 * half + 4, t * P:(t + 1) * P],
                                    psum[:, 1 + r % 2, :].rearrange("p (k n) -> p k n", k=4)).then_inc(xt_ready, 1)
                for k in range(KD):
                    norm.dve_add(dve, k)
                norm.dve_rstd(dve)

                def finish(a, b, part):
                    dve.wait_ge(modt_ps, part)
                    dve.tensor_tensor(cst.mod[:, a:b, :],
                                      psum[:, 0, 256 + 2 * a:256 + 2 * b].rearrange("p (j g) -> p j g", g=2),
                                      cst.cols_a[:, a:b].unsqueeze(2).to_broadcast([P, b - a, 2]), ALU.add
                                      ).then_inc(mod_ready, 1)
                    dve.wait_ge(mod_ready, part)

                finish(0, 4 * mod_chunks, 1)
                make_gain(dve, cst, cst.gain_mix, KD, "g_mix", gain1)


def stage_in_projection(nc, io, cst, arena, stage, x_t, rb, h_hi, h_lo, pqkv, pkr):
    with ExitStack() as ctx:
        sems = Signals(nc, ctx, "s2")
        w = WeightStream(nc, arena, sems, "s2")
        app = Apply(arena, sems, "a1", rb)
        psum = [ctx.enter_context(nc.psum_tensor(f"s2_psum{i}", [P, 4, 512], F32)) for i in range(2)]
        copied = sems("copied")
        stored = [sems(f"stored{i}") for i in range(2)]
        rot_ready = sems("rot_ready")
        tail = 6
        total = MAIN_CHUNKS + tail
        w_in = io["w_in"].rearrange("(k p) n -> p k n", p=P)

        with nc.Block() as block:
            @block.sync
            def _(sp):
                def load(c, s, free=True):
                    w.load(sp, c, s, [(w.raw[s][:, :, :], w_in[:, :, bass.ds(C_HG + c * P, P)])], free)

                def store(c, s):
                    sp.wait_ge(copied, c + 1)
                    sp.dma_start(io["proj"][bass.ds(c * P, P), :], stage[s][:, :]).then_inc(stored[s], 16)

                load(0, 0, False)
                load(1, 1, False)
                with sp.Fori(0, MAIN_CHUNKS // 2 - 1) as i:
                    for s in range(2):
                        load(2 * i + (2 + s), s)
                        store(2 * i + s, s)
                for c in range(MAIN_CHUNKS, total):
                    s = c % 2
                    m = c - MAIN_CHUNKS
                    if m < 5:
                        w.load(sp, c, s, [(w.raw[s][:, :, :], w_in[:, :, m * P:(m + 1) * P])])
                    else:
                        w.load(sp, c, s, [(w.raw[s][:, :, 0:96], w_in[:, :, C_PKR - 64:C_PKR + 32])])
                    if m < 2:
                        store(c - 2, s)
                for s in range(2):
                    sp.wait_ge(stored[s], 16 * MAIN_CHUNKS // 2)

            @block.scalar
            def _(act):
                w.split_hi(act, 0, 16, 0, False)
                for k in range(KD):
                    app.act(act, k, [(h_hi[:, k, :], 0, NT)])
                    if k == 3:
                        w.split_hi(act, 1, 16, 1, False)
                with act.Fori(1, MAIN_CHUNKS // 2) as i:
                    for s in range(2):
                        w.split_hi(act, s, 16 * i + 16, 2 * i + s)
                for c in range(MAIN_CHUNKS, total):
                    s = c % 2
                    if c == total - 1:
                        act.wait_ge(w.loaded[s], 16 * (c // 2 + 1))
                        act.activation(w.raw[s][:, :, 96:112], w.raw[s][:, :, 80:96], ACT.Copy, scale=-1.0)
                        act.activation(w.raw[s][:, :, 112:128], w.raw[s][:, :, 64:80], ACT.Copy).then_inc(rot_ready, 1)
                        act.wait_ge(rot_ready, 1)
                    w.split_hi(act, s, 16 * (c // 2 + 1), c)

            @block.gpsimd
            def _(pool):
                w.split_lo(pool, 0, 0)
                for k in range(KD):
                    app.pool(pool, k, [(h_lo[:, k, :], h_hi[:, k, :], 0, NT)])
                w.split_lo(pool, 1, 1)
                with pool.Fori(1, total // 2) as i:
                    for s in range(2):
                        w.split_lo(pool, s, 2 * i + s)

            @block.tensor
            def _(pe):
                def chunk(c, s, free, before=None):
                    pe.wait_ge(w.lo_ready, c + 1)
                    if free:
                        pe.wait_ge(copied, c - 1)
                    last = gemm_chunk(pe, psum[s], lambda k: w.hi[s][:, k, :], lambda k: w.lo[s][:, k, :],
                                      lambda k: h_hi[:, k, :], lambda k: h_lo[:, k, :], [(k, k) for k in range(KD)], before)
                    last.then_inc(w.used, 1)

                chunk(0, 0, False, lambda k: pe.wait_ge(app.lo_ready, k + 1))
                chunk(1, 1, False)
                with pe.Fori(1, total // 2) as i:
                    for s in range(2):
                        chunk(2 * i + s, s, True)

            @block.vector
            def _(dve):
                def copy(c, s, dst):
                    dve.wait_ge(w.used, c + 1)
                    dve.tensor_copy(tok3(dst), psum[s][:, 0:NCH, 0:CH]).then_inc(copied, 1)

                for k in range(KD):
                    app.dve(dve, k, x_t[:, k, :], [(a, b, cst.gain_mix[:, k, g:g + 1], cst.mod[:, k, g:g + 1])
                                                   for g, (a, b) in enumerate(GROUPS)])
                copy(0, 0, stage[0][:, :])
                copy(1, 1, stage[1][:, :])
                with dve.Fori(1, MAIN_CHUNKS // 2) as i:
                    for s in range(2):
                        dve.wait_ge(stored[s], 16 * i)
                        copy(2 * i + s, s, stage[s][:, :])
                for m in range(5):
                    copy(MAIN_CHUNKS + m, m % 2, pqkv[:, m, :])
                dve.wait_ge(w.used, total)
                dve.tensor_copy(tok3(pkr[64:128, :]), psum[1][64:128, 0:NCH, 0:CH]).then_inc(copied, 1)


def stage_low_rank(nc, io, cst, arena, pqkv, pkr, rope, q_hi, q_lo, c_hi, c_lo, k_hi, k_lo):
    with ExitStack() as ctx:
        sems = Signals(nc, ctx, "s3")
        norm_kv, norm_q = Norm(arena, sems, "nkv", cst, 2, KVL), Norm(arena, sems, "nq", cst, 3, QL)
        app_kv, app_q = Apply(arena, sems, "akv", norm_kv.rb, norm_kv.rb_ready), Apply(arena, sems, "aq", norm_q.rb, norm_q.rb_ready)
        ckv_rows = arena("ckv_rows", [P, KVL])
        kr_rows = arena("kr_rows", [P, 96])
        ckv_t = arena("ckv_t", [P, 2, PAST])
        key = arena("key", [P, NK])
        part = [arena(f"rope_part{i}", [P, NT]) for i in range(2)]
        out_ckv = arena("out_ckv", [P, KVL])
        out_kr = arena("out_kr", [P, ROPE])
        psum = ctx.enter_context(nc.psum_tensor("s3_psum", [P, 8, 512], F32))
        loaded, cleared = sems("loaded"), sems("cleared")
        cache_t, cache_copied = sems("cache_transposed"), sems("cache_copied")
        parts_ready, key_ready = sems("parts_ready"), sems("key_ready")
        cache_hi, key_hi = sems("cache_hi"), sems("key_hi")
        ckv_out_t, outs, stored = sems("ckv_out_transposed"), sems("outs"), sems("stored")
        r = slice(64, 96)

        def places(k, dst):
            return [(dst[:, k, 0:TL], 0, TL), (dst[:, k, KEY_CTX:NK], TL, NT)]

        with nc.Block() as block:
            @block.sync
            def _(sp):
                sp.dma_start(ckv_rows[:, :], io["cache_ckv"]).then_inc(loaded, 16)
                sp.wait_ge(cleared, 1)
                sp.dma_start(kr_rows[:, 64:96], io["cache_krope"]).then_inc(loaded, 16)
                sp.dma_start(rope[64:128, :], io["rope"]).then_inc(loaded, 16)
                sp.wait_ge(outs, 1)
                sp.dma_start(io["new_krope"], out_kr[:, :]).then_inc(stored, 16)
                sp.wait_ge(outs, 2)
                sp.dma_start(io["new_ckv"], out_ckv[:, :]).then_inc(stored, 16)
                sp.wait_ge(stored, 32)

            @block.gpsimd
            def _(pool):
                pool.memset(kr_rows[:, :], 0.0).then_inc(cleared, 1)
                pool.wait_ge(cache_hi, 1)
                pool.tensor_tensor(c_lo[:, :, TL:KEY_CTX], ckv_t[:, :, :], c_hi[:, :, TL:KEY_CTX], ALU.subtract)
                for k in range(2):
                    app_kv.pool(pool, k, [(lo, hi, a, b) for (lo, a, b), (hi, _, _) in zip(places(k, c_lo), places(k, c_hi))])
                for k in range(3):
                    app_q.pool(pool, k, [(q_lo[:, k, :], q_hi[:, k, :], 0, NT)])

            @block.tensor
            def _(pe):
                pe.wait_ge(loaded, 48)
                for k in range(2):
                    pe.transpose(psum[:, 0, k * P:(k + 1) * P], ckv_rows[:, k * P:(k + 1) * P], cst.ident[:, :])
                pe.transpose(psum[0:96, 0, 256:384], kr_rows[:, :], cst.ident[:, :])
                pe.transpose(psum[:, 0, 384:384 + ROPE], pkr[r, TL:NT], cst.ident[r, r]).then_inc(cache_t, 1)
                norm_kv.pe_sums(pe, psum[:, 2, :])
                norm_q.pe_sums(pe, psum[:, 5, :])
                norm_kv.pe_broadcast(pe, psum[:, 2:5, :])
                norm_q.pe_broadcast(pe, psum[:, 5:8, :])
                pe.wait_ge(app_kv.y_ready, 2)
                for k in range(2):
                    last = pe.transpose(psum[:, 1, k * P:(k + 1) * P], app_kv.y[k][:, TL:NT], cst.ident[:, :])
                last.then_inc(ckv_out_t, 1)

            @block.scalar
            def _(act):
                for k in range(2):
                    norm_kv.act_square(act, k, pqkv[:, 3 + k, :])
                for k in range(3):
                    norm_q.act_square(act, k, pqkv[:, k, :])
                norm_kv.act_std(act, psum[:, 2, :])
                norm_q.act_std(act, psum[:, 5, :])
                act.wait_ge(cache_copied, 1)
                act.activation(c_hi[:, :, TL:KEY_CTX], ckv_t[:, :, :], ACT.Copy).then_inc(cache_hi, 1)
                norm_kv.act_broadcast(act, psum[:, 2:5, :])
                norm_q.act_broadcast(act, psum[:, 5:8, :])
                for k in range(2):
                    app_kv.act(act, k, places(k, c_hi))
                act.wait_ge(key_ready, 1)
                act.activation(k_hi[0][r, :], key[r, :], ACT.Copy)
                act.activation(k_hi[1][r, :], key[r, :], ACT.Copy).then_inc(key_hi, 1)
                for k in range(3):
                    app_q.act(act, k, [(q_hi[:, k, :], 0, NT)])

            @block.vector
            def _(dve):
                for k in range(2):
                    norm_kv.dve_add(dve, k)
                for k in range(3):
                    norm_q.dve_add(dve, k)
                norm_kv.dve_rstd(dve)
                norm_q.dve_rstd(dve)
                dve.wait_ge(cache_t, 1)
                dve.tensor_copy(ckv_t[:, :, :], psum[:, 0, 0:256].rearrange("p (k n) -> p k n", k=2)).then_inc(cache_copied, 1)
                dve.tensor_copy(key[r, TL:KEY_CTX], psum[r, 0, 256:384])
                dve.tensor_copy(out_kr[:, :], psum[:, 0, 384:384 + ROPE]).then_inc(outs, 1)
                dve.wait_ge(loaded, 48)
                dve.tensor_tensor(part[0][r, :], pkr[r, :], rope[r, :], ALU.mult)
                dve.tensor_tensor(part[1][r, :], pkr[96:128, :], rope[96:128, :], ALU.mult).then_inc(parts_ready, 1)
                dve.wait_ge(parts_ready, 1)
                dve.tensor_tensor(key[r, 0:TL], part[0][r, 0:TL], part[1][r, 0:TL], ALU.add)
                dve.tensor_tensor(key[r, KEY_CTX:NK], part[0][r, TL:NT], part[1][r, TL:NT], ALU.add).then_inc(key_ready, 1)
                for k in range(2):
                    app_kv.dve(dve, k, pqkv[:, 3 + k, :], [(0, NT, cst.a("g_kv", k), None)])
                for k in range(3):
                    app_q.dve(dve, k, pqkv[:, k, :], [(0, NT, cst.a("g_q", k), None)])
                dve.wait_ge(key_hi, 1)
                for b in range(2):
                    dve.tensor_tensor(k_lo[b][r, :], key[r, :], k_hi[b][r, :], ALU.subtract)
                dve.wait_ge(ckv_out_t, 1)
                dve.tensor_copy(out_ckv[:, :], psum[:, 1, 0:256]).then_inc(outs, 1)


HEAD_ITEMS = (
    ("L", 0), ("K", 0),
    ("S", 2), ("K", 1), ("L", 1), ("V", 0), ("Q", 0),
    ("S", 3), ("L", 2), ("V", 1), ("Q", 1),
    ("S", 4), ("X", 0), ("H", 0), ("L", 3), ("V", 2), ("X", 1),
    ("S", 5), ("M", 8), ("L", 4), ("V", 3),
    ("S", 6), ("M", 9), ("L", 5), ("V", 4), ("R", 1),
    ("S", 7), ("M", 0), ("D", 0), ("L", 6), ("V", 5), ("M", 1),
    ("S", 8), ("M", 2), ("L", 7), ("V", 6), ("M", 3), ("M", 6), ("D", 1), ("M", 4), ("M", 5),
    ("S", 9), ("W", 0), ("M", 7), ("L", 8), ("D", 2), ("V", 7), ("L", 9), ("R", 0), ("V", 8), ("V", 9),
    ("S", 10),
    ("S", 11))
NEXT_KINDS = "KQXHMR"
FIRST_ITEMS = tuple(x for x in HEAD_ITEMS if x[0] in NEXT_KINDS or x[0] == "S" and x[1] >= 10)
LAST_ITEMS = tuple(x for x in HEAD_ITEMS if not (x[0] in NEXT_KINDS + "W" or x[0] == "S" and x[1] >= 10))
POOL_LO = (4, 5, 6, 7)
BY_ACT, BY_DVE = "KQXR", "QXMR"


def unit_counts():
    table, n, act, dve, before = {}, 0, 0, 0, None
    for kind, u in HEAD_ITEMS:
        if kind in "KQXMR":
            table[kind, u] = (n, act, dve, before)
            halves_read = 2 if kind == "M" and u < 8 else 1
            n, act, dve, before = n + halves_read, act + (kind in BY_ACT), dve + halves_read * (kind in BY_DVE), (kind, u)
    return table, n, act, dve


UNIT, UNITS, UNIT_ACT, UNIT_DVE = unit_counts()


def stage_attention(nc, io, cst, arena, rope, qn_hi, qn_lo, c_hi, c_lo, k_hi, k_lo):
    with ExitStack() as ctx:
        sems = Signals(nc, ctx, "s4")
        hw_raw = [arena(f"hw_raw{e}", [P, 5, P]) for e in range(2)]
        hw_hi = [arena(f"hw_hi{e}", [P, 5, P], F32R) for e in range(2)]
        hw_lo = [arena(f"hw_lo{e}", [P, 5, P], F32R) for e in range(2)]
        qf = arena("qf", [P, NT])
        part = [arena(f"q_part{i}", [P, NT]) for i in range(2)]
        q_hi = [arena(f"q_hi{e}", [P, NT], F32R) for e in range(2)]
        q_lo = [arena(f"q_lo{e}", [P, NT], F32R) for e in range(2)]
        kvf = arena("kvf", [P, NK])
        v_hi = [arena(f"v_hi{e}", [P, 10, P], F32R) for e in range(2)]
        v_lo = [arena(f"v_lo{e}", [P, 10, P], F32R) for e in range(2)]
        prob = [arena(f"prob{i}", [P, TL]) for i in range(2)]
        p_hi = [arena(f"p_hi{i}", [P, TL], F32R) for i in range(5)]
        p_lo = [arena(f"p_lo{i}", [P, TL], F32R) for i in range(5)]
        o_raw = arena("o_raw", [P, NT])
        out = arena("att_out", [P, NT])
        tops = arena("att_tops", [P, 8, 3])
        maxima = arena("att_maxima", [P, TILES])
        ps_s = [ctx.enter_context(nc.psum_tensor(f"ps_s{i}", [P, 2, 512], F32)) for i in range(2)]
        ps_m = ctx.enter_context(nc.psum_tensor("ps_m", [P, 2, 512], F32))
        ps_o = ctx.enter_context(nc.psum_tensor("ps_o", [P, 2, 512], F32))
        ps_oc = ps_s[1][:, 1, 0:TC]
        hw_loaded = [sems(f"hw_loaded{e}") for e in range(2)]
        hw_rot, hw_hi_ready, hw_lo_ready = sems("hw_rot"), sems("hw_hi_ready"), sems("hw_lo_ready")
        ones_set, fixed_set = sems("ones_set"), sems("fixed_set")
        m_full, m_act, m_dve = sems("m_full"), sems("m_act"), sems("m_dve")
        s_full, exp_done, hi_ready = sems("s_full"), sems("exp_done"), sems("hi_ready")
        lo_dve, lo_pool = sems("lo_dve"), sems("lo_pool")
        o_full, o_read, quotient, o_stored = sems("o_full"), sems("o_read"), sems("quotient"), sems("o_stored")
        inv_step = sems("inv_step")
        q_part_ready, q_roped, q_hi_ready, q_ready = sems("q_part_ready"), sems("q_roped"), sems("q_hi_ready"), sems("q_ready")
        k_hi_ready, k_ready, maxima_ready = sems("k_hi_ready"), sems("k_ready"), sems("maxima_ready")
        r = slice(64, 96)
        m_flat = ps_m[:, :, :].rearrange("p j c -> p (j c)")
        uq = io["w_uq"].rearrange("(k p) n -> p k n", p=P)
        ukv = io["w_ukv"].rearrange("(k p) n -> p k n", p=P)

        def heads(engine, one):
            first = tuple(x for x in HEAD_ITEMS if x[0] != "D")
            after = tuple(x for x in HEAD_ITEMS if x[0] != "W")
            one(0, 0, 0, first)
            one(0, 1, 1, HEAD_ITEMS)
            with engine.Fori(1, HEADS // 2 - 1) as i:
                for e in range(2):
                    one(i, 2 * i + e, e, HEAD_ITEMS)
            one(HEADS // 2 - 1, HEADS - 2, 0, after)
            one(HEADS // 2 - 1, HEADS - 1, 1, LAST_ITEMS)

        def lo_of(h, k):
            if k in POOL_LO:
                return lo_pool, len(POOL_LO) * h + (POOL_LO.index(k) + 1)
            return lo_dve, (10 - len(POOL_LO)) * h + (k - sum(x < k for x in POOL_LO) + 1)

        def pieces(u):
            return (0, TL) if u == 0 else (TL, NT)

        with nc.Block() as block:
            @block.sync
            def _(sp):
                def load(h, e, free):
                    if free:
                        sp.wait_ge(hw_lo_ready, h - 1)
                    sp.dma_start(hw_raw[e][:, 0:3, 0:QH], uq[:, :, bass.ds(h * QH, QH)]).then_inc(hw_loaded[e], 16)
                    sp.dma_start(hw_raw[e][:, 3:5, :], ukv[:, :, bass.ds(h * P, P)]).then_inc(hw_loaded[e], 16)

                def store(h):
                    sp.wait_ge(quotient, h + 1)
                    sp.dma_start(io["o_mla"][bass.ds(h * VD, VD), :], out[64:128, :]).then_inc(o_stored, 16)

                load(0, 0, False)
                load(1, 1, False)

                def one(i, h, e, items):
                    if ("W", 0) in items:
                        load(h + 2, e, True)
                    if ("D", 0) in items:
                        store(h - 1)

                heads(sp, one)
                store(HEADS - 1)
                sp.wait_ge(o_stored, 16 * HEADS)

            @block.tensor
            def _(pe):
                def item(kind, u, h, e, first=False):
                    n = 1 - e
                    if kind in "KQXMR":
                        units, act_reads, dve_reads, before = UNIT[kind, u]
                        if not (first and units == 0):
                            if before is None:
                                before = ("R", 0)
                            by_banks = kind == before[0] == "M" and max(u, before[1]) < 8
                            if before[0] in BY_ACT:
                                pe.wait_ge(m_act, UNIT_ACT * (h + 1) + act_reads)
                            if before[0] in BY_DVE:
                                pe.wait_ge(m_dve, UNIT_DVE * (h + 1) + dve_reads - by_banks)
                    if kind == "K":
                        a, width = (0, 512) if u == 0 else (TL, NK - TL)
                        if u == 0:
                            pe.wait_ge(hw_lo_ready, h + 2)
                        for j in range(2 - u):
                            m = 0
                            for k in range(2):
                                for w, c in ((hw_hi, c_hi), (hw_hi, c_lo), (hw_lo, c_hi)):
                                    last = pe.matmul(ps_m[:, j, 0:width], w[n][:, 3 + k, :],
                                                     c[:, k, a + j * 512:a + j * 512 + width], start=(m == 0), stop=(m == 5))
                                    m += 1
                        last.then_inc(m_full, 1)
                    if kind == "Q":
                        a, width = (0, 512) if u == 0 else (TL, TC)
                        m = 0
                        for k in range(3):
                            for w, x in ((hw_hi, qn_hi), (hw_hi, qn_lo), (hw_lo, qn_hi)):
                                for j in range(2 - u):
                                    last = pe.matmul(ps_m[:, j, 0:width], w[n][:, k, :],
                                                     x[:, k, a + j * 512:a + j * 512 + width], start=(m == 0), stop=(m == 8))
                                m += 1
                        last.then_inc(m_full, 1)
                    if kind == "X":
                        for t in range(8 if u == 0 else 2):
                            last = pe.transpose(m_flat[:, t * P:(t + 1) * P], kvf[:, (8 * u + t) * P:(8 * u + t + 1) * P],
                                                cst.ident[:, :])
                        last.then_inc(m_full, 1)
                    if kind == "M":
                        if u == 8:
                            pe.wait_ge(q_hi_ready, h + 2)
                            pe.wait_ge(k_hi_ready, h + 2)
                            for t in range(8):
                                last = pe.matmul(m_flat[:, t * P:(t + 1) * P], q_hi[n][0:QH, t * P:(t + 1) * P],
                                                 k_hi[n][0:QH, TL:KEY_CTX], start=True, stop=True)
                        elif u == 9:
                            last = pe.matmul(m_flat[:, 0:TC], q_hi[n][0:QH, TL:NT], k_hi[n][0:QH, KEY_CTX:NK],
                                             start=True, stop=True)
                        else:
                            for j in range(2):
                                if j == 1 and by_banks:
                                    pe.wait_ge(m_dve, UNIT_DVE * (h + 1) + dve_reads)
                                last = pe.matmul(ps_m[:, j, :], q_hi[n][0:QH, u * P:(u + 1) * P],
                                                 k_hi[n][0:QH, j * 512:(j + 1) * 512], start=True, stop=True)
                                if j == 0:
                                    last.then_inc(m_full, 1)
                        last.then_inc(m_full, 1)
                    if kind == "R":
                        if u == 0:
                            pe.wait_ge(maxima_ready, h + 2)
                        for n_t, t in enumerate(range(8) if u == 0 else (8,)):
                            last = pe.matmul(m_flat[0:1, n_t * P:(n_t + 1) * P], maxima[:, t:t + 1], cst.ident[:, :],
                                             start=True, stop=True)
                        last.then_inc(m_full, 1)
                    if kind == "S":
                        of, k = (h, u) if u < 10 else (h + 1, u - 10)
                        b = e if u < 10 else n
                        if not (first and u >= 10):
                            pe.wait_ge(exp_done, 10 * of + (k - 1))
                        if u == 11 and not first:
                            pe.wait_ge(o_read, 2 * h + 2)
                        if u == 10:
                            pe.wait_ge(q_ready, h + 2)
                            pe.wait_ge(k_ready, h + 2)
                            pe.wait_ge(m_dve, UNIT_DVE * (h + 2))
                        parts = ((k_hi, q_hi), (k_hi, q_lo), (k_lo, q_hi))
                        for m, (a, x) in enumerate(parts):
                            if k == 9:
                                last = pe.matmul(ps_s[1][:, 0, 0:TC], a[b][0:QH + 1, KEY_CTX:NK], x[b][0:QH + 1, TL:NT],
                                                 start=(m == 0), stop=(m == 2))
                            else:
                                for j in range(2):
                                    last = pe.matmul(ps_s[k % 2][:, j, :], a[b][0:QH + 1, k * P:(k + 1) * P],
                                                     x[b][0:QH + 1, j * 512:(j + 1) * 512], start=(m == 0), stop=(m == 2))
                        last.then_inc(s_full, 1)
                    if kind == "V":
                        pe.wait_ge(*lo_of(h, u))
                        if u == 0 and not first:
                            pe.wait_ge(o_read, 2 * h - 1)
                        parts = ((v_hi, p_hi), (v_hi, p_lo), (v_lo, p_hi))
                        for m, (a, x) in enumerate(parts):
                            if u == 9:
                                last = pe.matmul(ps_oc, a[e][:, 9, :], x[9 % 5][:, 0:TC], start=(m == 0), stop=(m == 2))
                            else:
                                for j in range(2):
                                    last = pe.matmul(ps_o[:, j, :], a[e][:, u, :], x[u % 5][:, j * 512:(j + 1) * 512],
                                                     start=(u == 0 and m == 0), stop=(u == 8 and m == 2))
                        if u >= 8:
                            last.then_inc(o_full, 1)

                for kind, u in FIRST_ITEMS:
                    if kind == "X" and u == 0:
                        pe.wait_ge(fixed_set, 1)
                    item(kind, u, -1, 1, True)

                def one(i, h, e, items):
                    for kind, u in items:
                        item(kind, u, h, e, isinstance(h, int) and h == 0 and kind == "V")

                heads(pe, one)

            @block.scalar
            def _(act):
                def split(h, e, uses):
                    act.wait_ge(hw_loaded[e], 32 * uses)
                    act.activation(hw_raw[e][:, 0:3, 96:112], hw_raw[e][:, 0:3, 80:96], ACT.Copy, scale=-1.0)
                    act.activation(hw_raw[e][:, 0:3, 112:128], hw_raw[e][:, 0:3, 64:80], ACT.Copy).then_inc(hw_rot, 1)
                    act.wait_ge(hw_rot, h + 1)
                    act.activation(hw_hi[e][:, :, :], hw_raw[e][:, :, :], ACT.Copy).then_inc(hw_hi_ready, 1)

                def inverse(h, step, store_before=True):
                    if step == 0:
                        act.wait_ge(o_read, 2 * h + 2)
                        if store_before:
                            act.wait_ge(o_stored, 16 * h)
                        act.activation(out[64:128, :], o_raw[0:64, :], ACT.Ln).then_inc(inv_step, 1)
                    if step == 1:
                        act.wait_ge(inv_step, 2 * h + 1)
                        act.activation(out[64:128, :], out[64:128, :], ACT.Exp, scale=-1.0).then_inc(inv_step, 1)

                def item(kind, u, i, h, e, first=False):
                    n = 1 - e
                    if kind in BY_ACT:
                        units, reads, _, _ = UNIT[kind, u]
                        act.wait_ge(m_full, UNITS * (h + 1) + (units + 1))
                        done = UNIT_ACT * (h + 1) + (reads + 1)
                    if kind == "K":
                        a, b = (0, TL) if u == 0 else (TL, NK)
                        act.activation(kvf[:, a:b], m_flat[:, 0:b - a], ACT.Copy).then_inc(m_act, 1)
                        if u == 1:
                            act.wait_ge(m_act, done)
                            act.activation(k_hi[n][0:64, :], kvf[0:64, :], ACT.Copy).then_inc(k_hi_ready, 1)
                    if kind == "Q":
                        a, b = pieces(u)
                        act.activation(qf[0:64, a:b], m_flat[0:64, 0:b - a], ACT.Copy).then_inc(m_act, 1)
                    if kind == "H":
                        act.wait_ge(q_roped, 2 * h + 4)
                        act.wait_ge(m_act, UNIT_ACT * (h + 1) + (UNIT["Q", 1][1] + 1))
                        act.activation(q_hi[n][0:QH, :], qf[0:QH, :], ACT.Copy).then_inc(q_hi_ready, 1)
                    if kind == "X":
                        t, tiles = 8 * u, 8 - 6 * u
                        src = m_flat[:, 0:tiles * P].rearrange("p (t n) -> p t n", n=P)[:, :, 64:128]
                        act.activation(v_hi[n][:, t:t + tiles, 64:128], src, ACT.Copy).then_inc(m_act, 1)
                    if kind == "R":
                        a, b = pieces(u)
                        act.activation(q_hi[n][96:97, a:b], m_flat[0:1, 0:b - a], ACT.Copy, scale=-1.0).then_inc(m_act, 1)
                    if kind == "S":
                        of, k = (h, u) if u < 10 else (h + 1, u - 10)
                        width = TC if k == 9 else TL
                        act.wait_ge(s_full, 10 * of + (k + 1))
                        if not (first and u >= 10):
                            act.wait_ge(*(lo_of(of, k - 2) if k >= 2 else lo_of(of - 1, k + 8)))
                        src = ps_s[k % 2][:, :, :].rearrange("p j c -> p (j c)")[:, 0:width]
                        act.activation(prob[k % 2][:, 0:width], src, ACT.Exp, scale=SCALE).then_inc(exp_done, 1)
                        act.wait_ge(exp_done, 10 * of + (k + 1))
                        act.activation(p_hi[k % 5][:, 0:width], prob[k % 2][:, 0:width], ACT.Copy).then_inc(hi_ready, 1)
                    if kind == "V" and u >= 8:
                        act.wait_ge(o_full, 2 * h + (u - 7))
                        if u == 8:
                            if not first:
                                act.wait_ge(quotient, h)
                            act.activation(o_raw[:, 0:TL].rearrange("p (j c) -> p j c", j=2), ps_o[:, :, :],
                                           ACT.Copy).then_inc(o_read, 1)
                        else:
                            act.activation(o_raw[:, TL:NT], ps_oc, ACT.Copy).then_inc(o_read, 1)
                    if kind == "W":
                        split(h + 2, e, i + 2)
                    if kind == "D":
                        inverse(h - 1, u, not (isinstance(h, int) and h == 1))

                split(0, 0, 1)
                split(1, 1, 1)
                act.wait_ge(ones_set, 1)
                for e in range(2):
                    act.activation(k_hi[e][96:97, :], kvf[96:97, :], ACT.Copy)
                    act.activation(k_lo[e][96:97, :], kvf[96:97, :], ACT.Copy, scale=0.0)
                    ones = kvf[:, 0:640].rearrange("p (t n) -> p t n", n=64)
                    act.activation(v_hi[e][:, :, 0:64], ones, ACT.Copy)
                    last = act.activation(v_lo[e][:, :, 0:64], ones, ACT.Copy, scale=0.0)
                last.then_inc(fixed_set, 1)
                act.wait_ge(fixed_set, 1)
                for kind, u in FIRST_ITEMS:
                    item(kind, u, -1, -1, 1, True)

                def one(i, h, e, items):
                    for kind, u in items:
                        item(kind, u, i, h, e, isinstance(h, int) and h == 0 and kind == "V")

                heads(act, one)
                for step in range(2):
                    inverse(HEADS - 1, step)

            @block.vector
            def _(dve):
                def quotients(h):
                    dve.wait_ge(inv_step, 2 * h + 2)
                    dve.tensor_tensor(out[64:128, :], out[64:128, :], o_raw[64:128, :], ALU.mult).then_inc(quotient, 1)

                def item(kind, u, h, e, first=False):
                    n = 1 - e
                    if kind in BY_DVE:
                        units, act_reads, reads, _ = UNIT[kind, u]
                        dve.wait_ge(m_full, UNITS * (h + 1) + (units + 1))
                    if kind == "Q":
                        a, b = pieces(u)
                        dve.tensor_tensor(part[0][r, a:b], m_flat[r, 0:b - a], rope[r, a:b], ALU.mult).then_inc(q_part_ready, 1)
                        dve.tensor_tensor(part[1][r, a:b], m_flat[96:128, 0:b - a], rope[96:128, a:b],
                                          ALU.mult).then_inc(m_dve, 1)
                        dve.wait_ge(q_part_ready, 2 * h + (3 + u))
                        dve.wait_ge(m_dve, UNIT_DVE * (h + 1) + (reads + 1))
                        dve.tensor_tensor(qf[r, a:b], part[0][r, a:b], part[1][r, a:b], ALU.add).then_inc(q_roped, 1)
                    if kind == "X":
                        t, tiles = 8 * u, 8 - 6 * u
                        dve.wait_ge(m_act, UNIT_ACT * (h + 1) + (act_reads + 1))
                        src = m_flat[:, 0:tiles * P].rearrange("p (t n) -> p t n", n=P)[:, :, 64:128]
                        dve.tensor_tensor(v_lo[n][:, t:t + tiles, 64:128], src, v_hi[n][:, t:t + tiles, 64:128],
                                          ALU.subtract).then_inc(m_dve, 1)
                    if kind == "M":
                        if u == 8:
                            dve.tensor_reduce(tops[:, :, 2:3], m_flat[:, :].rearrange("p (t n) -> p t n", n=P), axis=AX.X,
                                              op=ALU.max).then_inc(m_dve, 1)
                        elif u == 9:
                            dve.tensor_reduce(maxima[:, 8:9], m_flat[:, 0:TC], axis=AX.X, op=ALU.max).then_inc(m_dve, 1)
                        else:
                            for j in range(2):
                                if j == 1:
                                    dve.wait_ge(m_full, UNITS * (h + 1) + (units + 2))
                                dve.tensor_reduce(tops[:, u, j:j + 1], ps_m[:, j, :], axis=AX.X, op=ALU.max).then_inc(m_dve, 1)
                        if u == 7:
                            dve.wait_ge(m_dve, UNIT_DVE * (h + 1) + (reads + 2))
                            dve.tensor_reduce(maxima[:, 0:8], tops[:, :, :], axis=AX.X, op=ALU.max).then_inc(maxima_ready, 1)
                    if kind == "R":
                        a, b = pieces(u)
                        dve.wait_ge(m_act, UNIT_ACT * (h + 1) + (act_reads + 1))
                        dve.scalar_tensor_tensor(q_lo[n][96:97, a:b], m_flat[0:1, 0:b - a], -1.0, q_hi[n][96:97, a:b],
                                                 ALU.mult, ALU.subtract).then_inc(m_dve, 1)
                    if kind == "L" and u not in POOL_LO:
                        width = TC if u == 9 else TL
                        dve.wait_ge(hi_ready, 10 * h + (u + 1))
                        dve.tensor_tensor(p_lo[u % 5][:, 0:width], prob[u % 2][:, 0:width], p_hi[u % 5][:, 0:width],
                                          ALU.subtract).then_inc(lo_dve, 1)
                    if kind == "D" and u == 2:
                        quotients(h - 1)
                dve.wait_ge(fixed_set, 1)
                for kind, u in FIRST_ITEMS:
                    item(kind, u, -1, 1)

                def one(i, h, e, items):
                    for kind, u in items:
                        item(kind, u, h, e)

                heads(dve, one)
                quotients(HEADS - 1)

            @block.gpsimd
            def _(pool):
                def split_weights(h, e):
                    pool.wait_ge(hw_hi_ready, h + 1)
                    pool.tensor_tensor(hw_lo[e][:, :, :], hw_raw[e][:, :, :], hw_hi[e][:, :, :],
                                       ALU.subtract).then_inc(hw_lo_ready, 1)

                def item(kind, u, h, e):
                    n = 1 - e
                    if kind == "K" and u == 1:
                        pool.wait_ge(k_hi_ready, h + 2)
                        pool.tensor_tensor(k_lo[n][0:64, :], kvf[0:64, :], k_hi[n][0:64, :], ALU.subtract).then_inc(k_ready, 1)
                    if kind == "H":
                        pool.wait_ge(q_hi_ready, h + 2)
                        pool.tensor_tensor(q_lo[n][0:QH, :], qf[0:QH, :], q_hi[n][0:QH, :], ALU.subtract).then_inc(q_ready, 1)
                    if kind == "L" and u in POOL_LO:
                        pool.wait_ge(hi_ready, 10 * h + (u + 1))
                        pool.tensor_tensor(p_lo[u % 5][:, :], prob[u % 2][:, :], p_hi[u % 5][:, :],
                                           ALU.subtract).then_inc(lo_pool, 1)
                    if kind == "W":
                        split_weights(h + 2, e)

                pool.memset(kvf[:, :], 1.0).then_inc(ones_set, 1)
                split_weights(0, 0)
                split_weights(1, 1)
                for kind, u in FIRST_ITEMS:
                    item(kind, u, -1, 1)

                def one(i, h, e, items):
                    for kind, u in items:
                        item(kind, u, h, e)

                heads(pool, one)


def sibling_view(t, first, n, b):
    base = t[:, 0, first:first + n]
    return bass.AP(base.tensor, base.offset, [base.ap[0], [2 * b, n // (2 * b)], [NT + b, 2], [1, b]])


def halves(t, plane, g, b):
    v = t[:, plane, g * CH:(g + 1) * CH].rearrange("p (n h b) -> p n h b", h=2, b=b)
    return v[:, :, 0, :], v[:, :, 1, :]


def block_totals(t, plane, g, b):
    n = CH // (2 * b)
    v = t[:, plane, 2 * n * g:2 * n * (g + 1)].rearrange("p (n h) -> p n h", h=2)
    return [v[:, :, h].unsqueeze(2).to_broadcast([P, n, b]) for h in range(2)]


def stage_hgrn(nc, io, cst, arena):
    with ExitStack() as ctx:
        sems = Signals(nc, ctx, "s5")
        raw = arena("hg_raw", [P, 5, NT])
        tot = [arena(f"tot{n}", [P, 2, NT >> n]) for n in range(LEVELS + 1)]
        sig = arena("hg_sig", [P, 2, NT])
        q, kd = arena("hg_q", [P, NT]), arena("hg_kd", [P, NT])
        qd, kk = arena("hg_qd", [P, 2, NT]), arena("hg_kk", [P, 2, NT])
        k_level = [arena(f"k_level{i}", [P, NT]) for i in range(2)]
        gate = arena("hg_gate", [P, NT])
        v_tok, scores = arena("v_tok", [P, TILES, P]), arena("hg_scores", [P, TILES, P])
        k_tok = arena("k_tok", [P, 2, TILES, P])
        state = arena("hg_state", [P, 2, 8, P])
        ctx_state = arena("ctx_state", [P, 2, P])
        osq, gated = arena("osq", [P, NT]), arena("gated", [P, NT])
        ostat = arena("ostat", [P, 2 * TILES])
        out = arena("hg_out", [P, NT])
        masks = arena("masks", [P, LEVELS + 1, P], I32)
        w_mod = [arena(f"w_mod{i}", [P, KD, 512]) for i in range(2)]
        mod_rows = arena("hg_mod_rows", [2, D])
        hv = arena("hg_vec", [P, 8])
        psum = ctx.enter_context(nc.psum_tensor("s5_psum", [P, 8, 512], F32))
        masks_loaded, loaded, state_loaded = sems("masks_loaded"), sems("loaded"), sems("state_loaded")
        sig_ready, vec_ready, f_ready, in_ready = sems("sig_ready"), sems("vec_ready"), sems("f_ready"), sems("in_ready")
        k_in, kl_ready = sems("k_in"), sems("k_level_ready")
        v_ps, v_ready = sems("v_transposed"), sems("v_ready")
        lv_ps, a_done = sems("level_product"), sems("scores_taken")
        q_upd, k_upd, tot_ready = sems("q_updated"), sems("k_updated"), sems("tot_ready")
        kt_ps, kt_ready, u_ps = sems("k_transposed"), sems("k_tok_ready"), sems("u_product")
        s_step, ctx_ready, ctx_stored = sems("state_step"), sems("ctx_ready"), sems("ctx_stored")
        o_ps, osq_ready, m_ps, std_ready = sems("o_product"), sems("osq_ready"), sems("mean_product"), sems("std_ready")
        gated_ready, rstd_ready, rb_ps = sems("gated_ready"), sems("rstd_ready"), sems("rstd_broadcast")
        gate_ready, stored = sems("gate_ready"), sems("stored")
        wm_loaded = [sems(f"wm_loaded{i}") for i in range(2)]
        mod_ps, mod_row, modt_ps, mod_ready = [sems(f"mod_product{i}") for i in range(2)], sems("mod_row_ready"), sems("mod_transposed"), sems("mod_ready")
        gain_done = sems("gain_done")
        idle = sems("idle")
        LU, UPD = 3 * (LEVELS + 1), 3 * LEVELS
        STREAMS = (1, 2, 0, 4, 3)

        with nc.Block() as block:
            @block.sync
            def _(sp):
                sp.dma_start(masks[:, :, :], io["masks"]).then_inc(masks_loaded, 16)

                def load_streams(h):
                    for n, stream in enumerate(STREAMS):
                        sp.dma_start(raw[:, n, :], io["proj"][bass.ds((stream * HH + h) * P, P), :]).then_inc(loaded, 16)

                def load_mod(h):
                    for n in range(2):
                        if h:
                            sp.wait_ge(mod_ps[n], h)
                        sp.dma_start(w_mod[n][:, :, :], io["w_mod"][:, (4 + 2 * h + n) * 512:(5 + 2 * h + n) * 512]
                                     .rearrange("(k p) n -> p k n", p=P)).then_inc(wm_loaded[n], 16)

                def head(h, more):
                    sp.wait_ge(idle, h + 1)
                    for d, (name, c) in enumerate((("state_hgrn_fwd", 0), ("state_hgrn_bwd", 7))):
                        sp.dma_start(state[:, d, c, :], io[name][bass.ds(h * P, P), :]).then_inc(state_loaded, 16)
                    if more:
                        sp.wait_ge(v_ps, 3 * h + 3)
                        sp.wait_ge(gate_ready, h + 1)
                        load_streams(h + 1)
                    sp.wait_ge(ctx_ready, h + 1)
                    for d, name in enumerate(("new_state_fwd", "new_state_bwd")):
                        sp.dma_start(io[name][bass.ds(h * P, P), :], ctx_state[:, d, :]).then_inc(ctx_stored, 16)
                    if more:
                        load_mod(h + 1)
                    sp.wait_ge(idle, h + 2)
                    sp.dma_start(io["o_hg"][bass.ds(h * P, P), :], out[:, :]).then_inc(stored, 16)
                    sp.wait_ge(ctx_stored, 32 * h + 32)
                    sp.wait_ge(stored, 16 * h + 16)

                load_streams(0)
                load_mod(0)
                for h in range(HH):
                    head(h, h < HH - 1)

            @block.scalar
            def _(act):
                def gates(h):
                    act.wait_ge(loaded, 80 * h + 80)
                    act.activation(tot[0][:, :, :], raw[:, 0:2, :], ACT.Sigmoid).then_inc(sig_ready, 1)
                    act.activation(sig[:, :, :], raw[:, 2:4, :], ACT.Sigmoid).then_inc(sig_ready, 1)

                def head(h, more):
                    for g in range(3):
                        act.wait_ge(v_ps, 3 * h + (g + 1))
                        act.activation(v_tok[:, 3 * g:3 * g + 3, :],
                                       psum[:, 6 + g % 2, 0:CH].rearrange("p (t n) -> p t n", t=3),
                                       ACT.Copy).then_inc(v_ready, 1)
                    act.wait_ge(f_ready, 3 * h + 2)
                    for lv in range(1, LEVELS + 1):
                        b = 1 << (lv - 1)
                        for g in range(3):
                            if lv >= 2:
                                act.wait_ge(k_upd, UPD * h + (3 * (lv - 2) + g + 1))
                            if lv >= 3:
                                act.wait_ge(lv_ps, LU * h + (3 * (lv - 2) + g + 1))
                            act.activation(k_level[lv % 2][:, g * CH:(g + 1) * CH].rearrange("p (n h b) -> p n h b", h=2, b=b),
                                           sibling_view(kk, g * CH, CH, b), ACT.Copy).then_inc(kl_ready, 1)
                    for n in range(6):
                        d, g = divmod(n, 3)
                        act.wait_ge(kt_ps, 6 * h + (n + 1))
                        act.activation(k_tok[:, d, 3 * g:3 * g + 3, :],
                                       psum[:, n, 0:CH].rearrange("p (t n) -> p t n", t=3), ACT.Copy).then_inc(kt_ready, 1)
                    if more:
                        gates(h + 1)
                    for c in range(2):
                        act.wait_ge(mod_ps[c], h + 1)
                    act.activation(mod_rows[0:2, :].rearrange("p (j c) -> p j c", j=2), psum[0:2, 6:8, :],
                                   ACT.Copy).then_inc(mod_row, 1)
                    for g in range(3):
                        act.wait_ge(o_ps, 3 * h + (g + 1))
                        act.activation(osq[:, g * CH:(g + 1) * CH], psum[:, 5 + g, 0:CH], ACT.Square).then_inc(osq_ready, 1)
                    act.wait_ge(m_ps, h + 1)
                    act.activation(ostat[:, 0:TILES], psum[:, 0, 0:TILES], ACT.Sqrt, scale=1.0 / DK,
                                   bias=cst.eps[:, 0:1]).then_inc(std_ready, 1)

                gates(0)
                with act.Fori(0, HH - 1) as h:
                    head(h, True)
                head(HH - 1, False)

            @block.tensor
            def _(pe):
                def mod_product(h, c, k):
                    if k == 0:
                        pe.wait_ge(wm_loaded[c], 16 * h + 16)
                    mm = pe.matmul(psum[0:2, 6 + c, :], cst.cc[:, k, :], w_mod[c][:, k, :], start=(k == 0), stop=(k == KD - 1))
                    if k == KD - 1:
                        mm.then_inc(mod_ps[c], 1)

                with pe.Fori(0, HH) as h:
                    pe.wait_ge(loaded, 80 * h + 80)
                    pe.wait_ge(idle, h + 1)
                    for g in range(3):
                        if g == 2:
                            pe.wait_ge(v_ready, 3 * h + 1)
                        for x in range(3):
                            t = 3 * g + x
                            last = pe.transpose(psum[:, 6 + g % 2, x * P:(x + 1) * P], raw[:, 4, t * P:(t + 1) * P],
                                                cst.ident[:, :])
                        last.then_inc(v_ps, 1)
                    pe.wait_ge(v_ready, 3 * h + 3)
                    for k in range(3):
                        mod_product(h, 1, k)
                    pe.wait_ge(in_ready, h + 1)
                    pe.wait_ge(k_in, h + 1)
                    for lv in range(LEVELS + 1):
                        for g in range(3):
                            n = 3 * lv + g
                            if n >= 6:
                                pe.wait_ge(a_done, LU * h + (n - 5))
                            if lv >= 2:
                                pe.wait_ge(q_upd, UPD * h + (3 * (lv - 2) + g + 1))
                            if lv >= 1:
                                pe.wait_ge(kl_ready, UPD * h + (3 * (lv - 1) + g + 1))
                            for x in range(3):
                                t = 3 * g + x
                                dst = psum[:, n % 6, x * P:(x + 1) * P]
                                if lv == 0:
                                    last = pe.matmul(dst, kd[:, t * P:(t + 1) * P], q[:, t * P:(t + 1) * P],
                                                     start=True, stop=True)
                                else:
                                    b = 1 << (lv - 1)
                                    last = pe.matmul(dst.rearrange("p (n h b) -> p n h b", h=2, b=b),
                                                     k_level[lv % 2][:, t * P:(t + 1) * P], sibling_view(qd, t * P, P, b),
                                                     start=True, stop=True)
                            last.then_inc(lv_ps, 1)
                            if g == 2:
                                mod_product(h, 0, lv)
                    pe.wait_ge(k_upd, UPD * h + UPD)
                    for n in range(6):
                        d, g = divmod(n, 3)
                        pe.wait_ge(a_done, LU * h + (LU - 5 + n))
                        for x in range(3):
                            t = 3 * g + x
                            last = pe.transpose(psum[:, n, x * P:(x + 1) * P], kk[:, d, t * P:(t + 1) * P], cst.ident[:, :])
                        last.then_inc(kt_ps, 1)
                    pe.wait_ge(v_ready, 3 * h + 3)
                    for n in range(6):
                        d, g = divmod(n, 3)
                        pe.wait_ge(kt_ready, 6 * h + (n + 1))
                        for x in range(3):
                            t = 3 * g + x
                            last = pe.matmul(psum[:, n, x * P:(x + 1) * P], k_tok[:, d, t, :], v_tok[:, t, :],
                                             start=True, stop=True)
                        last.then_inc(u_ps, 1)
                    for k in range(3, KD):
                        mod_product(h, 1, k)
                    pe.wait_ge(a_done, LU * h + LU)
                    pe.wait_ge(q_upd, UPD * h + UPD)
                    pe.wait_ge(s_step, 14 * h + 14)
                    pe.wait_ge(ctx_ready, h + 1)
                    pe.wait_ge(mod_row, h + 1)
                    for g in range(3):
                        for x in range(3):
                            t = 3 * g + x
                            dst = psum[:, 5 + g, x * P:(x + 1) * P]
                            last = pe.matmul(dst, v_tok[:, t, :], scores[:, t, :], start=True, stop=(t == 8))
                            if t < 8:
                                pe.matmul(dst, state[:, 0, t, :], qd[:, 1, t * P:(t + 1) * P], start=False, stop=False)
                                last = pe.matmul(dst, state[:, 1, t, :], qd[:, 0, t * P:(t + 1) * P], start=False, stop=True)
                        last.then_inc(o_ps, 1)
                    for j in range(KD):
                        last = pe.transpose(psum[:, 4, 2 * j:2 * j + 2], mod_rows[0:2, j * P:(j + 1) * P], cst.ident[0:2, 0:2])
                    last.then_inc(modt_ps, 1)
                    pe.wait_ge(osq_ready, 3 * h + 3)
                    for t in range(TILES):
                        last = pe.matmul(psum[:, 0, t:t + 1], osq[:, t * P:(t + 1) * P], cst.ones[:, 0:1], start=True, stop=True)
                    last.then_inc(m_ps, 1)
                    pe.wait_ge(rstd_ready, h + 1)
                    for t in range(TILES):
                        last = pe.matmul(psum[:, 1 + t // 3, (t % 3) * P:(t % 3 + 1) * P],
                                         ostat[:, TILES + t:TILES + t + 1].to_broadcast([P, P]), cst.ident[:, :],
                                         start=True, stop=True)
                    last.then_inc(rb_ps, 1)

            @block.gpsimd
            def _(pool):
                with pool.Fori(0, HH) as h:
                    pool.wait_ge(f_ready, 3 * h + 2)
                    pool.tensor_tensor(kd[:, :], kk[:, 0, :], kk[:, 1, :], ALU.add).then_inc(k_in, 1)
                    pool.wait_ge(in_ready, h + 1)
                    pool.wait_ge(k_in, h + 1)
                    for lv in range(1, LEVELS + 1):
                        b = 1 << (lv - 1)
                        if lv >= 2:
                            pool.wait_ge(tot_ready, LEVELS * h + (lv - 1))
                        v = tot[lv - 1][:, :, :].rearrange("p d (n h) -> p d n h", h=2)
                        pool.tensor_tensor(tot[lv][:, :, :], v[:, :, :, 0], v[:, :, :, 1], ALU.mult).then_inc(tot_ready, 1)
                        for g in range(3):
                            pool.wait_ge(kl_ready, UPD * h + (3 * (lv - 1) + g + 1))
                            if lv >= 2:
                                pool.wait_ge(k_upd, UPD * h + (3 * (lv - 2) + g + 1))
                            lower, _ = halves(kk, 0, g, b)
                            _, of_upper = block_totals(tot[lv - 1], 0, g, b)
                            pool.tensor_tensor(lower, lower, of_upper, ALU.mult)
                            _, upper = halves(kk, 1, g, b)
                            of_lower, _ = block_totals(tot[lv - 1], 1, g, b)
                            pool.tensor_tensor(upper, upper, of_lower, ALU.mult).then_inc(k_upd, 1)

            @block.vector
            def _(dve):
                dve.wait_ge(masks_loaded, 16)
                dve.memset(hv[:, :], 0.0).then_inc(idle, 1)
                dve.wait_ge(idle, 1)

                def inputs(h):
                    dve.tensor_copy(hv[:, 0:2], cst.lb[:, :].rearrange("p (d h) -> p h d", d=2)[:, bass.ds(h, 1), :])
                    dve.tensor_copy(hv[:, 2:4], cst.lb1[:, :].rearrange("p (d h) -> p h d", d=2)[:, bass.ds(h, 1), :])
                    dve.tensor_copy(hv[:, 4:5], cst.cols_a[:, bass.ds(h + AT_A["g_hg"], 1)]).then_inc(vec_ready, 1)
                    dve.wait_ge(vec_ready, h + 1)
                    dve.wait_ge(sig_ready, 2 * h + 1)
                    for d in range(2):
                        last = dve.tensor_scalar(tot[0][:, d, :], tot[0][:, d, :], hv[:, 2 + d:3 + d], hv[:, d:d + 1],
                                                 ALU.mult, ALU.add)
                    last.then_inc(f_ready, 1)
                    dve.wait_ge(f_ready, 3 * h + 1)
                    dve.tensor_scalar(kk[:, :, :], tot[0][:, :, :], -1.0, 1.0, ALU.mult, ALU.add).then_inc(f_ready, 1)
                    dve.wait_ge(sig_ready, 2 * h + 2)
                    dve.tensor_tensor(q[:, :], sig[:, 0, :], raw[:, 2, :], ALU.mult).then_inc(f_ready, 1)

                def head(h, more):
                    dve.wait_ge(idle, h + 1)
                    dve.wait_ge(sig_ready, 2 * h + 2)
                    dve.wait_ge(f_ready, 3 * h + 3)
                    dve.tensor_tensor(qd[:, 0, :], q[:, :], tot[0][:, 1, :], ALU.mult)
                    dve.tensor_tensor(qd[:, 1, :], q[:, :], tot[0][:, 0, :], ALU.mult).then_inc(in_ready, 1)
                    dve.scalar_tensor_tensor(gate[:, :], raw[:, 3, :], hv[:, 4:5], sig[:, 1, :],
                                             ALU.mult, ALU.mult).then_inc(gate_ready, 1)
                    dve.wait_ge(in_ready, h + 1)
                    for lv in range(LEVELS + 1):
                        b = 1 << max(lv - 1, 0)
                        if lv >= 2:
                            dve.wait_ge(tot_ready, LEVELS * h + (lv - 1))
                        for g in range(3):
                            n = 3 * lv + g
                            dve.wait_ge(lv_ps, LU * h + (n + 1))
                            taken = psum[:, n % 6, 0:CH].rearrange("p (t n) -> p t n", t=3)
                            if lv == 0:
                                dve.tensor_copy(scores[:, 3 * g:3 * g + 3, :], taken).then_inc(a_done, 1)
                                continue
                            if lv >= 2:
                                dve.wait_ge(q_upd, UPD * h + (3 * (lv - 2) + g + 1))
                            dve.wait_ge(a_done, LU * h + (n - 2))
                            lower, _ = halves(qd, 0, g, b)
                            _, of_upper = block_totals(tot[lv - 1], 1, g, b)
                            dve.tensor_tensor(lower, lower, of_upper, ALU.mult)
                            _, upper = halves(qd, 1, g, b)
                            of_lower, _ = block_totals(tot[lv - 1], 0, g, b)
                            dve.tensor_tensor(upper, upper, of_lower, ALU.mult).then_inc(q_upd, 1)
                            dve.copy_predicated(scores[:, 3 * g:3 * g + 3, :],
                                                masks[:, lv:lv + 1, :].to_broadcast([P, 3, P]), taken).then_inc(a_done, 1)
                    dve.wait_ge(state_loaded, 32 * h + 32)
                    dve.wait_ge(tot_ready, LEVELS * h + LEVELS)
                    dve.wait_ge(u_ps, 6 * h + 6)
                    for n in range(14):
                        c, d = divmod(n, 2)
                        src, dst = (c, c + 1) if d == 0 else (7 - c, 6 - c)
                        if n >= 2:
                            dve.wait_ge(s_step, 14 * h + (n - 1))
                        dve.scalar_tensor_tensor(state[:, d, dst, :], state[:, d, src, :], tot[LEVELS][:, d, src:src + 1],
                                                 psum[:, 3 * d + src // 3, (src % 3) * P:(src % 3 + 1) * P],
                                                 ALU.mult, ALU.add).then_inc(s_step, 1)
                    dve.tensor_copy(ctx_state[:, 0, :], psum[:, 2, 2 * P:3 * P])
                    dve.tensor_copy(ctx_state[:, 1, :], psum[:, 5, 2 * P:3 * P]).then_inc(ctx_ready, 1)
                    if more:
                        inputs(h + 1)
                    dve.wait_ge(modt_ps, h + 1)
                    dve.tensor_tensor(cst.mod[:, bass.ds(8 * h + 2 * KD, KD), :],
                                      psum[:, 4, 0:2 * KD].rearrange("p (j g) -> p j g", g=2),
                                      cst.cols_a[:, bass.ds(8 * h + 2 * KD, KD)].unsqueeze(2).to_broadcast([P, KD, 2]),
                                      ALU.add).then_inc(mod_ready, 1)
                    dve.wait_ge(gate_ready, h + 1)
                    dve.wait_ge(osq_ready, 3 * h + 3)
                    dve.tensor_tensor(tok3(gated[:, :]), psum[:, 5:8, 0:CH], tok3(gate[:, :]), ALU.mult).then_inc(gated_ready, 1)
                    dve.wait_ge(std_ready, h + 1)
                    dve.reciprocal(ostat[:, TILES:2 * TILES], ostat[:, 0:TILES]).then_inc(rstd_ready, 1)
                    dve.wait_ge(gated_ready, h + 1)
                    dve.wait_ge(rb_ps, h + 1)
                    dve.tensor_tensor(tok3(out[:, :]), psum[:, 1:4, 0:CH], tok3(gated[:, :]), ALU.mult).then_inc(idle, 1)

                inputs(0)
                with dve.Fori(0, HH - 1) as h:
                    head(h, True)
                head(HH - 1, False)
                dve.wait_ge(mod_ready, HH)
                make_gain(dve, cst, cst.gain_ffn, 4 * KD, "g_ffn", gain_done)


def stage_merge(nc, io, cst, arena, m_hi, m_lo):
    with ExitStack() as ctx:
        sems = Signals(nc, ctx, "s6")
        o_hi, o_lo = arena("o_hi", [P, KD, NT], F32R), arena("o_lo", [P, KD, NT], F32R)
        w = WeightStream(nc, arena, sems, "s6")
        gates = [arena(f"merge_gates{i}", [P, 2, NT]) for i in range(2)]
        y = [arena(f"merge_y{i}", [P, NT]) for i in range(2)]
        o_f32 = [y[0][:, :], y[1][:, :], gates[1][:, 0, :], gates[1][:, 1, :]]
        psum = [ctx.enter_context(nc.psum_tensor(f"s6_psum{i}", [P, 4, 512], F32)) for i in range(2)]
        o_loaded = [sems(f"o_loaded{i}") for i in range(4)]
        g_loaded = [sems(f"g_loaded{i}") for i in range(2)]
        o_hi_ready, o_lo_ready = sems("o_hi_ready"), sems("o_lo_ready")
        g_ready, a_read, b_read = sems("gates_ready"), sems("a_read"), sems("b_read")
        y_ready, hi_ready, lo_ready = sems("y_ready"), sems("hi_ready"), sems("lo_ready")
        half_ps = sems("mla_product")
        mla = io["w_mla_o"].rearrange("(k p) n -> p k n", p=P)
        hg = io["w_hg_o"].rearrange("(k p) n -> p k n", p=P)

        with nc.Block() as block:
            @block.sync
            def _(sp):
                def load(c, s, free):
                    w.load(sp, c, s, [(w.raw[s][:, 0:4, :], mla[:, :, bass.ds(c * P, P)]),
                                      (w.raw[s][:, 4:8, :], hg[:, :, bass.ds(c * P, P)])], free)
                    if free:
                        sp.wait_ge(b_read, c - 1)
                    load_gates(c, s)

                def load_gates(c, s):
                    for n, chunk in enumerate((20, 28)):
                        sp.dma_start(gates[s][:, n, :], io["proj"][bass.ds((c + chunk) * P, P), :]).then_inc(g_loaded[s], 16)

                w.load(sp, 0, 0, [(w.raw[0][:, 0:4, :], mla[:, :, 0:P]), (w.raw[0][:, 4:8, :], hg[:, :, 0:P])], False)
                for k in range(KD):
                    if k >= 4:
                        sp.wait_ge(o_lo_ready, k - 3)
                    src = io["o_mla"][k * P:(k + 1) * P, :] if k < 4 else io["o_hg"][(k - 4) * P:(k - 3) * P, :]
                    sp.dma_start(o_f32[k % 4], src).then_inc(o_loaded[k % 4], 16)
                load_gates(0, 0)
                sp.wait_ge(o_lo_ready, KD)
                load(1, 1, False)
                with sp.Fori(1, KD // 2) as i:
                    for s in range(2):
                        load(2 * i + s, s, True)

            @block.scalar
            def _(act):
                def chunk(c, s, uses, free):
                    w.split_hi(act, s, 32 * uses, c, free)
                    act.wait_ge(g_loaded[s], 32 * uses)
                    act.activation(gates[s][:, :, :], gates[s][:, :, :], ACT.Sigmoid).then_inc(g_ready, 1)

                def split(c):
                    act.wait_ge(y_ready, c + 1)
                    act.activation(m_hi[:, bass.ds(c, 1), :].rearrange("p a n -> p (a n)"), y[1][:, :], ACT.Copy).then_inc(hi_ready, 1)

                w.split_hi(act, 0, 32, 0, False)
                for k in range(KD):
                    act.wait_ge(o_loaded[k % 4], 16 * (k // 4 + 1))
                    act.activation(o_hi[:, k, :], o_f32[k % 4], ACT.Copy).then_inc(o_hi_ready, 1)
                act.wait_ge(g_loaded[0], 32)
                act.activation(gates[0][:, :, :], gates[0][:, :, :], ACT.Sigmoid).then_inc(g_ready, 1)
                chunk(1, 1, 1, False)
                with act.Fori(1, KD // 2) as i:
                    for s in range(2):
                        split(2 * i + (s - 2))
                        chunk(2 * i + s, s, i + 1, True)
                split(KD - 2)
                split(KD - 1)

            @block.gpsimd
            def _(pool):
                def split(c):
                    pool.wait_ge(hi_ready, c + 1)
                    pool.tensor_tensor(m_lo[:, bass.ds(c, 1), :].rearrange("p a n -> p (a n)"), y[1][:, :],
                                       m_hi[:, bass.ds(c, 1), :].rearrange("p a n -> p (a n)"), ALU.subtract).then_inc(lo_ready, 1)

                w.split_lo(pool, 0, 0)
                w.split_lo(pool, 1, 1)
                with pool.Fori(1, KD // 2) as i:
                    for s in range(2):
                        split(2 * i + (s - 2))
                        w.split_lo(pool, s, 2 * i + s)
                split(KD - 2)
                split(KD - 1)

            @block.tensor
            def _(pe):
                def chunk(c, s, first):
                    before = (lambda k: pe.wait_ge(o_lo_ready, k + 1)) if first else None
                    parts = [lambda k: w.hi[s][:, k, :], lambda k: w.lo[s][:, k, :],
                             lambda k: o_hi[:, k, :], lambda k: o_lo[:, k, :]]
                    pe.wait_ge(w.lo_ready, c + 1)
                    if not first:
                        pe.wait_ge(a_read, c)
                    gemm_chunk(pe, psum[0], *parts, [(k, k) for k in range(4)], before).then_inc(half_ps, 1)
                    if not first:
                        pe.wait_ge(b_read, c)
                    gemm_chunk(pe, psum[1], *parts, [(k, k) for k in range(4, KD)], before).then_inc(w.used, 1)

                chunk(0, 0, True)
                chunk(1, 1, False)
                with pe.Fori(1, KD // 2) as i:
                    for s in range(2):
                        chunk(2 * i + s, s, False)

            @block.vector
            def _(dve):
                for k in range(KD):
                    dve.wait_ge(o_hi_ready, k + 1)
                    dve.tensor_tensor(o_lo[:, k, :], o_f32[k % 4], o_hi[:, k, :], ALU.subtract).then_inc(o_lo_ready, 1)
                dve.wait_ge(o_lo_ready, KD)

                def chunk(c, s, first):
                    dve.wait_ge(half_ps, c + 1)
                    dve.wait_ge(g_ready, c + 1)
                    dve.tensor_tensor(tok3(y[0][:, :]), psum[0][:, 0:NCH, 0:CH], tok3(gates[s][:, 0, :]), ALU.mult).then_inc(a_read, 1)
                    dve.wait_ge(w.used, c + 1)
                    if not first:
                        dve.wait_ge(lo_ready, c)
                    dve.tensor_tensor(tok3(y[1][:, :]), psum[1][:, 0:NCH, 0:CH], tok3(gates[s][:, 1, :]), ALU.mult).then_inc(b_read, 1)
                    dve.wait_ge(b_read, c + 1)
                    dve.wait_ge(a_read, c + 1)
                    dve.tensor_tensor(y[1][:, :], y[1][:, :], y[0][:, :], ALU.add).then_inc(y_ready, 1)
                    dve.wait_ge(y_ready, c + 1)

                chunk(0, 0, True)
                chunk(1, 1, False)
                with dve.Fori(1, KD // 2) as i:
                    for s in range(2):
                        chunk(2 * i + s, s, False)


def add_scaled(dve, x, psum, gate):
    v = tok3(x)
    dve.scalar_tensor_tensor(v[:, 0:2, :], psum[:, 0:2, 0:CH], gate[:, 0:1], v[:, 0:2, :], ALU.mult, ALU.add)
    cut = TL - 2 * CH
    dve.scalar_tensor_tensor(v[:, 2, 0:cut], psum[:, 2, 0:cut], gate[:, 0:1], v[:, 2, 0:cut], ALU.mult, ALU.add)
    return dve.scalar_tensor_tensor(v[:, 2, cut:CH], psum[:, 2, cut:CH], gate[:, 1:2], v[:, 2, cut:CH], ALU.mult, ALU.add)


def stage_out_projection(nc, io, cst, arena, m_hi, m_lo, x_t, rb):
    with ExitStack() as ctx:
        sems = Signals(nc, ctx, "s7")
        w = WeightStream(nc, arena, sems, "s7")
        norm = Norm(arena, sems, "n2", cst, KD, D, rb)
        psum = [ctx.enter_context(nc.psum_tensor(f"s7_psum{i}", [P, 4, 512], F32)) for i in range(2)]
        x_loaded, added = sems("x_loaded"), sems("added")
        wo = io["w_out"].rearrange("(k p) n -> p k n", p=P)
        with nc.Block() as block:
            @block.sync
            def _(sp):
                for s in range(2):
                    w.load(sp, s, s, [(w.raw[s][:, :, :], wo[:, :, s * P:(s + 1) * P])], False)
                sp.dma_start(x_t[:, :, :], io["x_t"].rearrange("(k p) n -> p k n", p=P)).then_inc(x_loaded, 16)
                with sp.Fori(1, KD // 2) as i:
                    for s in range(2):
                        c = 2 * i + s
                        w.load(sp, c, s, [(w.raw[s][:, :, :], wo[:, :, bass.ds(c * P, P)])])

            @block.scalar
            def _(act):
                for s in range(2):
                    w.split_hi(act, s, 16, s, False)
                with act.Fori(1, KD // 2) as i:
                    for s in range(2):
                        w.split_hi(act, s, 16 * i + 16, 2 * i + s)
                for k in range(KD):
                    act.wait_ge(added, k + 1)
                    norm.act_square(act, k, x_t[:, k, :])
                norm.act_std(act, psum[0][:, 3, :])
                norm.act_broadcast(act, psum[0])

            @block.gpsimd
            def _(pool):
                with pool.Fori(0, KD // 2) as i:
                    for s in range(2):
                        w.split_lo(pool, s, 2 * i + s)

            @block.tensor
            def _(pe):
                def chunk(c, s, free):
                    pe.wait_ge(w.lo_ready, c + 1)
                    if free:
                        pe.wait_ge(added, c - 1)
                    gemm_chunk(pe, psum[s], lambda k: w.hi[s][:, k, :], lambda k: w.lo[s][:, k, :],
                               lambda k: m_hi[:, k, :], lambda k: m_lo[:, k, :],
                               [(k, k) for k in range(KD)]).then_inc(w.used, 1)
                for s in range(2):
                    chunk(s, s, False)
                with pe.Fori(1, KD // 2) as i:
                    for s in range(2):
                        chunk(2 * i + s, s, True)
                norm.pe_sums(pe, psum[0][:, 3, :])
                norm.pe_broadcast(pe, psum[0])

            @block.vector
            def _(dve):
                dve.wait_ge(x_loaded, 16)
                for c in range(KD):
                    if c == KD - 1:
                        for k in range(KD - 1):
                            norm.dve_add(dve, k)
                    dve.wait_ge(w.used, c + 1)
                    add_scaled(dve, x_t[:, c, :], psum[c % 2], cst.mod[:, 2 * KD + c, :]).then_inc(added, 1)
                norm.dve_add(dve, KD - 1)
                norm.dve_rstd(dve)


PAIRS = DFF // P // 2
PAD = NT + 4
LAT0, CTX0 = 1, TL + 3


def stage_ffn(nc, io, cst, arena, over_h, rb, h_hi, h_lo, x_t):
    with ExitStack() as ctx:
        sems = Signals(nc, ctx, "s9")
        app = Apply(Arena(nc, arena.at + NT * 4), sems, "a2", rb)
        u = arena("u_f32", [P, NT])
        u_hi = arena("u_hi", [P, 2, NT], F32R)
        w = WeightStream(nc, arena, sems, "s9")
        gpad = [arena(f"gate_pad{i}", [P, PAD]) for i in range(2)]
        conv = [arena(f"conv{i}", [P, PAD]) for i in range(2)]
        u_lo = arena("u_lo", [P, 2, NT], F32R)
        taps = arena("taps", [P, 2, 4])
        psum = [ctx.enter_context(nc.psum_tensor(f"s9_psum{i}", [P, 4, 512], F32)) for i in range(2)]
        padded, taps_ready = sems("padded"), sems("taps_ready")
        y_ps = sems("out_product")
        g_read, v_read, y_read = sems("gate_read"), sems("value_read"), sems("out_added")
        conv_step, gelu_ready = sems("conv_step"), sems("gelu_ready")
        u_hi_ready, u_lo_ready = sems("u_hi_ready"), sems("u_lo_ready")
        norm = Norm(over_h, sems, "n3", cst, KD, D)
        rows = [over_h(f"final_rows{i}", [P, D]) for i in range(3)]
        scaled, y_t, row_ready = sems("scaled"), sems("y_transposed"), [sems(f"row_ready{i}") for i in range(2)]
        stored = [sems(f"stored{i}") for i in range(3)]
        ROUNDS = 2 * TILES

        def round_bank(r):
            return psum[r % 2][:, (r // 2) % 3, :]

        win = io["w_ffn_in"].rearrange("(k p) n -> p k n", p=P)
        wout = io["w_ffn_out"].rearrange("(k p) n -> p k n", p=P)
        cut = TL - 2 * CH

        def out_view(t, m):
            return t[:, :, :].rearrange("p k n -> p (k n)").rearrange("p (k n) -> p k n", k=2)[:, :, (m % 4) * P:(m % 4 + 1) * P]

        def pieces(padded_t, bank):
            return [(padded_t[:, LAT0:LAT0 + 2 * CH].rearrange("p (j c) -> p j c", j=2), bank[:, 0:2, 0:CH]),
                    (padded_t[:, LAT0 + 2 * CH:LAT0 + TL], bank[:, 2, 0:cut]),
                    (padded_t[:, CTX0:CTX0 + TC], bank[:, 2, cut:CH])]

        def all_chunks(engine, one):
            for n, (kind, x) in enumerate((("g", 0), ("g", 1), ("v", 0), ("v", 1))):
                one(n, n % 2, kind, x, 0)
            with engine.Fori(1, PAIRS) as g:
                for n, (kind, x) in enumerate((("g", 0), ("o", 0), ("o", 1), ("g", 1), ("v", 0), ("v", 1))):
                    one(6 * g + (n - 2), n % 2, kind, x, g)
            for n, x in enumerate((0, 1)):
                one(6 * PAIRS - 2 + n, n % 2, "o", x, PAIRS)

        def evacuate(engine, half):
            engine.wait_ge(norm.rstd_ready, 1)
            for t in range(TILES):
                engine.wait_ge(y_t, 2 * t + half + 1)
                if t >= 3:
                    engine.wait_ge(stored[t % 3], 16 * (t // 3))
                dst, src = rows[t % 3][:, 4 * half * P:4 * (half + 1) * P], round_bank(2 * t + half)
                factor = norm.stat[:, TILES + t:TILES + t + 1]
                if half:
                    last = engine.activation(dst, src, ACT.Copy, scale=factor)
                else:
                    last = engine.tensor_scalar(dst, src, factor, None, ALU.mult)
                last.then_inc(row_ready[half], 1)

        with nc.Block() as block:
            @block.sync
            def _(sp):
                def one(c, s, kind, x, g):
                    raw = w.raw[s]
                    free = not (isinstance(c, int) and c < 2)
                    if kind == "o":
                        dst = raw[:, :, :].rearrange("p k n -> p (k n)").rearrange("p (k n) -> p k n", k=2)
                        rows = wout[:, bass.ds(2 * (g - 1), 2), x * 512:(x + 1) * 512]
                        w.load(sp, c, s, [(dst, rows)], free)
                    else:
                        at = (0 if kind == "g" else DFF) + x * P
                        w.load(sp, c, s, [(raw[:, :, :], win[:, :, bass.ds(2 * P * g + at, P)])], free)
                all_chunks(sp, one)
                for t in range(TILES):
                    dst = io["y_prompt"] if t == TILES - 1 else io["y_sample"][t * P:(t + 1) * P, :]
                    for half in range(2):
                        sp.wait_ge(row_ready[half], t + 1)
                    sp.dma_start(dst, rows[t % 3][:, :]).then_inc(stored[t % 3], 16)
                for i in range(3):
                    sp.wait_ge(stored[i], 16 * TILES // 3)

            @block.scalar
            def _(act):
                act.wait_ge(padded, 1)

                def weights(c, s):
                    free = not (isinstance(c, int) and c < 2)
                    w.split_hi(act, s, 8 * (c - s) + 16, c, free)

                def gate(g, x, used):
                    act.wait_ge(w.used, used)
                    bank = psum[0] if x == 0 else psum[1]
                    for dst, src in pieces(gpad[x], bank):
                        last = act.activation(dst, src, ACT.Copy)
                    last.then_inc(g_read, 1)

                def gelu(g, x):
                    act.wait_ge(conv_step, 6 * g + 3 * x + 3)
                    act.activation(conv[x][:, 1:PAD - 1], conv[x][:, 1:PAD - 1], ACT.Gelu_apprx_tanh).then_inc(gelu_ready, 1)

                def split(g, x):
                    act.wait_ge(v_read, 2 * g + (x + 1))
                    act.activation(u_hi[:, x, :], u[:, :], ACT.Copy).then_inc(u_hi_ready, 1)

                weights(0, 0)
                for k in range(KD):
                    app.act(act, k, [(h_hi[:, k, :], 0, NT)])
                    if k == 3:
                        weights(1, 1)
                gate(0, 0, 1)
                weights(2, 0)
                gelu(0, 0)
                gate(0, 1, 2)
                weights(3, 1)
                gelu(0, 1)
                with act.Fori(1, PAIRS) as g:
                    c = 6 * g - 2
                    weights(c, 0)
                    split(g - 1, 0)
                    weights(c + 1, 1)
                    split(g - 1, 1)
                    gate(g, 0, c + 1)
                    weights(c + 2, 0)
                    gelu(g, 0)
                    weights(c + 3, 1)
                    weights(c + 4, 0)
                    gate(g, 1, c + 4)
                    weights(c + 5, 1)
                    gelu(g, 1)
                c = 6 * PAIRS - 2
                weights(c, 0)
                split(PAIRS - 1, 0)
                weights(c + 1, 1)
                split(PAIRS - 1, 1)
                for m in range(KD):
                    act.wait_ge(y_read, 8 * (PAIRS - 1) + m + 1)
                    norm.act_square(act, m, x_t[:, m, :])
                    act.wait_ge(norm.sq_ready, m + 1)
                    act.activation(x_t[:, m, :], x_t[:, m, :], ACT.Copy, scale=cst.a("g_final", m)).then_inc(scaled, 1)
                norm.act_std(act, psum[0][:, 3, :])
                evacuate(act, 1)

            @block.gpsimd
            def _(pool):
                def split(g, x):
                    pool.wait_ge(u_hi_ready, 2 * g + (x + 1))
                    pool.tensor_tensor(u_lo[:, x, :], u[:, :], u_hi[:, x, :], ALU.subtract).then_inc(u_lo_ready, 1)

                for x in range(2):
                    pool.memset(gpad[x][:, :], 0.0)
                pool.memset(conv[0][:, 0:1], 0.0).then_inc(padded, 1)
                w.split_lo(pool, 0, 0)
                for k in range(KD):
                    app.pool(pool, k, [(h_lo[:, k, :], h_hi[:, k, :], 0, NT)])
                w.split_lo(pool, 1, 1)
                w.split_lo(pool, 0, 2)
                w.split_lo(pool, 1, 3)
                with pool.Fori(1, PAIRS) as g:
                    c = 6 * g - 2
                    w.split_lo(pool, 0, c)
                    split(g - 1, 0)
                    w.split_lo(pool, 1, c + 1)
                    split(g - 1, 1)
                    for n in range(2, 6):
                        w.split_lo(pool, n % 2, c + n)
                c = 6 * PAIRS - 2
                w.split_lo(pool, 0, c)
                split(PAIRS - 1, 0)
                w.split_lo(pool, 1, c + 1)
                split(PAIRS - 1, 1)
                for k in range(KD):
                    norm.dve_add(pool, k)

            @block.tensor
            def _(pe):
                def h_product(c, s, bank, before=None):
                    pe.wait_ge(w.lo_ready, c + 1)
                    return gemm_chunk(pe, bank, lambda k: w.hi[s][:, k, :], lambda k: w.lo[s][:, k, :],
                                      lambda k: h_hi[:, k, :], lambda k: h_lo[:, k, :], [(k, k) for k in range(KD)], before)

                def h_tile(c, s, bank):
                    h_product(c, s, bank).then_inc(w.used, 1)

                def outs(c, s, x, g, last):
                    pe.wait_ge(w.lo_ready, c + 1)
                    pe.wait_ge(u_lo_ready, 2 * g)
                    for m in range(4 * x, 4 * x + 4):
                        if m == 0 or (m == 1 and last):
                            pe.wait_ge(v_read, 2 * g)
                        elif m == 1:
                            pe.wait_ge(g_read, 2 * g + 1)
                        else:
                            pe.wait_ge(y_read, 8 * (g - 1) + (m - 1))
                        mm = gemm_chunk(pe, psum[(m + 1) % 2], lambda k: out_view(w.hi[s], m)[:, k, :],
                                        lambda k: out_view(w.lo[s], m)[:, k, :],
                                        lambda k: u_hi[:, k, :], lambda k: u_lo[:, k, :], [(0, 0), (1, 1)])
                        mm.then_inc(w.used if m % 4 == 3 else y_ps, 1)

                h_product(0, 0, psum[0], lambda k: pe.wait_ge(app.lo_ready, k + 1)).then_inc(w.used, 1)
                h_tile(1, 1, psum[1])
                pe.wait_ge(g_read, 1)
                h_tile(2, 0, psum[0])
                pe.wait_ge(g_read, 2)
                h_tile(3, 1, psum[1])
                with pe.Fori(1, PAIRS) as g:
                    c = 6 * g - 2
                    pe.wait_ge(v_read, 2 * g - 1)
                    h_tile(c, 0, psum[0])
                    outs(c + 1, 1, 0, g, False)
                    outs(c + 2, 0, 1, g, False)
                    pe.wait_ge(y_read, 8 * g - 1)
                    h_tile(c + 3, 1, psum[1])
                    pe.wait_ge(y_read, 8 * g)
                    h_tile(c + 4, 0, psum[0])
                    pe.wait_ge(g_read, 2 * g + 2)
                    h_tile(c + 5, 1, psum[1])
                c = 6 * PAIRS - 2
                outs(c, 0, 0, PAIRS, True)
                outs(c + 1, 1, 1, PAIRS, True)

                def transposes(r):
                    t, half = r // 2, r % 2
                    pe.wait_ge(scaled, 4 * half + 4)
                    if r < 6:
                        pe.wait_ge(y_read, 8 * PAIRS)
                    else:
                        pe.wait_ge(row_ready[r % 2], r // 2 - 2)
                    for k in range(4):
                        last = pe.transpose(round_bank(r)[:, k * P:(k + 1) * P],
                                            x_t[:, 4 * half + k, t * P:(t + 1) * P], cst.ident[:, :])
                    last.then_inc(y_t, 1)

                for r in range(5):
                    transposes(r)
                norm.pe_sums(pe, psum[0][:, 3, :])
                for r in range(5, ROUNDS):
                    transposes(r)

            @block.vector
            def _(dve):
                def conv_gate(g, x):
                    n = 2 * g + x
                    dve.tensor_copy(taps[:, x, 0:3],
                                    cst.cols_b[:, AT_B["conv_w"]:AT_B["conv_w"] + 66].rearrange("p (j m) -> p j m", j=3)
                                    [:, :, bass.ds(n, 1)].rearrange("p j a -> p (j a)"))
                    dve.tensor_copy(taps[:, x, 3:4], cst.cols_a[:, bass.ds(n + AT_A["conv_b"], 1)]).then_inc(taps_ready, 1)
                    dve.wait_ge(taps_ready, n + 1)
                    dve.wait_ge(g_read, n + 1)
                    out = conv[x][:, 1:PAD - 1]
                    dve.tensor_scalar(out, gpad[x][:, 1:PAD - 1], taps[:, x, 1:2], taps[:, x, 3:4],
                                      ALU.mult, ALU.add).then_inc(conv_step, 1)
                    for j, first in ((0, 0), (2, 2)):
                        dve.wait_ge(conv_step, 3 * n + (1 + j // 2))
                        dve.scalar_tensor_tensor(out, gpad[x][:, first:first + PAD - 2], taps[:, x, j:j + 1], out,
                                                 ALU.mult, ALU.add).then_inc(conv_step, 1)

                def value(g, x, used):
                    dve.wait_ge(w.used, used)
                    dve.wait_ge(gelu_ready, 2 * g + (x + 1))
                    dve.wait_ge(u_lo_ready, 2 * g + x)
                    flat = tok3(u[:, :])
                    outs = [flat[:, 0:2, :], flat[:, 2, 0:cut], flat[:, 2, cut:CH]]
                    for dst, (a, b) in zip(outs, pieces(conv[x], psum[x])):
                        last = dve.tensor_tensor(dst, b, a, ALU.mult)
                    last.then_inc(v_read, 1)
                    dve.wait_ge(v_read, 2 * g + (x + 1))

                def adds(g, chunk0, chunk1):
                    for m in range(KD):
                        if m % 4 == 3:
                            dve.wait_ge(w.used, (chunk0 if m == 3 else chunk1) + 1)
                        else:
                            dve.wait_ge(y_ps, 6 * (g - 1) + (3 * (m // 4) + m % 4 + 1))
                        if m:
                            dve.wait_ge(y_read, 8 * (g - 1) + m)
                        add_scaled(dve, x_t[:, m, :], psum[(m + 1) % 2], cst.mod[:, 5 * KD + m, :]).then_inc(y_read, 1)

                for k in range(KD):
                    app.dve(dve, k, x_t[:, k, :], [(a, b, cst.gain_ffn[:, k, g:g + 1], cst.mod[:, 3 * KD + k, g:g + 1])
                                                   for g, (a, b) in enumerate(GROUPS)])
                conv_gate(0, 0)
                conv_gate(0, 1)
                value(0, 0, 3)
                value(0, 1, 4)
                with dve.Fori(1, PAIRS) as g:
                    c = 6 * g - 2
                    conv_gate(g, 0)
                    adds(g, c + 1, c + 2)
                    conv_gate(g, 1)
                    value(g, 0, c + 5)
                    value(g, 1, c + 6)
                c = 6 * PAIRS - 2
                adds(PAIRS, c, c + 1)
                norm.dve_rstd(dve)
                evacuate(dve, 0)


LOW = 16512


def program(nc, io):
    persistent = Arena(nc, LOW)
    cst = Constants(persistent)
    base = persistent.at
    arena = Arena(nc, base)
    h_hi, h_lo = arena("h_hi", [P, KD, NT], F32R), arena("h_lo", [P, KD, NT], F32R)
    x_first, rb = arena("x_first", [P, KD, NT]), arena("rb_first", [P, NT])
    stage_setup(nc, io, cst, Arena(nc, base), x_first, rb)
    over_x = Arena(nc, base + 2 * KD * NT * 4)
    pqkv, pkr = over_x("pqkv", [P, 5, NT]), over_x("pkr", [P, NT])
    after_pkr = over_x.at
    to_dram = [over_x(f"stage{s}", [P, NT]) for s in range(2)]
    stage_in_projection(nc, io, cst, arena, to_dram, x_first, rb, h_hi, h_lo, pqkv, pkr)
    low = Arena(nc, base)
    qn_hi, qn_lo = low("qn_hi", [P, 3, NT], F32R), low("qn_lo", [P, 3, NT], F32R)
    c_hi, c_lo = low("ckv_hi", [P, 2, NK], F32R), low("ckv_lo", [P, 2, NK], F32R)
    k_hi = [low(f"k_hi{e}", [P, NK], F32R) for e in range(2)]
    k_lo = [low(f"k_lo{e}", [P, NK], F32R) for e in range(2)]
    rope = low("rope", [P, NT])
    assert low.at <= base + 2 * KD * NT * 4
    stage_low_rank(nc, io, cst, Arena(nc, after_pkr), pqkv, pkr, rope, qn_hi, qn_lo, c_hi, c_lo, k_hi, k_lo)
    stage_attention(nc, io, cst, low, rope, qn_hi, qn_lo, c_hi, c_lo, k_hi, k_lo)
    stage_hgrn(nc, io, cst, Arena(nc, base))
    half = 2 * KD * NT * 4
    mix = Arena(nc, base)
    m_hi, m_lo = mix("m_hi", [P, KD, NT], F32R), mix("m_lo", [P, KD, NT], F32R)
    stage_merge(nc, io, cst, Arena(nc, base + half), m_hi, m_lo)
    rest = Arena(nc, base + half)
    x_t = rest("x_res", [P, KD, NT])
    after_x = rest.at
    rb = rest("rb_second", [P, NT])
    stage_out_projection(nc, io, cst, Arena(nc, rest.at), m_hi, m_lo, x_t, rb)
    again = Arena(nc, base)
    h2_hi, h2_lo = again("h2_hi", [P, KD, NT], F32R), again("h2_lo", [P, KD, NT], F32R)
    stage_ffn(nc, io, cst, Arena(nc, after_x), Arena(nc, base), rb, h2_hi, h2_lo, x_t)


def constants():
    ident = np.eye(P, dtype=np.float32)
    s, t = np.meshgrid(np.arange(P), np.arange(P), indexing="ij")
    masks = [s == t]
    for level in range(LEVELS):
        b = 1 << level
        masks.append((s // (2 * b) == t // (2 * b)) & (s // b != t // b))
    masks = np.stack(masks, 1).astype(np.int32)
    n_freq = ROPE // 4
    inv = np.power(np.float32(10000.0), -np.arange(n_freq, dtype=np.float32) / np.float32(n_freq)).astype(np.float32)
    tok = np.arange(TL)
    ang = np.concatenate([(tok // GRID_W)[:, None].astype(np.float32) * inv,
                          (tok % GRID_W)[:, None].astype(np.float32) * inv], -1)
    ang = np.concatenate([ang, ang], -1).astype(np.float32).T
    rope = np.zeros((2 * ROPE, NT), np.float32)
    rope[:ROPE, :TL], rope[ROPE:, :TL] = np.cos(ang), np.sin(ang)
    rope[:ROPE, TL:] = 1.0
    return {"ident": ident, "masks": masks, "rope": rope}


INPUTS = ["x_prompt", "x_sample", "cache_ckv", "cache_krope", "state_hgrn_fwd", "state_hgrn_bwd", "c", "c_ctx",
          "w_mod", "b_mod", "g_mix", "w_in", "g_q", "w_uq", "g_kv", "w_ukv", "w_mla_o", "lb_param", "g_hg",
          "w_hg_o", "w_out", "g_ffn", "w_ffn_in", "conv_w", "conv_b", "w_ffn_out", "g_final"]
ROW_VECTORS = ("b_mod", "g_mix", "g_ffn", "g_final", "conv_b", "g_q", "g_kv", "g_hg", "lb_param", "conv_w", "c", "c_ctx")
MATRICES = ("w_mod", "w_in", "w_uq", "w_ukv", "w_mla_o", "w_hg_o", "w_out", "w_ffn_in", "w_ffn_out")
OUTPUTS = [("y_prompt", (1, TC, D)), ("y_sample", (1, TL, D)), ("new_ckv", (1, 1, TC, KVL)),
           ("new_krope", (1, 1, TC, ROPE)), ("new_state_fwd", (1, 1, HH, DK, DK)),
           ("new_state_bwd", (1, 1, HH, DK, DK))]


def layout(inputs):
    arrays = {}
    for name in INPUTS:
        a = np.ascontiguousarray(inputs[name])
        if name in ROW_VECTORS:
            a = a.reshape(-1, P)
        elif name in MATRICES:
            a = a.reshape(a.shape[-2], a.shape[-1])
        elif name in ("state_hgrn_fwd", "state_hgrn_bwd"):
            a = a.reshape(HH * DK, DK)
        else:
            a = a.reshape(-1, a.shape[-1])
        arrays[name] = a
    arrays.update(constants())
    return arrays


def build(nc, arrays):
    io = {}
    for name, a in arrays.items():
        io[name] = nc.dram_tensor(f"in_{name}", a.shape, mybir.dt.from_np(a.dtype), kind="ExternalInput").ap()
    for name, shape in OUTPUTS:
        flat = (int(np.prod(shape[:-1])), shape[-1])
        io[name] = nc.dram_tensor(f"out_{name}", flat, F32, kind="ExternalOutput").ap()
    for name, rows in (("x_t", D), ("proj", MAIN_CHUNKS * P), ("o_mla", HEADS * VD), ("o_hg", HH * DK)):
        io[name] = nc.dram_tensor(f"scratch_{name}", (rows, NT), F32, kind=SCRATCH).ap()
    io["x"] = lambda t: io["x_prompt"] if t == TILES - 1 else io["x_sample"][t * P:(t + 1) * P, :]
    program(nc, io)


SCRATCH = "Internal"


def kernel(**inputs):
    import concourse.bacc as bacc
    from concourse.bass_utils import run_bass_kernel_spmd

    nc = bacc.Bacc("TRN2", target_bir_lowering=False, num_devices=1)
    arrays = layout(inputs)
    build(nc, arrays)
    r = run_bass_kernel_spmd(nc, [{f"in_{k}": v for k, v in arrays.items()}], core_ids=[0])
    return tuple(r.results[0][f"out_{name}"].reshape(shape) for name, shape in OUTPUTS)
```
